# Optimizing a Trainium2 kernel written in Bass

```python
import functools
import jax, jax.numpy as jnp
from jax import lax
import numpy as np

D_MODEL = 1024
BATCH = 1
SEQ = 256
DEPTH = 1
DEC_BATCH = 8
DEC_SEQ = 1
PAST_LEN = 2048
PAGE_SIZE = 128

ATTN_HEADS = 8
ATTN_KV_HEADS = 2
HEAD_DIM = 64
ATTN_GROUP = ATTN_HEADS // ATTN_KV_HEADS
ATTN_WIDTH = ATTN_HEADS * HEAD_DIM
WINDOW = 128
ATTN_BLOCK = WINDOW
ROT_DIM = HEAD_DIM // 4
ROPE_THETA = 500000.0
HG_HEADS = 4
HG_DK = 128
HG_DV = 128
HG_WIDTH = HG_HEADS * HG_DV
HG_CHUNK = 64
MIX_WIDTH = ATTN_WIDTH + HG_WIDTH
IN_SIZES = (ATTN_WIDTH, ATTN_KV_HEADS * HEAD_DIM, ATTN_KV_HEADS * HEAD_DIM,
            HG_HEADS * HG_DK, HG_HEADS * HG_DK, HG_HEADS * HG_DV, HG_HEADS * HG_DV)
IN_COLS = sum(IN_SIZES)
IN_SPLITS = tuple(int(s) for s in np.cumsum(IN_SIZES)[:-1])
N_EXPERTS = 32
TOP_K = 4
D_FF = D_MODEL
SWIGLU_ALPHA = 1.702
SWIGLU_LIMIT = 7.0
EPS = 1e-5

kernel_name = 'hymba_swa_sink_hgrn2_moe_adaln_step'

F32 = jnp.float32

def rmsnorm(x, g):
    xf = x.astype(F32)
    y = xf * lax.rsqrt(jnp.mean(xf * xf, axis=-1, keepdims=True) + EPS)
    return (y * g.astype(F32)).astype(x.dtype)

def rotary(x, pos):
    half = ROT_DIM // 2
    inv = ROPE_THETA ** (-(jnp.arange(half, dtype=F32) * 2.0 / ROT_DIM))
    ang = pos.astype(F32)[:, None] * inv[None, :]
    cos = jnp.cos(ang)[:, None, :]
    sin = jnp.sin(ang)[:, None, :]
    xr = x[..., :ROT_DIM].astype(F32)
    x1, x2 = xr[..., :half], xr[..., half:]
    rot = jnp.concatenate([x1 * cos - x2 * sin, x2 * cos + x1 * sin], axis=-1)
    return jnp.concatenate([rot.astype(x.dtype), x[..., ROT_DIM:]], axis=-1)

def sink_attention(q, k, v, q_pos, k_pos, sinks):
    s = jnp.einsum('...qhgd,...shd->...hgqs', q, k).astype(F32) * (HEAD_DIM ** -0.5)
    diff = q_pos[..., :, None] - k_pos[..., None, :]
    ok = (diff >= 0) & (diff <= WINDOW) & (k_pos[..., None, :] >= 0)
    s = jnp.where(ok[..., None, None, :, :], s, -jnp.inf)
    sink = sinks.astype(F32).reshape(ATTN_KV_HEADS, ATTN_GROUP)[:, :, None, None]
    m = jnp.maximum(jnp.max(s, axis=-1, keepdims=True), sink)
    p = jnp.exp(s - m)
    p = p / (jnp.sum(p, axis=-1, keepdims=True) + jnp.exp(sink - m))
    return jnp.einsum('...hgqs,...shd->...qhgd', p.astype(v.dtype), v)

def attn_prompt(q, k, v, sinks, *, win):
    B, S = q.shape[:2]
    nb = S // ATTN_BLOCK
    qb = q.reshape(B, nb, ATTN_BLOCK, ATTN_KV_HEADS, ATTN_GROUP, HEAD_DIM)
    kb = k.reshape(B, nb, ATTN_BLOCK, ATTN_KV_HEADS, HEAD_DIM)
    vb = v.reshape(B, nb, ATTN_BLOCK, ATTN_KV_HEADS, HEAD_DIM)
    shift = ((0, 0), (1, 0), (0, 0), (0, 0), (0, 0))
    k2 = jnp.concatenate([jnp.pad(kb[:, :-1], shift), kb], axis=2)
    v2 = jnp.concatenate([jnp.pad(vb[:, :-1], shift), vb], axis=2)
    pos = jnp.arange(S, dtype=jnp.int32).reshape(nb, ATTN_BLOCK)
    kpos = jnp.concatenate([pos - ATTN_BLOCK, pos], axis=1)
    o = sink_attention(qb, k2, v2, pos, kpos, sinks).reshape(B, S, ATTN_WIDTH)
    return o, k[:, S - win:], v[:, S - win:]

def attn_sample(q, k, v, sinks, *, k_buf, v_buf, q_pos):
    B, S = q.shape[:2]
    win = k_buf.shape[1]
    k_all = jnp.concatenate([k_buf.astype(k.dtype), k], axis=1)
    v_all = jnp.concatenate([v_buf.astype(v.dtype), v], axis=1)
    kpos = PAST_LEN - win + jnp.arange(win + S, dtype=jnp.int32)
    o = sink_attention(q, k_all, v_all, q_pos, kpos, sinks).reshape(B, S, ATTN_WIDTH)
    return o, k_all[:, S:], v_all[:, S:]

def hgrn_chunk(S0, q, k, v, logf):
    C = q.shape[1]
    b = jnp.cumsum(logf, axis=1)
    causal = jnp.tril(jnp.ones((C, C), dtype=bool))
    rel = b[:, :, None] - b[:, None, :]
    decay = jnp.exp(jnp.where(causal[None, :, :, None, None], rel, -jnp.inf))
    a = jnp.einsum('bthk,bshk,btshk->bhts', q, k, decay)
    o = (jnp.einsum('bhts,bshv->bthv', a, v)
         + jnp.einsum('bthk,bhkv->bthv', q * jnp.exp(b), S0))
    b_last = b[:, -1]
    S = (jnp.exp(b_last)[..., None] * S0
         + jnp.einsum('bshk,bshv->bhkv', k * jnp.exp(b_last[:, None] - b), v))
    return S, o

def hgrn_prompt(q, k, v, logf):
    B, S = q.shape[:2]
    nc = S // HG_CHUNK

    def chunks(t):
        return t.reshape(B, nc, HG_CHUNK, *t.shape[2:]).swapaxes(0, 1)

    S0 = jnp.zeros((B, HG_HEADS, HG_DK, HG_DV), F32)
    S_fin, o = lax.scan(lambda s, xs: hgrn_chunk(s, *xs), S0,
                        (chunks(q), chunks(k), chunks(v), chunks(logf)))
    return o.swapaxes(0, 1).reshape(B, S, HG_HEADS, HG_DV), S_fin

def hgrn_sample(q, k, v, logf, *, S0):
    S, o = hgrn_chunk(S0.astype(F32), q, k, v, logf)
    return o, S

def clamped_swiglu(u):
    glu, lin = u[..., ::2], u[..., 1::2]
    glu = jnp.minimum(glu, SWIGLU_LIMIT)
    lin = jnp.clip(lin, -SWIGLU_LIMIT, SWIGLU_LIMIT)
    return glu * jax.nn.sigmoid(SWIGLU_ALPHA * glu) * (lin + 1.0)

def moe_ffn(h, w_router, b_router, w_up, b_up, w_down, b_down):
    shp = h.shape
    t = h.reshape(-1, shp[-1])
    logits = (t @ w_router + b_router).astype(F32)
    top_v, top_i = lax.top_k(logits, TOP_K)
    wts = jax.nn.softmax(top_v, axis=-1)
    combine = jnp.sum(jax.nn.one_hot(top_i, N_EXPERTS, dtype=F32) * wts[..., None], axis=1)

    def expert(acc, e):
        wu, bu, wd, bd, cw = e
        y = clamped_swiglu(t @ wu + bu) @ wd + bd
        return acc + cw[:, None].astype(t.dtype) * y, None

    out, _ = lax.scan(expert, jnp.zeros_like(t), (w_up, b_up, w_down, b_down, combine.T))
    return out.reshape(shp)

def decoder_layer(x, c, pos, attn_core, hgrn_core, lb, w_ada, b_ada, g_mix, g_ffn, w_in,
                  attn_sinks, g_attn_out, g_hg_out, w_out, w_router, b_router,
                  w_up, b_up, w_down, b_down):
    B, S, _ = x.shape
    mod = jax.nn.silu(c) @ w_ada + b_ada
    sh1, sc1, gt1, sh2, sc2, gt2 = [m[:, None, :] for m in jnp.split(mod, 6, axis=-1)]
    h = rmsnorm(x, g_mix) * (1.0 + sc1) + sh1
    z = h @ w_in
    q_a, k_a, v_a, q_h, f_h, i_h, g_h = jnp.split(z, IN_SPLITS, axis=-1)
    q_a = rotary(q_a.reshape(B, S, ATTN_HEADS, HEAD_DIM), pos).reshape(
        B, S, ATTN_KV_HEADS, ATTN_GROUP, HEAD_DIM)
    k_a = rotary(k_a.reshape(B, S, ATTN_KV_HEADS, HEAD_DIM), pos)
    v_a = v_a.reshape(B, S, ATTN_KV_HEADS, HEAD_DIM)
    o_a, k_new, v_new = attn_core(q_a, k_a, v_a, attn_sinks)
    o_a = rmsnorm(o_a, g_attn_out)
    f = lb + (1.0 - lb) * jax.nn.sigmoid(f_h.reshape(B, S, HG_HEADS, HG_DK).astype(F32))
    o_h, S_new = hgrn_core(q_h.reshape(B, S, HG_HEADS, HG_DK).astype(F32), 1.0 - f,
                           i_h.reshape(B, S, HG_HEADS, HG_DV).astype(F32), jnp.log(f))
    o_h = rmsnorm(o_h, g_hg_out) * jax.nn.silu(g_h.reshape(B, S, HG_HEADS, HG_DV).astype(F32))
    o_h = o_h.reshape(B, S, HG_WIDTH).astype(x.dtype)
    x = x + gt1 * (jnp.concatenate([o_a, o_h], axis=-1) @ w_out)
    h = rmsnorm(x, g_ffn) * (1.0 + sc2) + sh2
    x = x + gt2 * moe_ffn(h, w_router, b_router, w_up, b_up, w_down, b_down)
    return x, k_new, v_new, S_new

def setup_inputs(seed: int = 0) -> dict:
    key = jax.random.key(seed)
    ks = jax.random.split(key, 32)
    D = D_MODEL
    win = min(WINDOW, PAST_LEN)

    def nrm(k, shape, scale):
        return jax.random.normal(k, shape, F32) * scale

    return {
        'x_prompt': nrm(ks[0], (BATCH, SEQ, D), 1.0),
        'x_sample': nrm(ks[1], (DEC_BATCH, DEC_SEQ, D), 1.0),
        'c_prompt': nrm(ks[2], (BATCH, D), 1.0),
        'c_sample': nrm(ks[3], (DEC_BATCH, D), 1.0),
        'cache_k_win': nrm(ks[4], (DEPTH, DEC_BATCH, win, ATTN_KV_HEADS, HEAD_DIM), 1.0),
        'cache_v_win': nrm(ks[5], (DEPTH, DEC_BATCH, win, ATTN_KV_HEADS, HEAD_DIM), 1.0),
        'state_hgrn': nrm(ks[6], (DEPTH, DEC_BATCH, HG_HEADS, HG_DK, HG_DV), 0.5),
        'w_ada': nrm(ks[7], (DEPTH, D, 6 * D), 0.5 * D ** -0.5),
        'b_ada': nrm(ks[8], (DEPTH, 6 * D), 0.02),
        'g_mix': 1.0 + nrm(ks[9], (DEPTH, D), 0.02),
        'g_ffn': 1.0 + nrm(ks[10], (DEPTH, D), 0.02),
        'w_in': nrm(ks[11], (DEPTH, D, IN_COLS), D ** -0.5),
        'attn_sinks': nrm(ks[12], (DEPTH, ATTN_HEADS), 0.5),
        'g_attn_out': 1.0 + nrm(ks[13], (DEPTH, ATTN_WIDTH), 0.02),
        'hg_lb_logits': nrm(ks[14], (DEPTH + 1, HG_HEADS * HG_DK), 0.5),
        'g_hg_out': 1.0 + nrm(ks[15], (DEPTH, HG_HEADS, HG_DV), 0.02),
        'w_out': nrm(ks[16], (DEPTH, MIX_WIDTH, D), MIX_WIDTH ** -0.5),
        'w_router': nrm(ks[17], (DEPTH, D, N_EXPERTS), D ** -0.5),
        'b_router': nrm(ks[18], (DEPTH, N_EXPERTS), 0.01),
        'w_up': nrm(ks[19], (DEPTH, N_EXPERTS, D, 2 * D_FF), D ** -0.5),
        'b_up': nrm(ks[20], (DEPTH, N_EXPERTS, 2 * D_FF), 0.02),
        'w_down': nrm(ks[21], (DEPTH, N_EXPERTS, D_FF, D), D_FF ** -0.5),
        'b_down': nrm(ks[22], (DEPTH, N_EXPERTS, D), 0.02),
        'g_final': 1.0 + nrm(ks[23], (D,), 0.02),
    }

def reference(x_prompt, x_sample, c_prompt, c_sample, cache_k_win, cache_v_win, state_hgrn,
              w_ada, b_ada, g_mix, g_ffn, w_in, attn_sinks, g_attn_out, hg_lb_logits, g_hg_out,
              w_out, w_router, b_router, w_up, b_up, w_down, b_down, g_final):
    win = cache_k_win.shape[2]
    pos_p = jnp.arange(x_prompt.shape[1], dtype=jnp.int32)
    pos_s = PAST_LEN + jnp.arange(x_sample.shape[1], dtype=jnp.int32)
    lb_all = jnp.cumsum(jax.nn.softmax(hg_lb_logits.astype(F32), axis=0), axis=0)
    xp, xs = x_prompt, x_sample
    kp_l, vp_l, sp_l, ks_l, vs_l, ss_l = [], [], [], [], [], []
    for l in range(DEPTH):
        lb = lb_all[l].reshape(HG_HEADS, HG_DK)
        w = (w_ada[l], b_ada[l], g_mix[l], g_ffn[l], w_in[l], attn_sinks[l], g_attn_out[l],
             g_hg_out[l], w_out[l], w_router[l], b_router[l], w_up[l], b_up[l], w_down[l],
             b_down[l])
        xp, kp, vp, sp = decoder_layer(
            xp, c_prompt, pos_p, functools.partial(attn_prompt, win=win), hgrn_prompt, lb, *w)
        xs, kn, vn, sn = decoder_layer(
            xs, c_sample, pos_s,
            functools.partial(attn_sample, k_buf=cache_k_win[l], v_buf=cache_v_win[l], q_pos=pos_s),
            functools.partial(hgrn_sample, S0=state_hgrn[l]), lb, *w)
        kp_l.append(kp); vp_l.append(vp); sp_l.append(sp)
        ks_l.append(kn); vs_l.append(vn); ss_l.append(sn)
    y_prompt = rmsnorm(xp, g_final)
    y_sample = rmsnorm(xs, g_final)
    k_win_prompt = jnp.stack(kp_l)
    v_win_prompt = jnp.stack(vp_l)
    hgrn_prompt_state = jnp.stack(sp_l)
    k_win_sample = jnp.stack(ks_l)
    v_win_sample = jnp.stack(vs_l)
    hgrn_sample_state = jnp.stack(ss_l)
    return (y_prompt, y_sample, k_win_prompt, v_win_prompt, hgrn_prompt_state,
            k_win_sample, v_win_sample, hgrn_sample_state)


_drawn_inputs = setup_inputs


def setup_inputs(seed=0):
    import zlib

    import numpy as np

    out = dict(_drawn_inputs(seed))
    spreads = {}
    factors = {'g_mix': 2.913,
     'g_ffn': 3.615,
     'attn_sinks': 8.0,
     'g_attn_out': 27.912,
     'g_hg_out': 7.192,
     'b_router': 16.291,
     'b_up': 8.0,
     'b_down': 53.581,
     'g_final': 8.497}
    for name, (base, spread) in spreads.items():
        noise = np.random.default_rng([zlib.crc32(name.encode()), seed]).standard_normal(out[name].shape)
        drawn = base * np.exp(spread * noise) if base else spread * noise
        out[name] = __import__('jax').numpy.asarray(drawn.astype(out[name].dtype))
    for name, factor in factors.items():
        out[name] = (out[name] * factor).astype(out[name].dtype)
    return out
```

```python
from contextlib import ExitStack

import numpy as np

import concourse.bass as bass
from concourse import mybir

F32 = mybir.dt.float32
I32 = mybir.dt.int32
U32 = mybir.dt.uint32
ALU = mybir.AluOpType
ACT = mybir.ActivationFunctionType
AX = mybir.AxisListType

P = 128
D = 1024
KT = D // P
S = 256
NB = 8
NTOK = S + NB
HEADS, KV, HD = 8, 2, 64
GRP = HEADS // KV
WIN = 128
ROT = HD // 4
HALF = ROT // 2
AW = HEADS * HD
HH = 4
HW_ = HH * P
QKV = AW + 2 * KV * HD
IN_COLS = QKV + 4 * HW_
ZC = 256
NZ = IN_COLS // ZC
E = 32
TOPK = 4
FF2 = 2 * D
EPS = 1e-5
PAST = 2048
SLOTS = 64
ARENA = 29300
N_STORED = 2 + 2 + 2 + 1 + NB
ROWS = E * SLOTS
MAXPASS = -(-NTOK // SLOTS)
PAIRS = E // 2
LIMIT = 7.0
ALPHA = 1.702
NEG = -1e30
LEVELS = [1 << i for i in range(7)]

RING = 8
CH = 2048
N_ADA = 8
Z0 = N_ADA
ADA1 = Z0 + NZ
ADA2 = ADA1 + N_ADA
WO0 = ADA2 + N_ADA
PRE = WO0 + 4
PER = 24

_COLS = {}
_at = 0
for _name, _n in (("ident", P), ("incl", P), ("after", P), ("before", P), ("ones", P), ("levels", 8 * P),
                  ("window", 2 * P), ("pick", NTOK), ("cos", 3 * HALF), ("sin", 3 * HALF), ("e64", E),
                  ("iota", E), ("tok", 3), ("spread", 64), ("onehot", NB), ("bias_row", SLOTS), ("group", 2)):
    _COLS[_name] = (_at, _at + _n)
    _at += _n
NCONST = _at


def constants():
    c = np.zeros((P, NCONST), np.float32)

    def put(name, a, rows=P):
        lo, hi = _COLS[name]
        c[:rows, lo:hi] = np.asarray(a, np.float32).reshape(rows, hi - lo)

    r = np.arange(P)
    put("ident", np.eye(P))
    put("incl", r[:, None] <= r[None, :])
    put("after", r[:, None] > r[None, :])
    put("before", r[:, None] < r[None, :])
    put("ones", np.ones((P, P)))
    masks = [np.eye(P)]
    for m in LEVELS:
        same = r[:, None] // (2 * m) == r[None, :] // (2 * m)
        masks.append(same & (r[:, None] % (2 * m) < m) & (r[None, :] % (2 * m) >= m))
    put("levels", np.stack(masks, 1))
    diff = r[:, None] + P - np.arange(2 * P)[None, :]
    put("window", np.where((diff >= 0) & (diff <= WIN), 0.0, NEG))
    pick = np.zeros((P, NTOK))
    for j in range(4):
        pick[32 * j, :S] = 1
        for b in range(NB):
            pick[32 * j + 1 + b, S + b] = 1
    put("pick", pick)
    inv = np.float32(500000.0) ** (-(np.arange(HALF, dtype=np.float32) * np.float32(2.0) / np.float32(ROT)))
    pos = np.zeros((3, P), np.float32)
    pos[0], pos[1], pos[2] = r, r + P, PAST
    ang = (pos[:, :, None] * inv.astype(np.float32)[None, None, :]).astype(np.float32)
    put("cos", np.cos(ang).transpose(1, 0, 2))
    put("sin", np.sin(ang).transpose(1, 0, 2))
    put("e64", np.tile(np.arange(E) * SLOTS, (P, 1)))
    put("iota", np.tile(np.arange(E), (P, 1)))
    put("tok", np.stack([r, r + P, r + 2 * P], 1))
    put("spread", np.repeat(np.eye(NB), HEADS, 1), NB)
    put("onehot", np.eye(NB), NB)
    br = np.zeros((P, SLOTS))
    br[0] = 1
    put("bias_row", br)
    h = np.arange(64) % HEADS
    put("group", np.stack([h < GRP, h >= GRP], 1), 64)
    return c


def wide(ap, dim, n):
    shape = list(ap.shape)
    shape[dim] = n
    return ap.broadcast_to(shape)


def hybrid_layer(nc, A, O):
    with ExitStack() as ctx:
        sems = {}

        def sem(name):
            if name not in sems:
                sems[name] = ctx.enter_context(nc.semaphore(name))
            return sems[name]

        def sb(name, shape, dt=F32):
            return ctx.enter_context(nc.sbuf_tensor(name, shape, dt))

        B = [ctx.enter_context(nc.psum_tensor(f"bank{i}", [P, 512], F32)) for i in range(8)]

        const = sb("const", [P, NCONST])

        def C(name, rows=slice(0, P)):
            lo, hi = _COLS[name]
            return const[rows, lo:hi]

        ident = C("ident")
        ring = sb("ring", [P, RING, CH])
        x = sb("x", [P, 3, D])
        mods = sb("mods", [P, 3, 512])
        slot_u = sb("slot_u", [P, 3, TOPK], U32)
        row_u = sb("row_u", [P, 3, TOPK], U32)
        topw = sb("topw", [P, 3, TOPK])
        npass = sb("npass", [1, 1], I32)
        small = sb("small", [P, 256])
        zeros = sb("zeros", [P, MAXPASS * ROWS // P], I32)
        tok_i = sb("tok_i", [P, 3], I32)
        idx = sb("idx", [P, 1], I32)

        arena = sb("arena", [P, ARENA])
        top = [0]

        def take(n, at=None):
            lo = top[0] if at is None else at
            if at is None:
                top[0] += n
            assert lo + n <= ARENA, (lo, n)
            return arena[:, lo:lo + n]

        z_at = top[0]
        z = take(2 * IN_COLS).rearrange("p (t c) -> p t c", t=2)
        zs = take(IN_COLS)
        zq = take(NZ * 64).rearrange("p (c n) -> p c n", c=NZ)
        h = take(3 * D).rearrange("p (t c) -> p t c", t=3)
        hT_at = top[0]
        hT = take(KT * 288).rearrange("p (k t) -> p k t", k=KT)
        bT, kkT, qqT = (take(HW_, hT_at + n * HW_) for n in range(3))
        lb, oml, g_att, g_hg = (take(512) for _ in range(4))
        ada_at = top[0]
        ba = take(3 * 512).rearrange("p (q c) -> p q c", q=3)
        gb = take(2 * 512).rearrange("p (q c) -> p q c", q=2)
        scT = take(KT * 32).rearrange("p (k t) -> p k t", k=KT)
        take(840)
        kc = take(NB * P, ada_at).rearrange("p (b c) -> p b c", b=NB)
        vc = take(NB * P, ada_at + 1024).rearrange("p (b c) -> p b c", b=NB)
        kcT = take(NB * 129, ada_at + 2048).rearrange("p (b s) -> p b s", b=NB)
        qbd = take(NB * 72, ada_at + 3080)
        pbd = take(NB * 72, ada_at)
        att_at = top[0]
        qT = take(4 * S).rearrange("p (j t) -> p j t", j=4)
        kT = take(S)
        sc_at = top[0]
        sc = take(HEADS * 2 * P)
        pT = take(HEADS * 2 * P).rearrange("p (n q) -> p n q", q=P)
        crow = take(D, sc_at)
        states = take(NB * HW_, att_at).rearrange("p (b h v) -> p b h v", b=NB, h=HH)
        km = [take(HW_, att_at + 4096 + n * HW_) for n in range(2)]
        logf_at = top[0]
        logf = take(2 * HW_).rearrange("p (t c) -> p t c", t=2)
        lbl = take(2 * 512, logf_at).rearrange("p (q c) -> p q c", q=2)
        ps = take(129, logf_at)
        pv = take(P, logf_at + 129)
        o64 = take(64, logf_at + 257)
        sq = take(2 * HH * NB, logf_at + 321)
        soT = take(HH * NB, logf_at + 385)
        lev = [take(HW_) for _ in range(2)]
        amat = take(HW_).rearrange("p (h t) -> p h t", h=HH)
        ks = take(HW_)
        st = take(HW_)
        gt1 = take(D, z_at)
        gt1s = take(D, z_at + D)
        tmp = take(D, z_at + 2 * D)
        tmps = take(D, z_at + 3 * D)
        lgT = take(NTOK, z_at + 4 * D)
        lg = take(3 * E, z_at + 4 * D + 264).rearrange("p (t e) -> p t e", t=3)
        chosen = take(3 * E, z_at + 4 * D + 360).rearrange("p (t e) -> p t e", t=3)
        onek = take(3 * TOPK * E, z_at + 4 * D + 456).rearrange("p (t k e) -> p t k e", t=3, k=TOPK)
        slotf = take(E, z_at + 4 * D + 840)
        over = take(E, z_at + 4 * D + 872)
        hit = take(E, z_at + 4 * D + 904)
        wr = take(KT * E, z_at + 5 * D).rearrange("p (k e) -> p k e", k=KT)
        bias = [take(FF2 + D, n * 3 * D) for n in range(2)]
        top2 = [6 * D]

        def later(n):
            top2[0] += n
            return take(n, top2[0] - n)

        xg = later(D)
        xT = later(D).rearrange("p (k t) -> p k t", k=KT)
        glu, lin, sg = (later(512) for _ in range(3))
        gg = [later(512) for _ in range(2)]
        gT = [later(512) for _ in range(2)]
        ysb = [later(512) for _ in range(2)]
        yk = [later(D) for n in range(TOPK)]
        moe = later(3 * D).rearrange("p (t c) -> p t c", t=3)
        g_fin = later(D)
        gt2 = [later(D) for n in range(2)]

        scol = [0]

        def stat(n):
            scol[0] += n
            return small[:, scol[0] - n:scol[0]]

        ssum3, root3 = stat(3), stat(3)
        sinkb, sink64, brout = stat(HEADS), stat(1), stat(1)
        mrow = stat(2 * HEADS).rearrange("p (t h) -> p t h", t=2)
        nmax = stat(2 * HEADS).rearrange("p (t h) -> p t h", t=2)
        dsink = stat(2 * HEADS).rearrange("p (t h) -> p t h", t=2)
        esink = stat(2 * HEADS).rearrange("p (t h) -> p t h", t=2)
        psums = stat(2 * HEADS).rearrange("p (t h) -> p t h", t=2)
        smx, snm, ssm, sesk, sra, srb = (stat(1) for _ in range(6))
        gmean, groot = stat(15), stat(15)
        eb = stat(HH)
        top8 = stat(24).rearrange("p (t k) -> p t k", t=3)
        topf = stat(12).rearrange("p (t k) -> p t k", t=3)
        ntop, tsum = stat(3), stat(3)
        cmax, csum = stat(1), stat(1)
        passf = stat(12).rearrange("p (t k) -> p t k", t=3)
        now, passw = stat(1), stat(12).rearrange("p (t k) -> p t k", t=3)
        chit = stat(MAXPASS)
        top8i = sb("top8i", [P, 24], U32)[:, :].rearrange("p (t k) -> p t k", t=3)
        rtmp = take(2 * 160, sc_at + 2048).rearrange("p (t n) -> p t n", t=2)

        h2_dram = nc.dram_tensor("h2_rows", [NTOK, D], F32, kind="Internal").ap()
        y_dram = nc.dram_tensor("y_rows", [ROWS, D], F32, kind="Internal").ap()
        list_dram = nc.dram_tensor("slot_tokens", [MAXPASS * ROWS, 1], I32, kind="Internal").ap()

        full = [sem(f"ring_full{i}") for i in range(RING)]
        chunks_used = sem("chunks_used")

        NT = [P, P, NB]
        Q0, F0, I0, G0 = QKV, QKV + HW_, QKV + 2 * HW_, QKV + 3 * HW_
        K0, V0 = AW, AW + P

        w_ada = A["w_ada"][0].rearrange("(k p) n -> k p n", p=P)
        w_in = A["w_in"][0].rearrange("(k p) n -> p k n", p=P)
        w_out = A["w_out"][0].rearrange("(c two p) n -> c p two n", two=2, p=P)
        w_up = A["w_up"][0].rearrange("e (k p) n -> (e k) p n", p=P)
        w_down = A["w_down"][0].rearrange("e (c two p) n -> (e c) p two n", two=2, p=P)

        def chunk(n):
            return ring[:, n % RING, :]

        def two(ap):
            return ap.rearrange("p (two n) -> p two n", two=2)

        def count_from_one(engine, *names):
            for name in names:
                engine.sem_inc(sem(name), 1)

        block = ctx.enter_context(nc.Block())

        @block.sync
        def _(sp):
            def room(n):
                if n >= RING:
                    sp.wait_ge(chunks_used, n - RING + 1)

            for k in range(N_ADA):
                room(k)
                sp.dma_start(chunk(k), w_ada[k, :, 0:CH]).then_inc(full[k % RING], 16)
            for c in range(NZ):
                room(Z0 + c)
                sp.dma_start(chunk(Z0 + c).rearrange("p (k n) -> p k n", k=KT),
                             w_in[:, :, c * ZC:(c + 1) * ZC]).then_inc(full[(Z0 + c) % RING], 16)
            for q, first in ((1, ADA1), (2, ADA2)):
                for k in range(N_ADA):
                    room(first + k)
                    sp.dma_start(chunk(first + k), w_ada[k, :, q * CH:(q + 1) * CH]).then_inc(full[(first + k) % RING], 16)
            for c in range(4):
                room(WO0 + c)
                sp.dma_start(two(chunk(WO0 + c)), w_out[c]).then_inc(full[(WO0 + c) % RING], 16)

            def expert_chunk(c, pair, it):
                n = PRE + c
                sp.wait_ge(chunks_used, it * PER + (n - RING + 1))
                if c < 16:
                    sp.dma_start(chunk(n), w_up[pair * 16 + c]).then_inc(full[n % RING], 16)
                else:
                    sp.dma_start(two(chunk(n)), w_down[pair * 8 + (c - 16)]).then_inc(full[n % RING], 16)

            for c in range(RING):
                expert_chunk(c, 0, 0)
            sp.wait_ge(sem("npass_ready"), 1)
            sp.wait_ge(sem("bias_cleared"), 2)
            passes = sp.value_load(npass[0:1, 0:1], min_val=1, max_val=MAXPASS)
            total = sp.snap(passes * PAIRS)
            with sp.Fori(0, total) as it:
                for c in range(RING, PER):
                    expert_chunk(c, it % PAIRS, it)
                with sp.If(it < total - 1):
                    for c in range(RING):
                        expert_chunk(c, (it + 1) % PAIRS, it + 1)

        @block.gpsimd
        def _(pool):
            pool.wait_ge(sem("cleared"), 1)
            for q in range(3):
                for j in range(4):
                    n0 = q * CH + j * 512
                    pool.dma_start(ba[32 * j:32 * j + 9, q, :],
                                   wide(A["b_ada"][0:1, n0:n0 + 512], 0, 9)).then_inc(sem("ada_rows_full"), 16)
            for j in range(2):
                pool.dma_start(gb[64 + 32 * j:64 + 32 * j + 9, 0, :],
                               wide(A["g_mix"][0:1, j * 512:(j + 1) * 512], 0, 9)).then_inc(sem("ada_rows_full"), 16)
                pool.dma_start(gb[32 * j:32 * j + 9, 1, :],
                               wide(A["g_ffn"][0:1, j * 512:(j + 1) * 512], 0, 9)).then_inc(sem("ada_rows_full"), 16)
            pool.dma_start(lbl[:, 0, :], wide(A["hg_lb_logits"][0:1, :], 0, P)).then_inc(sem("rows_full"), 16)
            pool.dma_start(lbl[:, 1, :], wide(A["hg_lb_logits"][1:2, :], 0, P)).then_inc(sem("rows_full"), 16)
            pool.dma_start(g_att, wide(A["g_attn_out"][0:1, :], 0, P)).then_inc(sem("rows_full"), 16)
            pool.dma_start(g_hg, wide(A["g_hg_out"].rearrange("a h v -> a (h v)"), 0, P)).then_inc(sem("rows_full"), 16)
            pool.dma_start(sinkb, wide(A["attn_sinks"][0:1, :], 0, P)).then_inc(sem("rows_full"), 16)
            for b in range(NB):
                pool.dma_start(sink64[HEADS * b:HEADS * (b + 1), :],
                               A["attn_sinks"].rearrange("a h -> h a")).then_inc(sem("rows_full"), 16)
            pool.dma_start(brout[0:E, :], A["b_router"].rearrange("a e -> e a")).then_inc(sem("rows_full"), 16)
            for src, dst in (("cache_k_win", "kws"), ("cache_v_win", "vws")):
                pool.dma_start(O[dst][0, :, 0:WIN - 1].rearrange("b s g d -> b (s g d)"),
                               A[src][0, :, 1:WIN].rearrange("b s g d -> b (s g d)")).then_inc(sem("stored"), 16)
            pool.dma_start(list_dram.rearrange("(p n) a -> p (n a)", p=P), zeros[:, :]).then_inc(sem("list_cleared"), 16)
            pool.wait_ge(sem("z_dec_copied"), NZ)
            for j in range(4):
                pool.dma_start(zs[0:NB, P * j:P * (j + 1)], zq[32 * j:32 * j + NB, 0:KV, :]).then_inc(sem("zs_full"), 16)
                pool.dma_start(zs[0:NB, :].rearrange("p (c j n) -> p c j n", c=NZ, j=4)[:, KV:, j, :],
                               zq[32 * j:32 * j + NB, KV:, :]).then_inc(sem("zs_full"), 16)
            pool.wait_ge(sem("rotated"), 1)
            pool.dma_start(O["kwp"][0, 0].rearrange("s g d -> s (g d)"), z[:, 1, K0:K0 + P]).then_inc(sem("stored"), 16)
            pool.dma_start(O["vwp"][0, 0].rearrange("s g d -> s (g d)"), z[:, 1, V0:V0 + P]).then_inc(sem("stored"), 16)
            pool.wait_ge(sem("rotated"), 2)
            pool.dma_start(O["kws"][0, :, WIN - 1].rearrange("b g d -> b (g d)"), zs[0:NB, K0:K0 + P]).then_inc(sem("stored"), 16)
            pool.dma_start(O["vws"][0, :, WIN - 1].rearrange("b g d -> b (g d)"), zs[0:NB, V0:V0 + P]).then_inc(sem("stored"), 16)
            pool.wait_ge(sem("mod_ready"), 3)
            pool.dma_start(kc, A["cache_k_win"][0].rearrange("b s g d -> s b (g d)")).then_inc(sem("cache_full"), 16)
            pool.dma_start(vc, A["cache_v_win"][0].rearrange("b s g d -> s b (g d)")).then_inc(sem("cache_full"), 16)
            pool.wait_ge(sem("att_summed"), 2)
            for b in range(NB):
                pool.dma_start(states[:, b], A["state_hgrn"][0, b].rearrange("h k v -> k h v")).then_inc(sem("states_full"), 16)
            pool.wait_ge(sem("state_final"), HH)
            pool.dma_start(O["hgp"][0, 0].rearrange("h k v -> k h v"), st.rearrange("p (h v) -> p h v", h=HH)).then_inc(sem("stored"), 16)
            pool.wait_ge(sem("o64_ready"), 1)
            pool.dma_start(h[0:NB, 2, 0:AW], o64[0:64, :]).then_inc(sem("o64_moved"), 16)
            pool.wait_ge(sem("states_new"), NB * HH)
            for b in range(NB):
                pool.dma_start(O["hgs"][0, b].rearrange("h k v -> k h v"), states[:, b]).then_inc(sem("stored"), 16)
            pool.wait_ge(sem("cat_ready"), 3)
            pool.dma_start(wr, A["w_router"][0].rearrange("(k p) e -> p k e", p=P)).then_inc(sem("router_full"), 16)
            pool.wait_ge(sem("wo_dec_copied"), 1)
            for j in range(4):
                pool.dma_start(tmps[0:NB, 256 * j:256 * (j + 1)], zq[32 * j:32 * j + NB, 0:4, :]).then_inc(sem("wo_dec_full"), 16)
            for t in range(3):
                pool.wait_ge(sem("h2_ready"), t + 1)
                pool.dma_start(h2_dram[P * t:P * t + NT[t], :], h[0:NT[t], t, :]).then_inc(sem("h2_stored"), 16)
            pool.wait_ge(sem("list_cleared"), 16)
            pool.wait_ge(sem("slots_ready"), 3 * TOPK)
            for t in range(3):
                for k in range(TOPK):
                    pool.indirect_dma_start(
                        out=list_dram, out_offset=bass.IndirectOffsetOnAxis(ap=slot_u[0:NT[t], t, k:k + 1], axis=0),
                        in_=tok_i[0:NT[t], t:t + 1], in_offset=None).then_inc(sem("list_full"), 16)
            pool.wait_ge(sem("list_full"), 16 * 3 * TOPK)
            pool.wait_ge(sem("npass_ready"), 1)
            pool.wait_ge(sem("stored"), 16 * N_STORED)
            passes = pool.value_load(npass[0:1, 0:1], min_val=1, max_val=MAXPASS)
            total = pool.snap(passes * PAIRS)
            pool.dma_start(g_fin, wide(A["g_final"].rearrange("(a n) -> a n", a=1), 0, P)).then_inc(sem("gfin_full"), 16)
            pool.wait_ge(sem("bias_cleared"), 2)
            with pool.Fori(0, passes) as p:
                with pool.Fori(0, PAIRS) as i:
                    it = pool.snap(p * PAIRS + i)
                    pool.wait_ge(sem("xT_made"), it * 2 + 1)
                    pool.dma_start(idx[:, :], list_dram[bass.ds(it * P, P), :]).then_inc(sem("idx_full"), 16)
                    pool.wait_ge(sem("idx_full"), it * 16 + 16)
                    pool.nop(nofuse=True)
                    pool.indirect_dma_start(
                        out=xg, out_offset=None, in_=h2_dram,
                        in_offset=bass.IndirectOffsetOnAxis(ap=idx[:, 0:1].bitcast(U32), axis=0)).then_inc(sem("x_full"), 16)
                    row = pool.snap(i * 2)
                    for e in range(2):
                        pool.wait_ge(sem(f"bias_used{e}"), it + 1)
                        pool.dma_start(bias[e][0:1, 0:FF2],
                                       A["b_up"][0][bass.ds(row + e, 1), :]).then_inc(sem(f"bias_full{e}"), 16)
                        pool.dma_start(bias[e][0:1, FF2:FF2 + D],
                                       A["b_down"][0][bass.ds(row + e, 1), :]).then_inc(sem(f"bias_full{e}"), 16)
                for e in range(2):
                    pool.wait_ge(sem(f"y_stored{e}"), (p + 1) * (32 * PAIRS) + 1)
                for t in range(3):
                    for k in range(TOPK):
                        pool.wait_ge(sem("y_added"), p * (3 * TOPK) + (TOPK * (t - 1) + k + 2 if t else 1))
                        pool.nop(nofuse=True)
                        pool.indirect_dma_start(
                            out=yk[k][0:NT[t], :], out_offset=None, in_=y_dram,
                            in_offset=bass.IndirectOffsetOnAxis(ap=row_u[0:NT[t], t, k:k + 1], axis=0)).then_inc(sem(f"y_full{k}"), 16)
            for t in range(3):
                pool.wait_ge(sem("result"), t + 1)
                dst = O["yp"][0, P * t:P * t + P] if t < 2 else O["ys"].rearrange("b s d -> (b s) d")
                pool.dma_start(dst, x[0:NT[t], t, :]).then_inc(sem("stored"), 16)
            pool.wait_ge(sem("stored"), 16 * (N_STORED + 3))

        @block.scalar
        def _(act):
            act.dma_start(crow[0:1, :], A["c_prompt"]).then_inc(sem("c_full"), 16)
            act.dma_start(crow[1:9, :], A["c_sample"]).then_inc(sem("c_full"), 16)
            act.dma_start(const[:, :], A["const"]).then_inc(sem("const_full"), 16)
            act.dma_start(x[:, 0, :], A["x_prompt"][0, 0:P]).then_inc(sem("x_full_in"), 16)
            act.dma_start(x[:, 1, :], A["x_prompt"][0, P:S]).then_inc(sem("x_full_in"), 16)
            act.dma_start(x[0:NB, 2, :], A["x_sample"].rearrange("b s d -> (b s) d")).then_inc(sem("x_full_in"), 16)
            act.wait_ge(sem("c_full"), 32)
            act.activation(crow[0:9, :], crow[0:9, :], ACT.Silu).then_inc(sem("c_silu"), 1)

            def squares(t, signal):
                act.activation(h[0:NT[t], t, :], x[0:NT[t], t, :], ACT.Square,
                               accum_out=ssum3[0:NT[t], t:t + 1]).then_inc(sem(signal), 1)

            def root(t, signal):
                act.activation(root3[0:NT[t], t:t + 1], ssum3[0:NT[t], t:t + 1], ACT.Sqrt).then_inc(sem(signal), 1)

            act.wait_ge(sem("x_full_in"), 48)
            for t in range(3):
                squares(t, "sums1")
            act.wait_ge(sem("means1"), 3)
            for t in range(3):
                root(t, "roots1")

            def even_tiles(made, copied):
                for k in range(0, KT, 2):
                    act.wait_ge(sem(made), k + 1)
                    act.activation(hT[:, k, 0:NTOK], B[k][:, 0:NTOK], ACT.Copy).then_inc(sem(copied), 1)

            even_tiles("hT_made", "hT_copied_a")
            for c in range(NZ):
                act.wait_ge(sem("z_made"), c + 1)
                src = B[c % 4][:, :].rearrange("p (t n) -> p t n", t=2)
                if c < KV:
                    for t in range(2):
                        done = act.activation(z[:, t, 0:AW].rearrange("p (j g d) -> p g j d", g=KV, j=GRP)[:, c],
                                              src[:, t, :].rearrange("p (j d) -> p j d", j=GRP), ACT.Copy)
                else:
                    done = act.activation(z[:, :, c * ZC:(c + 1) * ZC], src, ACT.Copy)
                done.then_inc(sem("z_copied"), 1)
            act.wait_ge(sem("z_copied"), NZ)
            act.activation(z[:, :, F0:F0 + HW_], z[:, :, F0:F0 + HW_], ACT.Sigmoid).then_inc(sem("f_sig"), 1)
            act.wait_ge(sem("qk_made"), 3)
            act.activation(qT[:, :, 0:P], B[0][:, :].rearrange("p (j t) -> p j t", j=4), ACT.Copy).then_inc(sem("qk_copied"), 1)
            act.activation(qT[:, :, P:S], B[1][:, :].rearrange("p (j t) -> p j t", j=4), ACT.Copy).then_inc(sem("qk_copied"), 1)
            act.activation(kT, B[2][:, 0:S], ACT.Copy).then_inc(sem("qk_copied"), 1)
            act.wait_ge(sem("zs_full"), 128)
            act.activation(zs[0:NB, F0:F0 + HW_], zs[0:NB, F0:F0 + HW_], ACT.Sigmoid).then_inc(sem("f_sig"), 1)
            act.activation(z[:, :, G0:G0 + HW_], z[:, :, G0:G0 + HW_], ACT.Silu).then_inc(sem("g_silu"), 1)
            act.activation(zs[0:NB, G0:G0 + HW_], zs[0:NB, G0:G0 + HW_], ACT.Silu).then_inc(sem("g_silu"), 1)
            act.wait_ge(sem("lb_less_max"), 2)
            act.activation(lbl[:, :, :], lbl[:, :, :], ACT.Exp).then_inc(sem("lb_exp"), 1)
            act.wait_ge(sem("f_ready"), 1)
            act.activation(logf, z[:, :, F0:F0 + HW_], ACT.Ln).then_inc(sem("logf_ready"), 1)
            for n, t in enumerate((1, 0)):
                act.wait_ge(sem("max_ready"), n + 1)
                w = P * (t + 1)
                for hd in range(HEADS):
                    act.activation(sc[:, hd * w:(hd + 1) * w], sc[:, hd * w:(hd + 1) * w], ACT.Exp,
                                   bias=nmax[:, t, hd:hd + 1], accum_out=psums[:, t, hd:hd + 1]).then_inc(sem("probs"), 1)
                act.activation(esink[:, t, :], dsink[:, t, :], ACT.Exp).then_inc(sem("esink_ready"), 1)
                for i in range(2 * (t + 1)):
                    act.wait_ge(sem("pT_made"), 4 * n + i + 1)
                    if n and i == 0:
                        act.wait_ge(sem("pv_made"), 1)
                    act.activation(pT[:, 4 * i:4 * i + 4, :], B[3 + i][:, :].rearrange("p (n q) -> p n q", n=4),
                                   ACT.Copy).then_inc(sem("pT_copied"), 1)
            for t in range(2):
                act.wait_ge(sem("hg_made"), 4 * t + 4)
                if t:
                    act.wait_ge(sem("G_made"), 8)
                    act.wait_ge(sem("lev_ready"), 7)
                act.activation(bT, B[0][:, :], ACT.Copy).then_inc(sem("hg_copied"), 1)
                act.activation(kkT, B[1][:, :], ACT.Copy).then_inc(sem("hg_copied"), 1)
                act.activation(qqT, B[2][:, :], ACT.Copy).then_inc(sem("hg_copied"), 1)
                if t:
                    act.wait_ge(sem("st_made"), 1)
                act.activation(ks, B[3][:, :], ACT.Exp).then_inc(sem("tail_exp"), 1)
                for n in range(7):
                    act.wait_ge(sem("lev_diff"), 14 * t + 2 * n + 2)
                    act.activation(lev[n % 2], lev[n % 2], ACT.Exp).then_inc(sem("lev_exp"), 1)
                if t:
                    act.wait_ge(sem("G_made"), 16)
                    act.wait_ge(sem("hg_copied"), 6)
                    act.activation(lev[0], bT, ACT.Exp).then_inc(sem("b_exp"), 1)
                    act.activation(eb, bT.rearrange("p (h t) -> p h t", h=HH)[:, :, P - 1], ACT.Exp).then_inc(sem("b_exp"), 1)
            act.wait_ge(sem("smax_ready"), 1)
            act.activation(ps[0:64, :], ps[0:64, :], ACT.Exp, bias=snm[0:64, :], accum_out=ssm[0:64, :]).then_inc(sem("sprobs"), 1)
            act.activation(sesk[0:64, :], snm[0:64, :], ACT.Exp, bias=sink64[0:64, :]).then_inc(sem("sprobs"), 1)
            act.wait_ge(sem("spv_made"), 2)
            act.activation(pv[0:64, :], B[2][0:64, 0:P], ACT.Copy).then_inc(sem("pv_copied"), 1)
            act.wait_ge(sem("gmeans"), 1)
            act.activation(groot[:, 0:10], gmean[:, 0:10], ACT.Sqrt).then_inc(sem("groots"), 1)
            act.wait_ge(sem("gmeans"), 2)
            act.activation(groot[0:NB, 10:15], gmean[0:NB, 10:15], ACT.Sqrt).then_inc(sem("groots"), 1)
            even_tiles("catT_made", "catT_copied_a")
            act.wait_ge(sem("gate1_made"), 1)
            act.wait_ge(sem("cat_ready"), 3)
            for n in range(2):
                act.activation(gt1[:, n * 512:(n + 1) * 512], B[5 + n][:, :], ACT.Copy).then_inc(sem("gate1_copied"), 1)
            act.wait_ge(sem("gate1_made"), 2)
            for n in range(2):
                act.activation(gt1s[0:NB, n * 512:(n + 1) * 512], B[5 + n][0:NB, :], ACT.Copy).then_inc(sem("gate1_copied"), 1)
            for t in range(3):
                act.wait_ge(sem("x1_ready"), t + 1)
                squares(t, "sums2")
            act.wait_ge(sem("means2"), 3)
            for t in range(3):
                root(t, "roots2")
            even_tiles("h2T_made", "h2T_copied_a")
            act.wait_ge(sem("top_ready"), 3)
            for t in range(3):
                act.activation(topw[0:NT[t], t, :], top8[0:NT[t], t, 0:TOPK], ACT.Exp, bias=ntop[0:NT[t], t:t + 1],
                               accum_out=tsum[0:NT[t], t:t + 1]).then_inc(sem("top_exp"), 1)

            def store(e, it, i):
                act.wait_ge(sem(f"y_stored{e}"), it * 32 + 1)
                act.wait_ge(chunks_used, it * PER + (PRE + 20 + 4 * e))
                act.activation(ysb[e], B[4 + e][:, :], ACT.Copy).then_inc(sem(f"y_copied{e}"), 1)
                act.wait_ge(sem(f"y_copied{e}"), it + 2)
                for a in range(2):
                    act.dma_start(y_dram[bass.ds(i * P + 64 * e, SLOTS), 512 * a:512 * (a + 1)],
                                  ysb[e][64 * a:64 * (a + 1), :]).then_inc(sem(f"y_stored{e}"), 16)

            act.wait_ge(sem("npass_ready"), 1)
            act.wait_ge(sem("stored"), 16 * N_STORED)
            passes = act.value_load(npass[0:1, 0:1], min_val=1, max_val=MAXPASS)
            count_from_one(act, "y_copied0", "y_copied1", "y_stored0", "y_stored1", "gT_copied")
            with act.Fori(0, passes) as p:
                act.wait_ge(sem("y_added"), p * (3 * TOPK) + 1)
                with act.Fori(0, PAIRS) as i:
                    it = act.snap(p * PAIRS + i)
                    act.wait_ge(sem("xT_made"), it * 2 + 3)
                    act.activation(xT[:, 4:8, :], B[7][:, :].rearrange("p (k t) -> p k t", k=4), ACT.Copy).then_inc(sem("xT_copied_a"), 1)
                    for e in range(2):
                        act.wait_ge(sem("glu_ready"), it * 2 + (e + 1))
                        act.activation(sg, glu, ACT.Sigmoid, scale=ALPHA).then_inc(sem("sig_ready"), 1)
                        act.wait_ge(sem("gT_made"), it * 2 + (e + 2))
                        act.activation(gT[e], B[6 + e][:, :], ACT.Copy).then_inc(sem("gT_copied"), 1)
                        if e:
                            store(0, it, i)
                    store(1, it, i)
            for t in range(3):
                act.wait_ge(sem("x2_ready"), t + 1)
                act.activation(moe[0:NT[t], t, :], x[0:NT[t], t, :], ACT.Square,
                               accum_out=ssum3[0:NT[t], t:t + 1]).then_inc(sem("sums3"), 1)
                act.wait_ge(sem("means3"), t + 1)
                root(t, "roots3")

        @block.tensor
        def _(pe):
            def landed(n):
                pe.wait_ge(full[n % RING], 16 * (n // RING + 1))

            def turn(out, in_, rows):
                return pe.transpose(out, in_, ident[0:rows, 0:rows])

            def pick_rows(out, q, j, tile):
                lo, hi = (0, P) if tile == 0 else (S, NTOK)
                return pe.matmul(out, lhsT=C("pick", slice(32 * j, 32 * j + 32))[:, lo:hi], rhs=mods[32 * j:32 * j + 32, q, :],
                                 start=True, stop=True)

            def transpose_tiles(src, made):
                for k in range(KT):
                    for t in range(3):
                        mm = turn(B[k][:, P * t:P * t + NT[t]], src[0:NT[t], t, P * k:P * (k + 1)], NT[t])
                    mm.then_inc(sem(made), 1)

            def modulation(first, bank):
                for k in range(N_ADA):
                    landed(first + k)
                    for j in range(4):
                        mm = pe.matmul(bank[32 * j:32 * j + 32, :], lhsT=scT[:, k, :], rhs=chunk(first + k)[:, 512 * j:512 * (j + 1)],
                                       start=(k == 0), stop=(k == N_ADA - 1), skip_group_check=True)
                    mm.then_inc(chunks_used, 1)

            pe.wait_ge(sem("const_full"), 16)
            pe.wait_ge(sem("c_silu"), 1)
            for k in range(KT):
                mm = turn(B[0][:, 16 * k:16 * k + 9], crow[0:9, P * k:P * (k + 1)], 9)
            mm.then_inc(sem("cT_made"), 1)
            pe.wait_ge(sem("scT_ready"), 1)
            modulation(0, B[1])
            pe.wait_ge(sem("mod_ready"), 1)
            for n in range(2):
                pick_rows(B[2 + n][:, :], 0, 2 + n, 0)
                mm = pick_rows(B[4 + n][:, :], 0, n, 0)
            mm.then_inc(sem("bc1_made"), 1)
            for n in range(2):
                pick_rows(B[6 + n][0:NB, :], 0, 2 + n, 2)
                mm = pick_rows(B[n][0:NB, :], 0, n, 2)
            mm.then_inc(sem("bc1_made"), 1)
            pe.wait_ge(sem("h_ready"), 3)
            transpose_tiles(h, "hT_made")
            pe.wait_ge(sem("hT_copied_a"), 4)
            pe.wait_ge(sem("hT_copied_d"), 4)
            for c in range(NZ):
                n = Z0 + c
                w = chunk(n).rearrange("p (k n) -> p k n", k=KT)
                landed(n)
                if c >= 4:
                    pe.wait_ge(sem("z_copied"), c - 3)
                for t in range(2):
                    for k in range(KT):
                        mm = pe.matmul(B[c % 4][:, ZC * t:ZC * (t + 1)], lhsT=hT[:, k, P * t:P * (t + 1)], rhs=w[:, k, :],
                                       start=(k == 0), stop=(k == KT - 1))
                mm.then_inc(sem("z_made"), 1)
                if c >= 2:
                    pe.wait_ge(sem("z_dec_copied"), c - 1)
                for k in range(KT):
                    for j in range(4):
                        mm = pe.matmul(B[4 + c % 2][32 * j:32 * j + 32, 0:64], lhsT=hT[:, k, S:S + 32], rhs=w[:, k, 64 * j:64 * (j + 1)],
                                       start=(k == 0), stop=(k == KT - 1), skip_group_check=True)
                mm.then_inc(chunks_used, 1)
            modulation(ADA1, B[6])
            modulation(ADA2, B[7])
            pe.wait_ge(sem("z_copied"), NZ)
            pe.wait_ge(sem("rotated"), 1)
            for t in range(2):
                for j in range(GRP):
                    mm = turn(B[t][:, P * j:P * (j + 1)], z[:, t, P * j:P * (j + 1)], P)
                mm.then_inc(sem("qk_made"), 1)
            for t in range(2):
                mm = turn(B[2][:, P * t:P * (t + 1)], z[:, t, K0:K0 + P], P)
            mm.then_inc(sem("qk_made"), 1)
            pe.wait_ge(sem("qk_copied"), 3)
            pe.wait_ge(sem("mod_ready"), 3)
            pe.wait_ge(sem("z_dec_copied"), NZ)
            for jj in range(2):
                for g in range(KV):
                    for j in (2 * jj, 2 * jj + 1):
                        mm = pe.matmul(B[3 + 2 * g + jj][:, 256 * (j % 2):256 * (j % 2 + 1)],
                                       lhsT=qT[64 * g:64 * g + 64, j, P:S], rhs=kT[64 * g:64 * g + 64, :], start=True, stop=True)
                    mm.then_inc(sem("sc_made"), 1)
            for g in range(KV):
                for j in range(GRP):
                    mm = pe.matmul(B[(7 + g) % 8][:, P * j:P * (j + 1)],
                                   lhsT=qT[64 * g:64 * g + 64, j, 0:P], rhs=kT[64 * g:64 * g + 64, 0:P], start=True, stop=True)
                mm.then_inc(sem("sc_made"), 1)
            for n, t in enumerate((1, 0)):
                nb = t + 1
                for i in range(2 * nb):
                    per = 4 // nb
                    pe.wait_ge(sem("probs"), 8 * n + per * (i + 1))
                    if n:
                        pe.wait_ge(sem("pT_copied"), i + 1)
                    for u in range(4):
                        m = 4 * i + u
                        mm = turn(B[3 + i][:, P * u:P * (u + 1)], sc[:, P * m:P * (m + 1)], P)
                    mm.then_inc(sem("pT_made"), 1)
                pe.wait_ge(sem("pT_copied"), 4 * n + 2 * nb)
                for hd in range(HEADS):
                    g = hd // GRP
                    for s in range(nb):
                        mm = pe.matmul(B[1 + n][:, HD * hd:HD * (hd + 1)], lhsT=pT[:, nb * hd + s, :],
                                       rhs=z[:, s, V0 + HD * g:V0 + HD * (g + 1)], start=(s == 0), stop=(s == nb - 1))
                mm.then_inc(sem("pv_made"), 1)
            pe.wait_ge(sem("k_ready"), 1)
            for t in range(2):
                if t == 0:
                    pe.wait_ge(sem("att_summed"), 2)
                    pe.wait_ge(sem("masked"), 6)
                else:
                    pe.wait_ge(sem("hg_copied"), 3)
                    pe.wait_ge(sem("st_copied"), 1)
                for hd in range(HH):
                    c = slice(P * hd, P * (hd + 1))
                    mm = pe.matmul(B[0][:, c], lhsT=logf[:, t, c], rhs=C("incl"), start=True, stop=True)
                mm.then_inc(sem("hg_made"), 1)
                for hd in range(HH):
                    mm = turn(B[1][:, P * hd:P * (hd + 1)], z[:, t, F0 + P * hd:F0 + P * (hd + 1)], P)
                mm.then_inc(sem("hg_made"), 1)
                for hd in range(HH):
                    mm = turn(B[2][:, P * hd:P * (hd + 1)], z[:, t, Q0 + P * hd:Q0 + P * (hd + 1)], P)
                mm.then_inc(sem("hg_made"), 1)
                pe.matmul(B[3][:, :], lhsT=C("after"), rhs=logf[:, t, :], start=True, stop=True).then_inc(sem("hg_made"), 1)
                pe.wait_ge(sem("hg_copied"), 3 * t + 3)
                for n in range(8):
                    g = 8 * t + n
                    if n:
                        pe.wait_ge(sem("lev_ready"), 7 * t + n)
                    if g >= 2:
                        pe.wait_ge(sem("lev_masked"), g - 1)
                    for hd in range(HH):
                        c = slice(P * hd, P * (hd + 1))
                        left = kkT if n == 0 else lev[(n - 1) % 2]
                        right = qqT if n == 0 else lev[(n - 1) % 2]
                        mm = pe.matmul(B[4 + n % 2][:, c], lhsT=left[:, c], rhs=right[:, c], start=True, stop=True)
                    mm.then_inc(sem("G_made"), 1)
                pe.wait_ge(sem("ks_ready"), t + 1)
                for hd in range(HH):
                    c = slice(P * hd, P * (hd + 1))
                    mm = pe.matmul(B[3][:, c], lhsT=ks[:, c], rhs=z[:, t, I0 + P * hd:I0 + P * (hd + 1)], start=True, stop=True)
                mm.then_inc(sem("st_made"), 1)
                pe.wait_ge(sem("lev_masked"), 8 * t + 8)
                if t:
                    pe.wait_ge(sem("qb_ready"), 1)
                for hd in range(HH):
                    c = slice(P * hd, P * (hd + 1))
                    mm = pe.matmul(B[6 + t][:, c], lhsT=amat[:, hd, :], rhs=z[:, t, I0 + P * hd:I0 + P * (hd + 1)],
                                   start=True, stop=(t == 0))
                    if t:
                        mm = pe.matmul(B[6 + t][:, c], lhsT=lev[0][:, c], rhs=st[:, c], start=False, stop=True)
                mm.then_inc(sem("hgo_made"), 1)
            pe.wait_ge(sem("cache_full"), 32)
            pe.wait_ge(sem("hg_copied"), 6)
            for b in range(NB):
                mm = turn(B[b // 4][:, P * (b % 4):P * (b % 4 + 1)], kc[:, b, :], P)
                if b % 4 == 3:
                    mm.then_inc(sem("kcT_made"), 1)
            pe.wait_ge(sem("rotated"), 2)
            turn(B[2][:, 0:NB], zs[0:NB, K0:K0 + P], NB)
            for j in range(GRP):
                mm = turn(B[2][:, 16 + 8 * j:24 + 8 * j], zs[0:NB, P * j:P * (j + 1)], NB)
            mm.then_inc(sem("snew_made"), 1)
            pe.wait_ge(sem("kcT_copied"), 2)
            pe.wait_ge(sem("snew_copied"), 3)
            for b in range(NB):
                mm = pe.matmul(B[4][0:64, 0:129], lhsT=qbd[:, 64 * b:64 * b + 64], rhs=kcT[:, b, :], start=(b == 0), stop=(b == NB - 1))
            mm.then_inc(sem("ss_made"), 1)
            pe.wait_ge(sem("k_ready"), 2)
            for hd in range(HH):
                turn(B[0][:, NB * hd:NB * (hd + 1)], zs[0:NB, Q0 + P * hd:Q0 + P * (hd + 1)], NB)
                mm = turn(B[0][:, 32 + NB * hd:32 + NB * (hd + 1)], zs[0:NB, F0 + P * hd:F0 + P * (hd + 1)], NB)
            mm.then_inc(sem("sqf_made"), 1)
            pe.wait_ge(sem("sprobs"), 1)
            turn(B[5][:, 0:64], ps[0:64, 0:P], 64).then_inc(sem("spT_made"), 1)
            pe.wait_ge(sem("pbd_ready"), 1)
            for b in range(NB):
                mm = pe.matmul(B[2][0:64, 0:P], lhsT=pbd[:, 64 * b:64 * b + 64], rhs=vc[:, b, :], start=(b == 0), stop=(b == NB - 1))
            mm.then_inc(sem("spv_made"), 1)
            pe.matmul(B[1][0:64, 0:P], lhsT=C("spread", slice(0, NB)), rhs=zs[0:NB, V0:V0 + P], start=True, stop=True).then_inc(sem("spv_made"), 1)
            pe.wait_ge(sem("state_final"), HH)
            pe.wait_ge(sem("smax_ready"), 1)
            for b in range(NB):
                pe.wait_ge(sem("km_ready"), b + 1)
                if b >= 2:
                    pe.wait_ge(sem("states_new"), HH * (b - 1))
                for hd in range(HH):
                    c = slice(P * hd, P * (hd + 1))
                    mm = pe.matmul(B[3 + b % 2][:, c], lhsT=km[b % 2][0:NB, c], rhs=zs[0:NB, I0 + P * hd:I0 + P * (hd + 1)], start=True, stop=True)
                mm.then_inc(sem("outer_made"), 1)
            pe.wait_ge(sem("states_new"), HH * NB)
            for b in range(NB):
                for hd in range(HH):
                    col = NB * hd + b
                    mm = pe.matmul(B[5][:, col:col + 1], lhsT=states[:, b, hd, :], rhs=sq[:, col:col + 1], start=True, stop=True)
            mm.then_inc(sem("soT_made"), 1)
            pe.wait_ge(sem("soT_copied"), 1)
            for hd in range(HH):
                mm = turn(B[0][0:NB, P * hd:P * (hd + 1)], soT[:, NB * hd:NB * (hd + 1)], P)
            mm.then_inc(sem("so_made"), 1)
            pe.wait_ge(sem("cat_ready"), 3)
            transpose_tiles(h, "catT_made")
            pe.wait_ge(sem("catT_copied_a"), 4)
            pe.wait_ge(sem("catT_copied_d"), 4)
            for n in range(2):
                mm = pick_rows(B[5 + n][:, :], 1, n, 0)
            mm.then_inc(sem("gate1_made"), 1)
            for c in range(4):
                n = WO0 + c
                w = two(chunk(n))
                landed(n)
                for k in (2 * c, 2 * c + 1):
                    for t in range(2):
                        for a in range(2):
                            pe.matmul(B[2 * t + a][:, :], lhsT=hT[:, k, P * t:P * (t + 1)], rhs=w[:, k % 2, 512 * a:512 * (a + 1)],
                                      start=(k == 0), stop=(k == KT - 1))
                    for j in range(4):
                        mm = pe.matmul(B[4][32 * j:32 * j + 32, 0:256], lhsT=hT[:, k, S:S + 32], rhs=w[:, k % 2, 256 * j:256 * (j + 1)],
                                       start=(k == 0), stop=(k == KT - 1), skip_group_check=True)
                mm.then_inc(chunks_used, 1)
            pe.wait_ge(sem("gate1_copied"), 2)
            for n in range(2):
                mm = pick_rows(B[5 + n][0:NB, :], 1, n, 2)
            mm.then_inc(sem("gate1_made"), 1)
            pe.wait_ge(sem("x1_ready"), 2)
            for n in range(2):
                pick_rows(B[n][:, :], 2, n, 0)
                mm = pick_rows(B[2 + n][:, :], 1, 2 + n, 0)
            mm.then_inc(sem("bc2_made"), 1)
            pe.wait_ge(sem("wo_dec_copied"), 1)
            pe.wait_ge(sem("gate1_copied"), 4)
            for n in range(2):
                pick_rows(B[4 + n][0:NB, :], 2, n, 2)
                mm = pick_rows(B[6 + n][0:NB, :], 1, 2 + n, 2)
            mm.then_inc(sem("bc2_made"), 1)
            pe.wait_ge(sem("h2_ready"), 3)
            transpose_tiles(h, "h2T_made")
            pe.wait_ge(sem("h2T_copied_a"), 4)
            pe.wait_ge(sem("h2T_copied_d"), 4)
            pe.wait_ge(sem("router_full"), 16)
            for k in range(KT):
                mm = pe.matmul(B[0][0:E, 0:NTOK], lhsT=wr[:, k, :], rhs=hT[:, k, 0:NTOK], start=(k == 0), stop=(k == KT - 1))
            mm.then_inc(sem("lgT_made"), 1)
            pe.wait_ge(sem("lgT_ready"), 1)
            for t in range(3):
                mm = turn(B[1][0:NT[t], E * t:E * (t + 1)], lgT[0:E, P * t:P * t + NT[t]], E)
            mm.then_inc(sem("lg_made"), 1)
            pe.wait_ge(sem("chosen_ready"), 3)
            for t in range(3):
                for u in range(t + 1):
                    left = C("before", slice(0, NT[t]))[:, 0:NT[t]] if u == t else C("ones")[:, 0:NT[t]]
                    pe.matmul(B[2][0:NT[t], E * t:E * (t + 1)], lhsT=left, rhs=chosen[0:NT[u], u, :], start=(u == 0), stop=(u == t))
            for u in range(3):
                mm = pe.matmul(B[3][0:1, 0:E], lhsT=C("ones", slice(0, NT[u]))[:, 0:1], rhs=chosen[0:NT[u], u, :], start=(u == 0), stop=(u == 2))
            mm.then_inc(sem("rank_made"), 1)

            pe.wait_ge(sem("npass_ready"), 1)
            pe.wait_ge(sem("bias_cleared"), 2)
            passes = pe.value_load(npass[0:1, 0:1], min_val=1, max_val=MAXPASS)
            total = pe.snap(passes * PAIRS)
            one = C("bias_row")
            count_from_one(pe, "xT_made", "gT_made", "bias_used0", "bias_used1")
            with pe.Fori(0, total) as it:
                def chunk_landed(n):
                    pe.wait_ge(full[n % RING], it * (16 * PER // RING) + 16 * (n // RING + 1))

                def turn_g(e):
                    pe.wait_ge(sem("g_ready"), it * 2 + (e + 2))
                    for j in range(4):
                        mm = turn(B[6 + e][:, P * j:P * (j + 1)], gg[e][:, P * j:P * (j + 1)], P)
                    mm.then_inc(sem("gT_made"), 1)

                pe.wait_ge(sem("x_full"), it * 16 + 16)
                pe.wait_ge(sem("gT_copied"), it * 2 + 1)
                for k in range(KT):
                    mm = turn(B[6 + k // 4][:, P * (k % 4):P * (k % 4 + 1)], xg[:, P * k:P * (k + 1)], P)
                    if k % 4 == 3:
                        mm.then_inc(sem("xT_made"), 1)
                for e in range(2):
                    pe.wait_ge(sem(f"bias_full{e}"), it * 32 + 32)
                    pe.wait_ge(sem("u_read"), it * 2 + 1)
                    for c in range(4):
                        a = c // 2
                        pe.matmul(B[2 * e + c % 2][64 * a:64 * a + 64, :], lhsT=one, rhs=bias[e][:, 512 * c:512 * (c + 1)],
                                  start=True, stop=False, skip_group_check=True)
                    if e == 0:
                        pe.wait_ge(sem("xT_copied_d"), it + 1)
                        pe.wait_ge(sem("xT_copied_a"), it + 1)
                    for k in range(KT):
                        if e and k == 4:
                            turn_g(0)
                        n = PRE + 8 * e + k
                        chunk_landed(n)
                        for c in (0, 2, 1, 3):
                            a = c // 2
                            mm = pe.matmul(B[2 * e + c % 2][64 * a:64 * a + 64, :], lhsT=xT[:, k, 64 * e:64 * e + 64],
                                           rhs=chunk(n)[:, 512 * c:512 * (c + 1)], start=False, stop=(k == KT - 1),
                                           skip_group_check=True)
                        mm.then_inc(chunks_used, 1)
                for e in range(2):
                    pe.wait_ge(sem(f"y_copied{e}"), it + 1)
                    for a in range(2):
                        pe.matmul(B[4 + e][64 * a:64 * a + 64, :], lhsT=one,
                                  rhs=bias[e][:, FF2 + 512 * a:FF2 + 512 * (a + 1)],
                                  start=True, stop=False, skip_group_check=True)
                    pe.wait_ge(sem("gT_copied"), it * 2 + (e + 2))
                    for k in range(KT):
                        n = PRE + 16 + 4 * e + k // 2
                        if k % 2 == 0:
                            chunk_landed(n)
                        if e == 0 and k == 4:
                            turn_g(1)
                        for a in range(2):
                            mm = pe.matmul(B[4 + e][64 * a:64 * a + 64, :],
                                           lhsT=gT[e].rearrange("p (j a t) -> p j a t", j=4, a=2)[:, k % 4, k // 4, :],
                                           rhs=two(chunk(n))[:, k % 2, 512 * a:512 * (a + 1)],
                                           start=False, stop=(k == KT - 1), skip_group_check=True)
                            if k == KT - 1 and a == 0:
                                mm.then_inc(sem(f"bias_used{e}"), 1)
                        if k % 2:
                            mm.then_inc(chunks_used, 1)
            for n in range(2):
                mm = pick_rows(B[n][:, :], 2, 2 + n, 0)
            mm.then_inc(sem("gate2_made"), 1)
            for n in range(2):
                mm = pick_rows(B[2 + n][0:NB, :], 2, 2 + n, 2)
            mm.then_inc(sem("gate2_made"), 1)

        @block.vector
        def _(dve):
            steps = [0]

            def link(ins):
                steps[0] += 1
                ins.then_inc(sem("dve_step"), 1)
                dve.wait_ge(sem("dve_step"), steps[0])

            dve.memset(scT[:, :, :], 0.0)
            dve.memset(hT[:, :, NTOK:288], 0.0)
            dve.memset(zeros[:, :], 0)
            dve.memset(ba[:, :, :], 0.0)
            dve.memset(gb[:, :, :], 0.0).then_inc(sem("cleared"), 1)
            dve.wait_ge(sem("cleared"), 1)

            def means(t, sums, signal):
                dve.wait_ge(sem(sums), t + 1)
                dve.tensor_scalar(ssum3[0:NT[t], t:t + 1], ssum3[0:NT[t], t:t + 1], 1.0 / D, EPS, ALU.mult, ALU.add).then_inc(sem(signal), 1)

            def scaled(t, roots, out):
                n = NT[t]
                dve.wait_ge(sem(roots), t + 1)
                link(dve.reciprocal(root3[0:n, t:t + 1], root3[0:n, t:t + 1]))
                link(dve.tensor_scalar(out, x[0:n, t, :], root3[0:n, t:t + 1], None, ALU.mult))

            for t in range(3):
                means(t, "sums1", "means1")
            for t in range(3):
                scaled(t, "roots1", h[0:NT[t], t, :])
            dve.wait_ge(sem("cT_made"), 1)
            dve.tensor_copy(scT[:, :, 0:9], B[0][:, 0:P].rearrange("p (k t) -> p k t", k=KT)[:, :, 0:9]).then_inc(sem("scT_ready"), 1)

            dve.wait_ge(sem("rows_full"), 16 * 14)
            link(dve.tensor_tensor(lb, lbl[:, 0, :], lbl[:, 1, :], ALU.max))
            for r in range(2):
                dve.tensor_tensor(lbl[:, r, :], lbl[:, r, :], lb, ALU.subtract).then_inc(sem("lb_less_max"), 1)

            def modulation(q, used, bank, fold):
                dve.wait_ge(sem("ada_rows_full"), 16 * 16)
                dve.wait_ge(chunks_used, used)
                done = dve.tensor_tensor(mods[:, q, :], bank[:, :], ba[:, q, :], ALU.add)
                if fold is None:
                    done.then_inc(sem("mod_ready"), 1)
                    return
                link(done)
                rows, g = fold
                dve.scalar_tensor_tensor(out=mods[rows, q, :], in0=mods[rows, q, :], scalar=1.0, in1=gb[rows, g, :],
                                         op0=ALU.add, op1=ALU.mult).then_inc(sem("mod_ready"), 1)

            modulation(0, N_ADA, B[1], (slice(64, 128), 0))

            def modulated(signal, made, scale, shift):
                for t in range(3):
                    n = NT[t]
                    s = 0 if t < 2 else 1
                    dve.wait_ge(sem(made), s + 1)
                    for a in range(2):
                        c = slice(512 * a, 512 * (a + 1))
                        link(dve.tensor_tensor(h[0:n, t, c], h[0:n, t, c], B[scale[s] + a][0:n, :], ALU.mult))
                        done = dve.tensor_tensor(h[0:n, t, c], h[0:n, t, c], B[shift[s] + a][0:n, :], ALU.add)
                        if a == 0:
                            link(done)
                    done.then_inc(sem(signal), 1)

            def odd_tiles(made, copied):
                for k in range(1, KT, 2):
                    dve.wait_ge(sem(made), k + 1)
                    dve.tensor_copy(hT[:, k, 0:NTOK], B[k][:, 0:NTOK]).then_inc(sem(copied), 1)

            modulated("h_ready", "bc1_made", (2, 6), (4, 0))
            odd_tiles("hT_made", "hT_copied_d")
            for c in range(NZ):
                dve.wait_ge(chunks_used, Z0 + c + 1)
                dve.tensor_copy(zq[:, c, :], B[4 + c % 2][:, 0:64]).then_inc(sem("z_dec_copied"), 1)

            def rotary(src, n, t0, nt):
                def part(lo):
                    return src.rearrange("p t (h d) -> p t h d", d=HD)[:, :, :, lo:lo + HALF]

                def table(name):
                    tab = C(name, slice(0, n)).rearrange("p (t f) -> p t f", t=3)[:, t0:t0 + nt, :]
                    return wide(tab.unsqueeze(2), 2, 10)

                def prod(i):
                    return rtmp[0:n, 0:nt, 80 * i:80 * (i + 1)].rearrange("p t (h f) -> p t h f", h=10)

                a, b = part(0), part(HALF)
                dve.tensor_tensor(prod(0), a, table("sin"), ALU.mult)
                link(dve.tensor_tensor(prod(1), b, table("sin"), ALU.mult))
                link(dve.tensor_tensor(a, a, table("cos"), ALU.mult))
                link(dve.tensor_tensor(b, b, table("cos"), ALU.mult))
                dve.tensor_tensor(a, a, prod(1), ALU.subtract)
                dve.tensor_tensor(b, b, prod(0), ALU.add).then_inc(sem("rotated"), 1)

            dve.wait_ge(sem("z_copied"), NZ)
            dve.wait_ge(sem("const_full"), 16)
            rotary(z[:, :, 0:AW + P], P, 0, 2)
            dve.wait_ge(sem("lb_exp"), 1)
            link(dve.tensor_tensor(lb, lbl[:, 0, :], lbl[:, 1, :], ALU.add))
            link(dve.reciprocal(lb, lb))
            link(dve.tensor_tensor(lb, lb, lbl[:, 0, :], ALU.mult))
            link(dve.tensor_scalar(oml, lb, -1.0, 1.0, ALU.mult, ALU.add))
            dve.wait_ge(sem("f_sig"), 1)
            f = z[:, :, F0:F0 + HW_]
            link(dve.tensor_tensor(f, f, wide(oml.unsqueeze(1), 1, 2), ALU.mult))
            dve.tensor_tensor(f, f, wide(lb.unsqueeze(1), 1, 2), ALU.add).then_inc(sem("f_ready"), 1)
            modulation(1, ADA1 + N_ADA, B[6], None)
            modulation(2, ADA2 + N_ADA, B[7], (slice(0, 64), 1))
            dve.wait_ge(sem("zs_full"), 128)
            rotary(zs[0:NB, 0:AW + P].unsqueeze(1), NB, 2, 1)
            dve.wait_ge(sem("f_sig"), 2)
            fs = zs[0:NB, F0:F0 + HW_]
            link(dve.tensor_tensor(fs, fs, oml[0:NB, :], ALU.mult))
            link(dve.tensor_tensor(fs, fs, lb[0:NB, :], ALU.add))
            dve.wait_ge(sem("logf_ready"), 1)
            dve.tensor_scalar(f, f, -1.0, 1.0, ALU.mult, ALU.add).then_inc(sem("k_ready"), 1)
            dve.tensor_scalar(oml[0:NB, :], fs, -1.0, 1.0, ALU.mult, ALU.add).then_inc(sem("k_ready"), 1)
            ksam = oml[0:NB, :]

            window = C("window")
            for n, t in enumerate((1, 0)):
                w = P * (t + 1)
                nb = 4 // (t + 1)
                if n:
                    dve.wait_ge(sem("pT_made"), 4)
                for i in range(8 // nb):
                    g, first = (i % 2, 2 * (i // 2)) if t else (i, 0)
                    bank = B[3 + 2 * g + i // 2] if t else B[(7 + g) % 8]
                    hd = GRP * g + first
                    dve.wait_ge(sem("sc_made"), 4 * n + i + 1)
                    ins = dve.scalar_tensor_tensor(
                        out=sc[:, hd * w:(hd + nb) * w].rearrange("p (m s) -> p m s", s=w),
                        in0=bank[:, :].rearrange("p (m s) -> p m s", s=w), scalar=HD ** -0.5,
                        in1=wide(window[:, 2 * P - w:2 * P].unsqueeze(1), 1, nb), op0=ALU.mult, op1=ALU.add)
                    ins.then_inc(sem("masked"), 1)
                dve.wait_ge(sem("masked"), 4 if n == 0 else 6)
                link(dve.tensor_reduce(mrow[:, t, :], sc[:, 0:HEADS * w].rearrange("p (m s) -> p m s", s=w), AX.X, ALU.max))
                link(dve.tensor_tensor(mrow[:, t, :], mrow[:, t, :], sinkb, ALU.max))
                link(dve.tensor_tensor(dsink[:, t, :], sinkb, mrow[:, t, :], ALU.subtract))
                dve.tensor_scalar(nmax[:, t, :], mrow[:, t, :], -1.0, None, ALU.mult).then_inc(sem("max_ready"), 1)
            for n, t in enumerate((1, 0)):
                dve.wait_ge(sem("esink_ready"), n + 1)
                link(dve.tensor_tensor(psums[:, t, :], psums[:, t, :], esink[:, t, :], ALU.add))
                link(dve.reciprocal(psums[:, t, :], psums[:, t, :]))
                dve.wait_ge(sem("pv_made"), n + 1)
                o = h[:, t, 0:AW]
                dve.tensor_tensor(o.rearrange("p (m d) -> p m d", d=HD), B[1 + n][:, :].rearrange("p (m d) -> p m d", d=HD),
                                  wide(psums[:, t, :].unsqueeze(2), 2, HD), ALU.mult).then_inc(sem("att_summed"), 1)
            dve.wait_ge(sem("att_summed"), 2)

            def mean_of(col, n):
                link(dve.tensor_scalar(gmean[0:n, col[0]:col[1]], gmean[0:n, col[0]:col[1]], 1.0, EPS, ALU.mult, ALU.add))

            lvl_mask = C("levels").bitcast(U32).rearrange("p (n t) -> p n t", n=8)
            for t in range(2):
                if t:
                    dve.wait_ge(sem("hgo_made"), 1)
                link(dve.memset(amat[:, :, :], 0.0))
                dve.wait_ge(sem("hg_copied"), 3 * t + 3)

                def diff(n):
                    m = LEVELS[n]
                    v = bT.rearrange("p (n two m) -> p n two m", two=2, m=m)
                    d = lev[n % 2].rearrange("p (n two m) -> p n two m", two=2, m=m)
                    ref = v[:, :, 0, m - 1:m]
                    ref = ref if m == 1 else wide(ref, 2, m)
                    if n >= 2:
                        dve.wait_ge(sem("G_made"), 8 * t + n)
                    elif t:
                        dve.wait_ge(sem("G_made"), 8)
                    dve.tensor_tensor(d[:, :, 0, :], ref, v[:, :, 0, :], ALU.subtract).then_inc(sem("lev_diff"), 1)
                    dve.tensor_tensor(d[:, :, 1, :], v[:, :, 1, :], ref, ALU.subtract).then_inc(sem("lev_diff"), 1)

                def weigh(n):
                    m = LEVELS[n]
                    d = lev[n % 2].rearrange("p (n two m) -> p n two m", two=2, m=m)
                    dve.wait_ge(sem("lev_exp"), 7 * t + n + 1)
                    dve.tensor_tensor(d[:, :, 0, :], d[:, :, 0, :], kkT.rearrange("p (n two m) -> p n two m", two=2, m=m)[:, :, 0, :], ALU.mult)
                    dve.tensor_tensor(d[:, :, 1, :], d[:, :, 1, :], qqT.rearrange("p (n two m) -> p n two m", two=2, m=m)[:, :, 1, :],
                                      ALU.mult).then_inc(sem("lev_ready"), 1)

                def take_level(n):
                    dve.wait_ge(sem("G_made"), 8 * t + n + 1)
                    dve.copy_predicated(amat[:, :, :], wide(lvl_mask[:, n, :].unsqueeze(1), 1, HH),
                                        B[4 + n % 2][:, :].rearrange("p (h t) -> p h t", h=HH)).then_inc(sem("lev_masked"), 1)

                diff(0)
                diff(1)
                take_level(0)
                for n in range(7):
                    weigh(n)
                    take_level(n + 1)
                    if n + 2 < 7:
                        diff(n + 2)
                dve.wait_ge(sem("tail_exp"), t + 1)
                dve.tensor_tensor(ks, ks, z[:, t, F0:F0 + HW_], ALU.mult).then_inc(sem("ks_ready"), 1)
                if t == 0:
                    dve.wait_ge(sem("st_made"), 1)
                    dve.tensor_copy(st, B[3][:, :]).then_inc(sem("st_copied"), 1)
                else:
                    dve.wait_ge(sem("b_exp"), 2)
                    dve.tensor_tensor(lev[0], lev[0], qqT, ALU.mult).then_inc(sem("qb_ready"), 1)
                    dve.wait_ge(sem("hgo_made"), 2)
                    dve.wait_ge(sem("st_made"), 2)
                    for hd in range(HH):
                        c = slice(P * hd, P * (hd + 1))
                        dve.scalar_tensor_tensor(out=st[:, c], in0=st[:, c], scalar=eb[:, hd:hd + 1], in1=B[3][:, c],
                                                 op0=ALU.mult, op1=ALU.add).then_inc(sem("state_final"), 1)
            for t in range(2):
                link(dve.tensor_tensor(amat[:, :, :].rearrange("p h t -> p (h t)"), h[:, t, 0:AW], h[:, t, 0:AW], ALU.mult))
                link(dve.tensor_reduce(gmean[:, t:t + 1], amat[:, :, :].rearrange("p h t -> p (h t)"), AX.X, ALU.add))
                dve.wait_ge(sem("hgo_made"), 2)
                link(dve.tensor_copy(h[:, t, AW:D], B[6 + t][:, :]))
                link(dve.tensor_tensor(amat[:, :, :].rearrange("p h t -> p (h t)"), h[:, t, AW:D], h[:, t, AW:D], ALU.mult))
                link(dve.tensor_reduce(gmean[:, 2 + 4 * t:6 + 4 * t], amat[:, :, :], AX.X, ALU.add))
            link(dve.tensor_scalar(gmean[:, 0:2], gmean[:, 0:2], 1.0 / AW, EPS, ALU.mult, ALU.add))
            dve.tensor_scalar(gmean[:, 2:10], gmean[:, 2:10], 1.0 / P, EPS, ALU.mult, ALU.add).then_inc(sem("gmeans"), 1)

            dve.wait_ge(sem("mod_ready"), 3)
            link(dve.memset(qbd, 0.0))
            for i in range(2):
                dve.wait_ge(sem("kcT_made"), i + 1)
                dve.tensor_copy(kcT[:, 4 * i:4 * i + 4, 0:P], B[i][:, :].rearrange("p (b s) -> p b s", b=4)).then_inc(sem("kcT_copied"), 1)
            dve.wait_ge(sem("snew_made"), 1)
            dve.tensor_copy(kcT[:, :, P], B[2][:, 0:NB]).then_inc(sem("snew_copied"), 1)
            for g in range(KV):
                r = slice(64 * g, 64 * g + 64)
                dve.tensor_copy(qbd[r, :].rearrange("p (b c) -> p b c", b=NB)[:, :, GRP * g:GRP * (g + 1)],
                                B[2][r, 16:48].rearrange("p (j b) -> p b j", j=GRP)).then_inc(sem("snew_copied"), 1)
            dve.wait_ge(sem("kcT_made"), 2)
            link(dve.memset(pbd, 0.0))
            dve.wait_ge(sem("ss_made"), 1)
            link(dve.tensor_scalar(ps[0:64, :], B[4][0:64, 0:129], HD ** -0.5, None, ALU.mult))
            link(dve.tensor_reduce(smx[0:64, :], ps[0:64, :], AX.X, ALU.max))
            dve.tensor_scalar(snm[0:64, :], smx[0:64, :], sink64[0:64, :], -1.0, ALU.max, ALU.mult).then_inc(sem("smax_ready"), 1)
            dve.wait_ge(sem("sqf_made"), 1)
            link(dve.tensor_copy(sq, B[0][:, 0:64]))
            onehot = C("onehot", slice(0, NB))

            def mask_keys(b):
                dve.tensor_scalar(km[b % 2][0:NB, :], ksam, onehot[:, b:b + 1], None, ALU.mult).then_inc(sem("km_ready"), 1)

            dve.wait_ge(sem("spT_made"), 1)
            dve.tensor_copy(pbd.rearrange("p (b c) -> p b c", b=NB)[:, :, 0:HEADS],
                            B[5][:, 0:64].rearrange("p (b h) -> p b h", b=NB)).then_inc(sem("pbd_ready"), 1)
            dve.wait_ge(sem("k_ready"), 2)
            mask_keys(0)
            mask_keys(1)
            dve.wait_ge(sem("states_full"), 16 * NB)
            for b in range(NB):
                dve.wait_ge(sem("outer_made"), b + 1)
                for hd in range(HH):
                    fcol = 32 + NB * hd + b
                    dve.scalar_tensor_tensor(out=states[:, b, hd, :], in0=states[:, b, hd, :], scalar=sq[:, fcol:fcol + 1],
                                             in1=B[3 + b % 2][:, P * hd:P * (hd + 1)], op0=ALU.mult, op1=ALU.add).then_inc(sem("states_new"), 1)
                if b + 2 < NB:
                    mask_keys(b + 2)
            dve.wait_ge(sem("sprobs"), 2)
            link(dve.tensor_tensor(ssm[0:64, :], ssm[0:64, :], sesk[0:64, :], ALU.add))
            link(dve.reciprocal(ssm[0:64, :], ssm[0:64, :]))
            dve.tensor_tensor(sra[0:64, :], ssm[0:64, :], C("group", slice(0, 64))[:, 0:1], ALU.mult)
            link(dve.tensor_tensor(srb[0:64, :], ssm[0:64, :], C("group", slice(0, 64))[:, 1:2], ALU.mult))
            dve.wait_ge(sem("pv_copied"), 1)
            link(dve.scalar_tensor_tensor(out=pv[0:64, :], in0=B[1][0:64, 0:P], scalar=ps[0:64, P:P + 1], in1=pv[0:64, :],
                                          op0=ALU.mult, op1=ALU.add))
            link(dve.tensor_scalar(o64[0:64, :], pv[0:64, 0:HD], sra[0:64, :], None, ALU.mult))
            dve.scalar_tensor_tensor(out=o64[0:64, :], in0=pv[0:64, HD:P], scalar=srb[0:64, :], in1=o64[0:64, :],
                                     op0=ALU.mult, op1=ALU.add).then_inc(sem("o64_ready"), 1)
            dve.wait_ge(sem("soT_made"), 1)
            dve.tensor_copy(soT, B[5][:, 0:HH * NB]).then_inc(sem("soT_copied"), 1)

            def normed(t, n, c0, h0, silu):
                link(dve.reciprocal(groot[0:n, c0:c0 + 1], groot[0:n, c0:c0 + 1]))
                link(dve.reciprocal(groot[0:n, h0:h0 + HH], groot[0:n, h0:h0 + HH]))
                dve.scalar_tensor_tensor(out=h[0:n, t, 0:AW], in0=h[0:n, t, 0:AW], scalar=groot[0:n, c0:c0 + 1],
                                         in1=g_att[0:n, :], op0=ALU.mult, op1=ALU.mult)
                for hd in range(HH):
                    c = slice(AW + P * hd, AW + P * (hd + 1))
                    ins = dve.scalar_tensor_tensor(out=h[0:n, t, c], in0=h[0:n, t, c], scalar=groot[0:n, h0 + hd:h0 + hd + 1],
                                                   in1=g_hg[0:n, P * hd:P * (hd + 1)], op0=ALU.mult, op1=ALU.mult)
                link(ins)
                dve.tensor_tensor(h[0:n, t, AW:D], h[0:n, t, AW:D], silu, ALU.mult).then_inc(sem("cat_ready"), 1)

            dve.wait_ge(sem("g_silu"), 2)
            dve.wait_ge(sem("groots"), 1)
            for t in range(2):
                normed(t, P, t, 2 + 4 * t, z[:, t, G0:G0 + HW_])
            dve.wait_ge(sem("so_made"), 1)
            dve.wait_ge(sem("o64_moved"), 16)
            link(dve.tensor_copy(h[0:NB, 2, AW:D], B[0][0:NB, :]))
            sqs = ks[0:NB, :]
            dve.wait_ge(sem("st_made"), 2)
            link(dve.tensor_tensor(sqs, h[0:NB, 2, 0:AW], h[0:NB, 2, 0:AW], ALU.mult))
            link(dve.tensor_reduce(gmean[0:NB, 10:11], sqs, AX.X, ALU.add))
            link(dve.tensor_tensor(sqs, h[0:NB, 2, AW:D], h[0:NB, 2, AW:D], ALU.mult))
            link(dve.tensor_reduce(gmean[0:NB, 11:15], sqs.rearrange("p (h v) -> p h v", h=HH), AX.X, ALU.add))
            link(dve.tensor_scalar(gmean[0:NB, 10:11], gmean[0:NB, 10:11], 1.0 / AW, EPS, ALU.mult, ALU.add))
            dve.tensor_scalar(gmean[0:NB, 11:15], gmean[0:NB, 11:15], 1.0 / P, EPS, ALU.mult, ALU.add).then_inc(sem("gmeans"), 1)
            dve.wait_ge(sem("groots"), 2)
            normed(2, NB, 10, 11, zs[0:NB, G0:G0 + HW_])
            link(dve.memset(hT[:, :, NTOK:288], 0.0))
            odd_tiles("catT_made", "catT_copied_d")
            dve.wait_ge(chunks_used, PRE)
            dve.tensor_copy(zq[:, 0:4, :], B[4][:, 0:256].rearrange("p (c n) -> p c n", c=4)).then_inc(sem("wo_dec_copied"), 1)
            dve.wait_ge(sem("gate1_copied"), 2)
            for t in range(2):
                for a in range(2):
                    c = slice(512 * a, 512 * (a + 1))
                    ins = dve.tensor_tensor(tmp[:, c], B[2 * t + a][:, :], gt1[:, c], ALU.mult)
                link(ins)
                dve.tensor_tensor(x[:, t, :], x[:, t, :], tmp, ALU.add).then_inc(sem("x1_ready"), 1)
                dve.wait_ge(sem("x1_ready"), t + 1)
            dve.wait_ge(sem("gate1_copied"), 4)
            dve.wait_ge(sem("wo_dec_full"), 64)
            link(dve.tensor_tensor(tmps[0:NB, :], tmps[0:NB, :], gt1s[0:NB, :], ALU.mult))
            dve.tensor_tensor(x[0:NB, 2, :], x[0:NB, 2, :], tmps[0:NB, :], ALU.add).then_inc(sem("x1_ready"), 1)
            dve.wait_ge(sem("x1_ready"), 3)
            for t in range(3):
                means(t, "sums2", "means2")
            for t in range(3):
                scaled(t, "roots2", h[0:NT[t], t, :])
            modulated("h2_ready", "bc2_made", (0, 4), (2, 6))
            odd_tiles("h2T_made", "h2T_copied_d")
            dve.tensor_copy(tok_i[:, :], C("tok"))
            dve.wait_ge(sem("lgT_made"), 1)
            dve.tensor_scalar(lgT[0:E, :], B[0][0:E, 0:NTOK], brout[0:E, :], None, ALU.add).then_inc(sem("lgT_ready"), 1)
            dve.wait_ge(sem("lg_made"), 1)
            for t in range(3):
                n = NT[t]
                link(dve.tensor_copy(lg[0:n, t, :], B[1][0:n, E * t:E * (t + 1)]))
                link(dve.max(top8[0:n, t, :], lg[0:n, t, :]))
                dve.tensor_scalar(ntop[0:n, t:t + 1], top8[0:n, t, 0:1], -1.0, None, ALU.mult).then_inc(sem("top_ready"), 1)
                link(dve.max_index(top8i[0:n, t, :], top8[0:n, t, :], lg[0:n, t, :]))
                link(dve.tensor_copy(topf[0:n, t, :], top8i[0:n, t, 0:TOPK]))
                for k in range(TOPK):
                    link(dve.tensor_scalar(onek[0:n, t, k, :], C("iota", slice(0, n)), topf[0:n, t, k:k + 1], None, ALU.is_equal))
                link(dve.tensor_tensor(chosen[0:n, t, :], onek[0:n, t, 0, :], onek[0:n, t, 1, :], ALU.add))
                link(dve.tensor_tensor(chosen[0:n, t, :], chosen[0:n, t, :], onek[0:n, t, 2, :], ALU.add))
                dve.tensor_tensor(chosen[0:n, t, :], chosen[0:n, t, :], onek[0:n, t, 3, :], ALU.add).then_inc(sem("chosen_ready"), 1)
            dve.wait_ge(sem("rank_made"), 1)
            for t in range(3):
                n = NT[t]
                rank = B[2][0:n, E * t:E * (t + 1)]
                link(dve.tensor_scalar(over[0:n, :], rank, float(SLOTS), None, ALU.is_ge))
                for m in range(2, MAXPASS):
                    link(dve.tensor_scalar(hit[0:n, :], rank, float(SLOTS * m), None, ALU.is_ge))
                    link(dve.tensor_tensor(over[0:n, :], over[0:n, :], hit[0:n, :], ALU.add))
                link(dve.tensor_tensor(slotf[0:n, :], rank, C("e64", slice(0, n)), ALU.add))
                link(dve.scalar_tensor_tensor(out=slotf[0:n, :], in0=over[0:n, :], scalar=-float(SLOTS), in1=slotf[0:n, :],
                                              op0=ALU.mult, op1=ALU.add))
                for k in range(TOPK):
                    link(dve.tensor_tensor(hit[0:n, :], onek[0:n, t, k, :], over[0:n, :], ALU.mult))
                    link(dve.tensor_reduce(passf[0:n, t, k:k + 1], hit[0:n, :], AX.X, ALU.add))
                    link(dve.tensor_tensor(hit[0:n, :], onek[0:n, t, k, :], slotf[0:n, :], ALU.mult))
                    link(dve.tensor_reduce(topf[0:n, t, k:k + 1], hit[0:n, :], AX.X, ALU.add))
                    dve.tensor_copy(row_u[0:n, t, k:k + 1], topf[0:n, t, k:k + 1]).then_inc(sem("rows_ready"), 1)
                    dve.scalar_tensor_tensor(out=slot_u[0:n, t, k:k + 1], in0=passf[0:n, t, k:k + 1], scalar=float(ROWS),
                                             in1=topf[0:n, t, k:k + 1], op0=ALU.mult, op1=ALU.add).then_inc(sem("slots_ready"), 1)
            link(dve.tensor_reduce(cmax[0:1, :], B[3][0:1, 0:E], AX.X, ALU.max))
            link(dve.memset(chit[0:1, 0:1], 1.0))
            for m in range(1, MAXPASS):
                link(dve.tensor_scalar(chit[0:1, m:m + 1], cmax[0:1, :], float(SLOTS * m), None, ALU.is_gt))
            link(dve.tensor_reduce(csum[0:1, :], chit[0:1, :], AX.X, ALU.add))
            for t in range(3):
                n = NT[t]
                dve.wait_ge(sem("top_exp"), t + 1)
                link(dve.reciprocal(tsum[0:n, t:t + 1], tsum[0:n, t:t + 1]))
                link(dve.tensor_scalar(topw[0:n, t, :], topw[0:n, t, :], tsum[0:n, t:t + 1], None, ALU.mult))
            dve.wait_ge(sem("stored"), 16 * N_STORED)
            for e in range(2):
                dve.memset(bias[e], 0.0).then_inc(sem("bias_cleared"), 1)
            dve.wait_ge(sem("bias_cleared"), 2)
            link(dve.memset(moe[:, :, :], 0.0))
            link(dve.memset(now, 0.0))
            dve.tensor_copy(npass[:, :], csum[0:1, :]).then_inc(sem("npass_ready"), 1)
            dve.wait_ge(sem("npass_ready"), 1)

            passes = dve.value_load(npass[0:1, 0:1], min_val=1, max_val=MAXPASS)
            count_from_one(dve, "g_ready", "u_read", "y_added")
            with dve.Fori(0, passes) as p:
                with dve.Fori(0, PAIRS) as i:
                    it = dve.snap(p * PAIRS + i)
                    dve.wait_ge(sem("xT_made"), it * 2 + 2)
                    dve.tensor_copy(xT[:, 0:4, :], B[6][:, :].rearrange("p (k t) -> p k t", k=4)).then_inc(sem("xT_copied_d"), 1)
                    for e in range(2):
                        dve.wait_ge(chunks_used, it * PER + (PRE + 8 * (e + 1)))
                        dve.wait_ge(sem("g_ready"), it * 2 + (e + 1))
                        for b in range(2):
                            u = B[2 * e + b][:, :].rearrange("p (n two) -> p n two", two=2)
                            ins = dve.tensor_scalar(glu[:, 256 * b:256 * (b + 1)], u[:, :, 0], LIMIT, None, ALU.min)
                        ins.then_inc(sem("glu_ready"), 1)
                        for b in range(2):
                            u = B[2 * e + b][:, :].rearrange("p (n two) -> p n two", two=2)
                            ins = dve.tensor_scalar(lin[:, 256 * b:256 * (b + 1)], u[:, :, 1], LIMIT, -LIMIT, ALU.min, ALU.max)
                        ins.then_inc(sem("u_read"), 1)
                        dve.wait_ge(sem("u_read"), it * 2 + (e + 2))
                        dve.scalar_tensor_tensor(out=lin, in0=lin, scalar=1.0, in1=glu, op0=ALU.add, op1=ALU.mult).then_inc(sem("lin_ready"), 1)
                        dve.wait_ge(sem("lin_ready"), it * 2 + (e + 1))
                        dve.wait_ge(sem("sig_ready"), it * 2 + (e + 1))
                        dve.wait_ge(sem("gT_made"), it * 2 + 1)
                        dve.tensor_tensor(gg[e], lin, sg, ALU.mult).then_inc(sem("g_ready"), 1)
                for t in range(3):
                    n = NT[t]
                    dve.tensor_scalar(passw[0:n, t, :], passf[0:n, t, :], now[0:n, :], None, ALU.is_equal).then_inc(sem("pass_step"), 1)
                    dve.wait_ge(sem("pass_step"), p * 7 + (2 * t + 1))
                    dve.tensor_tensor(passw[0:n, t, :], passw[0:n, t, :], topw[0:n, t, :], ALU.mult).then_inc(sem("pass_step"), 1)
                    dve.wait_ge(sem("pass_step"), p * 7 + (2 * t + 2))
                    for k in range(TOPK):
                        dve.wait_ge(sem(f"y_full{k}"), p * 48 + 16 * (t + 1))
                        dve.scalar_tensor_tensor(out=moe[0:n, t, :], in0=yk[k][0:n, :], scalar=passw[0:n, t, k:k + 1],
                                                 in1=moe[0:n, t, :], op0=ALU.mult, op1=ALU.add).then_inc(sem("y_added"), 1)
                        dve.wait_ge(sem("y_added"), p * (3 * TOPK) + (TOPK * t + k + 2))
                dve.tensor_scalar(now, now, 1.0, None, ALU.add).then_inc(sem("pass_step"), 1)
                dve.wait_ge(sem("pass_step"), p * 7 + 7)
            dve.wait_ge(sem("gate2_made"), 2)
            for n in range(2):
                dve.tensor_copy(gt2[0][:, 512 * n:512 * (n + 1)], B[n][:, :])
                ins = dve.tensor_copy(gt2[1][0:NB, 512 * n:512 * (n + 1)], B[2 + n][0:NB, :])
            link(ins)
            dve.wait_ge(sem("gfin_full"), 16)
            for t in range(3):
                n = NT[t]
                link(dve.tensor_tensor(moe[0:n, t, :], moe[0:n, t, :], gt2[t // 2][0:n, :], ALU.mult))
                dve.tensor_tensor(x[0:n, t, :], x[0:n, t, :], moe[0:n, t, :], ALU.add).then_inc(sem("x2_ready"), 1)
                dve.wait_ge(sem("x2_ready"), t + 1)
                means(t, "sums3", "means3")
                scaled(t, "roots3", x[0:n, t, :])
                dve.tensor_tensor(x[0:n, t, :], x[0:n, t, :], g_fin[0:n, :], ALU.mult).then_inc(sem("result"), 1)


INS = ["x_prompt", "x_sample", "c_prompt", "c_sample", "cache_k_win", "cache_v_win", "state_hgrn", "w_ada", "b_ada",
       "g_mix", "g_ffn", "w_in", "attn_sinks", "g_attn_out", "hg_lb_logits", "g_hg_out", "w_out", "w_router",
       "b_router", "w_up", "b_up", "w_down", "b_down", "g_final"]
OUTS = [("yp", (1, S, D)), ("ys", (NB, 1, D)), ("kwp", (1, 1, WIN, KV, HD)), ("vwp", (1, 1, WIN, KV, HD)),
        ("hgp", (1, 1, HH, P, P)), ("kws", (1, NB, WIN, KV, HD)), ("vws", (1, NB, WIN, KV, HD)),
        ("hgs", (1, NB, HH, P, P))]


def kernel(**inputs):
    import concourse.bacc as bacc
    from concourse.bass_utils import run_bass_kernel_spmd as run

    nc = bacc.Bacc("TRN2", target_bir_lowering=False, num_devices=1)
    arrays, ins, outs = {}, {}, {}
    given = {name: np.ascontiguousarray(inputs[name]) for name in INS}
    given["const"] = constants()
    for name, a in given.items():
        arrays[f"in_{name}"] = a
        ins[name] = nc.dram_tensor(f"in_{name}", a.shape, mybir.dt.from_np(a.dtype), kind="ExternalInput").ap()
    for name, shape in OUTS:
        outs[name] = nc.dram_tensor(f"out_{name}", shape, F32, kind="ExternalOutput").ap()
    hybrid_layer(nc, ins, outs)
    r = run(nc, [arrays], core_ids=[0])
    return tuple(r.results[0][f"out_{name}"] for name, _ in OUTS)
```

```python
from contextlib import ExitStack

import numpy as np

import concourse.bass as bass
from concourse import mybir

F32 = mybir.dt.float32
I32 = mybir.dt.int32
U32 = mybir.dt.uint32
ALU = mybir.AluOpType
ACT = mybir.ActivationFunctionType
AX = mybir.AxisListType

P = 128
D = 1024
KT = D // P
S = 256
NB = 8
NTOK = S + NB
HEADS, KV, HD = 8, 2, 64
GRP = HEADS // KV
WIN = 128
ROT = HD // 4
HALF = ROT // 2
AW = HEADS * HD
HH = 4
HW_ = HH * P
QKV = AW + 2 * KV * HD
IN_COLS = QKV + 4 * HW_
ZC = 256
NZ = IN_COLS // ZC
E = 32
TOPK = 4
FF2 = 2 * D
EPS = 1e-5
PAST = 2048
SLOTS = 64
ARENA = 29300
N_STORED = 2 + 2 + 2 + 1 + NB
ROWS = E * SLOTS
MAXPASS = -(-NTOK // SLOTS)
PAIRS = E // 2
LIMIT = 7.0
ALPHA = 1.702
NEG = -1e30
LEVELS = [1 << i for i in range(7)]

RING = 8
RING2 = 12
CH = 2048
N_ADA = 8
Z0 = N_ADA
ADA1 = Z0 + NZ
ADA2 = ADA1 + N_ADA
WO0 = ADA2 + N_ADA
PRE = WO0 + 4
PER = 24

_COLS = {}
_at = 0
for _name, _n in (("ident", P), ("incl", P), ("after", P), ("before", P), ("ones", P), ("levels", 8 * P),
                  ("window", 2 * P), ("pick", P), ("cos", 3 * HALF), ("sin", 3 * HALF), ("e64", E),
                  ("iota", E), ("tok", 3), ("spread", 64), ("onehot", NB), ("bias_row", SLOTS), ("group", 2)):
    _COLS[_name] = (_at, _at + _n)
    _at += _n
NCONST = _at


def constants():
    c = np.zeros((P, NCONST), np.float32)

    def put(name, a, rows=P):
        lo, hi = _COLS[name]
        c[:rows, lo:hi] = np.asarray(a, np.float32).reshape(rows, hi - lo)

    r = np.arange(P)
    put("ident", np.eye(P))
    put("incl", r[:, None] <= r[None, :])
    put("after", r[:, None] > r[None, :])
    put("before", r[:, None] < r[None, :])
    put("ones", np.ones((P, P)))
    masks = [np.eye(P)]
    for m in LEVELS:
        same = r[:, None] // (2 * m) == r[None, :] // (2 * m)
        masks.append(same & (r[:, None] % (2 * m) < m) & (r[None, :] % (2 * m) >= m))
    put("levels", np.stack(masks, 1))
    diff = r[:, None] + P - np.arange(2 * P)[None, :]
    put("window", np.where((diff >= 0) & (diff <= WIN), 0.0, NEG))
    pick = np.zeros((P, P))
    pick[::32] = 1
    put("pick", pick)
    inv = np.float32(500000.0) ** (-(np.arange(HALF, dtype=np.float32) * np.float32(2.0) / np.float32(ROT)))
    pos = np.zeros((3, P), np.float32)
    pos[0], pos[1], pos[2] = r, r + P, PAST
    ang = (pos[:, :, None] * inv.astype(np.float32)[None, None, :]).astype(np.float32)
    put("cos", np.cos(ang).transpose(1, 0, 2))
    put("sin", np.sin(ang).transpose(1, 0, 2))
    put("e64", np.tile(np.arange(E) * SLOTS, (P, 1)))
    put("iota", np.tile(np.arange(E), (P, 1)))
    put("tok", np.stack([r, r + P, r + 2 * P], 1))
    put("spread", np.repeat(np.eye(NB), HEADS, 1), NB)
    put("onehot", np.eye(NB), NB)
    br = np.zeros((P, SLOTS))
    br[0] = 1
    put("bias_row", br)
    h = np.arange(64) % HEADS
    put("group", np.stack([h < GRP, h >= GRP], 1), 64)
    return c


def wide(ap, dim, n):
    shape = list(ap.shape)
    shape[dim] = n
    return ap.broadcast_to(shape)


def hybrid_layer(nc, A, O):
    with ExitStack() as ctx:
        sems = {}

        def sem(name):
            if name not in sems:
                sems[name] = ctx.enter_context(nc.semaphore(name))
            return sems[name]

        def sb(name, shape, dt=F32):
            return ctx.enter_context(nc.sbuf_tensor(name, shape, dt))

        B = [ctx.enter_context(nc.psum_tensor(f"bank{i}", [P, 512], F32)) for i in range(8)]

        const = sb("const", [P, NCONST])

        def C(name, rows=slice(0, P)):
            lo, hi = _COLS[name]
            return const[rows, lo:hi]

        ident = C("ident")
        ring = sb("ring", [P, RING, CH])
        x = sb("x", [P, 3, D])
        mods = sb("mods", [P, 3, 512])
        slot_u = sb("slot_u", [P, 3, TOPK], U32)
        row_u = sb("row_u", [P, 3, TOPK], U32)
        topw = sb("topw", [P, 3, TOPK])
        npass = sb("npass", [1, 1], I32)
        small = sb("small", [P, 256])
        zeros = sb("zeros", [P, MAXPASS * ROWS // P], I32)
        tok_i = sb("tok_i", [P, 3], I32)
        idx = sb("idx", [P, 1], I32)

        arena = sb("arena", [P, ARENA])
        top = [0]

        def take(n, at=None):
            lo = top[0] if at is None else at
            if at is None:
                top[0] += n
            assert lo + n <= ARENA, (lo, n)
            return arena[:, lo:lo + n]

        z_at = top[0]
        z = take(2 * IN_COLS).rearrange("p (t c) -> p t c", t=2)
        zs_at = top[0]
        zs = take(IN_COLS)
        zq = take(NZ * 64).rearrange("p (c n) -> p c n", c=NZ)
        h = take(3 * D).rearrange("p (t c) -> p t c", t=3)
        hT_at = top[0]
        hT = take(KT * 288).rearrange("p (k t) -> p k t", k=KT)
        bT, kkT, qqT = (take(HW_, hT_at + n * HW_) for n in range(3))
        lb, oml, g_att, g_hg = (take(512) for _ in range(4))
        ada_at = top[0]
        ba = take(3 * 512).rearrange("p (q c) -> p q c", q=3)
        gb = take(2 * 512).rearrange("p (q c) -> p q c", q=2)
        scT = take(KT * 32).rearrange("p (k t) -> p k t", k=KT)
        take(840)
        kc = take(NB * P, ada_at).rearrange("p (b c) -> p b c", b=NB)
        vc = take(NB * P, ada_at + 1024).rearrange("p (b c) -> p b c", b=NB)
        kcT = take(NB * 129, ada_at + 2048).rearrange("p (b s) -> p b s", b=NB)
        qbd = take(NB * 72, ada_at + 3080)
        pbd = take(NB * 72, ada_at)
        att_at = top[0]
        qT = take(4 * S).rearrange("p (j t) -> p j t", j=4)
        kT = take(S)
        sc_at = top[0]
        sc = take(HEADS * 2 * P)
        pT = take(HEADS * 2 * P).rearrange("p (n q) -> p n q", q=P)
        crow = take(D, sc_at)
        states = take(NB * HW_, att_at).rearrange("p (b h v) -> p b h v", b=NB, h=HH)
        km = [take(HW_, att_at + 4096 + n * HW_) for n in range(2)]
        logf_at = top[0]
        logf = take(2 * HW_).rearrange("p (t c) -> p t c", t=2)
        lbl = take(2 * 512, logf_at).rearrange("p (q c) -> p q c", q=2)
        ps = take(129, logf_at)
        pv = take(P, logf_at + 129)
        o64 = take(64, logf_at + 257)
        sq = take(2 * HH * NB, logf_at + 321)
        soT = take(HH * NB, logf_at + 385)
        lev = [take(HW_) for _ in range(2)]
        amat = take(HW_).rearrange("p (h t) -> p h t", h=HH)
        ks = take(HW_)
        st = take(HW_)
        rows0s = take(2 * D, z_at)
        rows1 = take(2 * D, z_at)
        scale2 = take(D, z_at + 2 * D)
        tmps = take(D, z_at + 3 * D)
        lgT = take(NTOK, z_at + 4 * D)
        lg = take(3 * E, z_at + 4 * D + 264).rearrange("p (t e) -> p t e", t=3)
        chosen = take(3 * E, z_at + 4 * D + 360).rearrange("p (t e) -> p t e", t=3)
        onek = take(3 * TOPK * E, z_at + 4 * D + 456).rearrange("p (t k e) -> p t k e", t=3, k=TOPK)
        hit = take(3 * TOPK * E, zs_at).rearrange("p (t k e) -> p t k e", t=3, k=TOPK)
        over = take(3 * E, zs_at + 384)
        slotf = take(3 * E, zs_at + 480)
        wr = take(KT * E, z_at + 5 * D).rearrange("p (k e) -> p k e", k=KT)
        bias = [take(FF2 + D, n * 3 * D) for n in range(2)]
        top2 = [6 * D]

        def later(n):
            top2[0] += n
            return take(n, top2[0] - n)

        xg = later(D)
        xT = later(D).rearrange("p (k t) -> p k t", k=KT)
        glu, lin, sg = (later(512) for _ in range(3))
        gg = [later(512) for _ in range(2)]
        gT = [later(512) for _ in range(2)]
        ysb = [later(512) for _ in range(2)]
        yk = [[ring[:, (t * TOPK + k) // 2, D * (k % 2):D * (k % 2 + 1)] for k in range(TOPK)] for t in range(3)]
        moe = later(3 * D).rearrange("p (t c) -> p t c", t=3)
        g_fin = later(D)
        more_ring = [later(CH) for n in range(RING2 - RING)]
        gate2 = later(D)
        rows2s = later(2 * D)
        rows1s = take(2 * D, zs_at + 640)

        scol = [0]

        def stat(n):
            scol[0] += n
            return small[:, scol[0] - n:scol[0]]

        ssum3, root3 = stat(3), stat(3)
        sinkb, sink64, brout = stat(HEADS), stat(1), stat(1)
        mrow = stat(2 * HEADS).rearrange("p (t h) -> p t h", t=2)
        nmax = stat(2 * HEADS).rearrange("p (t h) -> p t h", t=2)
        dsink = stat(2 * HEADS).rearrange("p (t h) -> p t h", t=2)
        esink = stat(2 * HEADS).rearrange("p (t h) -> p t h", t=2)
        psums = stat(2 * HEADS).rearrange("p (t h) -> p t h", t=2)
        smx, snm, ssm, sesk, sra, srb = (stat(1) for _ in range(6))
        gmean, groot = stat(15), stat(15)
        eb = stat(HH)
        top8 = stat(24).rearrange("p (t k) -> p t k", t=3)
        topf = stat(12).rearrange("p (t k) -> p t k", t=3)
        ntop, tsum = stat(3), stat(3)
        cmax, csum = stat(1), stat(1)
        chit = stat(MAXPASS)
        passf = stat(12).rearrange("p (t k) -> p t k", t=3)
        now, passw = stat(1), stat(12).rearrange("p (t k) -> p t k", t=3)
        top8i = sb("top8i", [P, 24], U32)[:, :].rearrange("p (t k) -> p t k", t=3)
        rtmp = take(2 * 160, sc_at + 2048).rearrange("p (t n) -> p t n", t=2)

        mod_dram = nc.dram_tensor("mod_rows", [2, 1 + NB, 2 * D], F32, kind="Internal").ap()
        h2_dram = nc.dram_tensor("h2_rows", [NTOK, D], F32, kind="Internal").ap()
        y_dram = nc.dram_tensor("y_rows", [ROWS, D], F32, kind="Internal").ap()
        list_dram = nc.dram_tensor("slot_tokens", [MAXPASS * ROWS, 1], I32, kind="Internal").ap()

        full = [sem(f"ring_full{i}") for i in range(RING2)]
        chunks_used = sem("chunks_used")

        NT = [P, P, NB]
        Q0, F0, I0, G0 = QKV, QKV + HW_, QKV + 2 * HW_, QKV + 3 * HW_
        K0, V0 = AW, AW + P

        w_ada = A["w_ada"][0].rearrange("(k p) n -> k p n", p=P)
        w_in = A["w_in"][0].rearrange("(k p) n -> p k n", p=P)
        w_out = A["w_out"][0].rearrange("(c two p) n -> c p two n", two=2, p=P)
        w_up = A["w_up"][0].rearrange("e (k p) n -> (e k) p n", p=P)
        w_down = A["w_down"][0].rearrange("e (c two p) n -> (e c) p two n", two=2, p=P)

        def place(n):
            c = (n - PRE) % RING2
            return n % RING if n < PRE else (PRE + c) % RING if c < RING else c

        def loads(n):
            return sum(place(m) == place(n) for m in range(n + 1))

        def chunk(n):
            return ring[:, place(n), :] if place(n) < RING else more_ring[place(n) - RING]

        def two(ap):
            return ap.rearrange("p (two n) -> p two n", two=2)

        def count_from_one(engine, *names):
            for name in names:
                engine.sem_inc(sem(name), 1)

        def y_full(t, k):
            return sem(f"y_full{t}" if t else f"y_full0_{k // 2}")

        block = ctx.enter_context(nc.Block())

        @block.sync
        def _(sp):
            def room(n):
                if n >= RING:
                    sp.wait_ge(chunks_used, n - RING + 1)

            for k in range(N_ADA):
                room(k)
                sp.dma_start(chunk(k), w_ada[k, :, 0:CH]).then_inc(full[place(k)], 16)
            for c in range(NZ):
                room(Z0 + c)
                if c == 3:
                    sp.wait_ge(sem("mod_rows0_full"), 64)
                sp.dma_start(chunk(Z0 + c).rearrange("p (k n) -> p k n", k=KT),
                             w_in[:, :, c * ZC:(c + 1) * ZC]).then_inc(full[place(Z0 + c)], 16)
            for q, first in ((1, ADA1), (2, ADA2)):
                for k in range(N_ADA):
                    room(first + k)
                    sp.dma_start(chunk(first + k), w_ada[k, :, q * CH:(q + 1) * CH]).then_inc(full[place(first + k)], 16)
            for c in range(4):
                room(WO0 + c)
                sp.dma_start(two(chunk(WO0 + c)), w_out[c]).then_inc(full[place(WO0 + c)], 16)

            def expert_chunk(c, pair):
                n = PRE + c
                if c < 16:
                    sp.dma_start(chunk(n), w_up[pair * 16 + c]).then_inc(full[place(n)], 16)
                else:
                    sp.dma_start(two(chunk(n)), w_down[pair * 8 + (c - 16)]).then_inc(full[place(n)], 16)

            for c in range(RING):
                room(PRE + c)
                if c == 4:
                    sp.wait_ge(sem("wo_dec_full"), 64)
                expert_chunk(c, 0)
            sp.wait_ge(sem("cat_ready"), 3)
            sp.wait_ge(sem("stored"), 16 * N_STORED)
            for c in range(RING, RING2):
                expert_chunk(c, 0)
            sp.wait_ge(sem("npass_ready"), 1)
            sp.wait_ge(sem("bias_cleared"), 2)
            passes = sp.value_load(npass[0:1, 0:1], min_val=1, max_val=MAXPASS)
            total = sp.snap(passes * PAIRS)
            with sp.Fori(0, total) as it:
                for c in range(RING2, PER):
                    sp.wait_ge(chunks_used, it * PER + (PRE + c - RING2 + 1))
                    expert_chunk(c, it % PAIRS)
                with sp.If(it < total - 1):
                    for c in range(RING2):
                        sp.wait_ge(chunks_used, it * PER + (PRE + PER + c - RING2 + 1))
                        expert_chunk(c, (it + 1) % PAIRS)
            for t in range(3):
                sp.wait_ge(sem("result"), t + 1)
                dst = O["yp"][0, P * t:P * t + P] if t < 2 else O["ys"].rearrange("b s d -> (b s) d")
                sp.dma_start(dst, x[0:NT[t], t, :]).then_inc(sem("result_stored"), 16)
            sp.wait_ge(sem("result_stored"), 48)

        @block.gpsimd
        def _(pool):
            pool.wait_ge(sem("cleared"), 1)
            for q in range(3):
                for j in range(4):
                    n0 = q * CH + j * 512
                    pool.dma_start(ba[32 * j:32 * j + 9, q, :],
                                   wide(A["b_ada"][0:1, n0:n0 + 512], 0, 9)).then_inc(sem("ada_rows_full"), 16)
            for j in range(2):
                pool.dma_start(gb[64 + 32 * j:64 + 32 * j + 9, 0, :],
                               wide(A["g_mix"][0:1, j * 512:(j + 1) * 512], 0, 9)).then_inc(sem("ada_rows_full"), 16)
                pool.dma_start(gb[32 * j:32 * j + 9, 1, :],
                               wide(A["g_ffn"][0:1, j * 512:(j + 1) * 512], 0, 9)).then_inc(sem("ada_rows_full"), 16)
            pool.dma_start(lbl[:, 0, :], wide(A["hg_lb_logits"][0:1, :], 0, P)).then_inc(sem("rows_full"), 16)
            pool.dma_start(lbl[:, 1, :], wide(A["hg_lb_logits"][1:2, :], 0, P)).then_inc(sem("rows_full"), 16)
            pool.dma_start(g_att, wide(A["g_attn_out"][0:1, :], 0, P)).then_inc(sem("rows_full"), 16)
            pool.dma_start(g_hg, wide(A["g_hg_out"].rearrange("a h v -> a (h v)"), 0, P)).then_inc(sem("rows_full"), 16)
            pool.dma_start(sinkb, wide(A["attn_sinks"][0:1, :], 0, P)).then_inc(sem("rows_full"), 16)
            for b in range(NB):
                pool.dma_start(sink64[HEADS * b:HEADS * (b + 1), :],
                               A["attn_sinks"].rearrange("a h -> h a")).then_inc(sem("rows_full"), 16)
            pool.dma_start(brout[0:E, :], A["b_router"].rearrange("a e -> e a")).then_inc(sem("rows_full"), 16)
            for src, dst in (("cache_k_win", "kws"), ("cache_v_win", "vws")):
                pool.dma_start(O[dst][0, :, 0:WIN - 1].rearrange("b s g d -> b (s g d)"),
                               A[src][0, :, 1:WIN].rearrange("b s g d -> b (s g d)")).then_inc(sem("stored"), 16)
            pool.dma_start(list_dram.rearrange("(p n) a -> p (n a)", p=P), zeros[:, :]).then_inc(sem("list_cleared"), 16)
            pool.wait_ge(sem("z_dec_copied"), NZ)
            for j in range(4):
                pool.dma_start(zs[0:NB, P * j:P * (j + 1)], zq[32 * j:32 * j + NB, 0:KV, :]).then_inc(sem("zs_full"), 16)
                pool.dma_start(zs[0:NB, :].rearrange("p (c j n) -> p c j n", c=NZ, j=4)[:, KV:, j, :],
                               zq[32 * j:32 * j + NB, KV:, :]).then_inc(sem("zs_full"), 16)
            pool.wait_ge(sem("rotated"), 1)
            pool.dma_start(O["kwp"][0, 0].rearrange("s g d -> s (g d)"), z[:, 1, K0:K0 + P]).then_inc(sem("stored"), 16)
            pool.dma_start(O["vwp"][0, 0].rearrange("s g d -> s (g d)"), z[:, 1, V0:V0 + P]).then_inc(sem("stored"), 16)
            pool.wait_ge(sem("rotated"), 2)
            pool.dma_start(O["kws"][0, :, WIN - 1].rearrange("b g d -> b (g d)"), zs[0:NB, K0:K0 + P]).then_inc(sem("stored"), 16)
            pool.dma_start(O["vws"][0, :, WIN - 1].rearrange("b g d -> b (g d)"), zs[0:NB, V0:V0 + P]).then_inc(sem("stored"), 16)
            pool.wait_ge(sem("att_summed"), 2)
            for b in range(NB):
                pool.dma_start(states[:, b], A["state_hgrn"][0, b].rearrange("h k v -> k h v")).then_inc(sem("states_full"), 16)
            pool.wait_ge(sem("mod_ready"), 3)
            pool.dma_start(kc, A["cache_k_win"][0].rearrange("b s g d -> s b (g d)")).then_inc(sem("cache_full"), 16)
            pool.dma_start(vc, A["cache_v_win"][0].rearrange("b s g d -> s b (g d)")).then_inc(sem("cache_full"), 16)
            pool.wait_ge(sem("stored"), 16 * 6)
            pool.wait_ge(sem("mod_stored"), 64)
            pool.wait_ge(sem("cat_ready"), 2)
            pool.dma_start(rows1, wide(mod_dram[0, 0:1, :], 0, P)).then_inc(sem("mod_rows_full"), 16)
            pool.dma_start(scale2, wide(mod_dram[1, 0:1, 0:D], 0, P)).then_inc(sem("mod_rows_full"), 16)
            pool.dma_start(wr, A["w_router"][0].rearrange("(k p) e -> p k e", p=P)).then_inc(sem("router_full"), 16)
            pool.wait_ge(sem("state_final"), HH)
            pool.dma_start(O["hgp"][0, 0].rearrange("h k v -> k h v"), st.rearrange("p (h v) -> p h v", h=HH)).then_inc(sem("stored"), 16)
            pool.wait_ge(sem("states_new"), NB * HH)
            for b in range(NB):
                pool.dma_start(O["hgs"][0, b].rearrange("h k v -> k h v"), states[:, b]).then_inc(sem("stored"), 16)
            pool.wait_ge(sem("cat_ready"), 3)
            pool.wait_ge(sem("stored"), 16 * N_STORED)
            pool.dma_start(rows1s[0:NB, :], mod_dram[0, 1:1 + NB, :]).then_inc(sem("mod_rows_s_full"), 16)
            pool.dma_start(rows2s[0:NB, :], mod_dram[1, 1:1 + NB, :]).then_inc(sem("mod_rows_s_full"), 16)
            pool.dma_start(gate2, wide(mod_dram[1, 0:1, D:2 * D], 0, P)).then_inc(sem("mod_rows_s_full"), 16)
            pool.wait_ge(sem("stored"), 16 * N_STORED)
            pool.dma_start(g_fin, wide(A["g_final"].rearrange("(a n) -> a n", a=1), 0, P)).then_inc(sem("gfin_full"), 16)
            pool.wait_ge(sem("list_cleared"), 16)
            pool.wait_ge(sem("slots_ready"), 1)
            for t in range(3):
                for k in range(TOPK):
                    pool.indirect_dma_start(
                        out=list_dram, out_offset=bass.IndirectOffsetOnAxis(ap=slot_u[0:NT[t], t, k:k + 1], axis=0),
                        in_=tok_i[0:NT[t], t:t + 1], in_offset=None).then_inc(sem("list_full"), 16)
            pool.wait_ge(sem("list_full"), 16 * 3 * TOPK)
            pool.wait_ge(sem("npass_ready"), 1)
            passes = pool.value_load(npass[0:1, 0:1], min_val=1, max_val=MAXPASS)
            pool.wait_ge(sem("slots_ready"), 2)
            pool.wait_ge(sem("h2_stored"), 48)
            pool.wait_ge(sem("bias_cleared"), 2)
            with pool.Fori(0, passes) as p:
                with pool.Fori(0, PAIRS) as i:
                    it = pool.snap(p * PAIRS + i)
                    pool.wait_ge(sem("xT_made"), it * 2 + 1)
                    pool.dma_start(idx[:, :], list_dram[bass.ds(it * P, P), :]).then_inc(sem("idx_full"), 16)
                    pool.wait_ge(sem("idx_full"), it * 16 + 16)
                    pool.nop(nofuse=True)
                    pool.indirect_dma_start(
                        out=xg, out_offset=None, in_=h2_dram,
                        in_offset=bass.IndirectOffsetOnAxis(ap=idx[:, 0:1].bitcast(U32), axis=0)).then_inc(sem("x_full"), 16)
                    row = pool.snap(i * 2)
                    for e in range(2):
                        pool.wait_ge(sem(f"bias_used{e}"), it + 1)
                        pool.dma_start(bias[e][0:1, 0:FF2],
                                       A["b_up"][0][bass.ds(row + e, 1), :]).then_inc(sem(f"bias_full{e}"), 16)
                        pool.dma_start(bias[e][0:1, FF2:FF2 + D],
                                       A["b_down"][0][bass.ds(row + e, 1), :]).then_inc(sem(f"bias_full{e}"), 16)
                for e in range(2):
                    pool.wait_ge(sem(f"y_stored{e}"), (p + 1) * (32 * PAIRS) + 1)
                with pool.If(p < passes - 1):
                    for n in range(3 * TOPK):
                        t, k = divmod(n, TOPK)
                        pool.wait_ge(sem("y_added"), p * (3 * TOPK) + n + 1)
                        pool.nop(nofuse=True)
                        pool.indirect_dma_start(
                            out=xg[0:NT[t], :], out_offset=None, in_=y_dram,
                            in_offset=bass.IndirectOffsetOnAxis(ap=row_u[0:NT[t], t, k:k + 1], axis=0)).then_inc(sem("y_part"), 16)
                    pool.wait_ge(sem("y_added"), (p + 1) * (3 * TOPK) + 1)
            total = pool.snap(passes * PAIRS)
            pool.wait_ge(chunks_used, total * PER + PRE)
            pool.nop(nofuse=True)
            for t in range(3):
                for k in range(TOPK):
                    pool.indirect_dma_start(
                        out=yk[t][k][0:NT[t], :], out_offset=None, in_=y_dram,
                        in_offset=bass.IndirectOffsetOnAxis(ap=row_u[0:NT[t], t, k:k + 1], axis=0)).then_inc(y_full(t, k), 16)

        @block.scalar
        def _(act):
            act.dma_start(crow[0:1, :], A["c_prompt"]).then_inc(sem("c_full"), 16)
            act.dma_start(crow[1:9, :], A["c_sample"]).then_inc(sem("c_full"), 16)
            act.dma_start(const[:, :], A["const"]).then_inc(sem("const_full"), 16)
            act.dma_start(x[:, 0, :], A["x_prompt"][0, 0:P]).then_inc(sem("x_full_in"), 16)
            act.dma_start(x[:, 1, :], A["x_prompt"][0, P:S]).then_inc(sem("x_full_in"), 16)
            act.dma_start(x[0:NB, 2, :], A["x_sample"].rearrange("b s d -> (b s) d")).then_inc(sem("x_full_in"), 16)
            act.wait_ge(sem("c_full"), 32)
            act.activation(crow[0:9, :], crow[0:9, :], ACT.Silu).then_inc(sem("c_silu"), 1)

            def squares(t):
                act.activation(h[0:NT[t], t, :], x[0:NT[t], t, :], ACT.Square,
                               accum_out=ssum3[0:NT[t], t:t + 1]).then_inc(sem("sums"), 1)

            def root(t):
                act.activation(root3[0:NT[t], t:t + 1], ssum3[0:NT[t], t:t + 1], ACT.Sqrt).then_inc(sem("roots"), 1)

            def store_h2(t):
                act.wait_ge(sem("h2_ready"), t + 1)
                act.dma_start(h2_dram[P * t:P * t + NT[t], :], h[0:NT[t], t, :]).then_inc(sem("h2_stored"), 16)

            act.wait_ge(sem("x_full_in"), 48)
            for t in range(3):
                squares(t)
            act.wait_ge(sem("means"), 3)
            for t in range(3):
                root(t)

            def even_tiles(made, copied):
                for k in range(0, KT, 2):
                    act.wait_ge(sem(made), k + 1)
                    act.activation(hT[:, k, 0:NTOK], B[k][:, 0:NTOK], ACT.Copy).then_inc(sem(copied), 1)

            act.wait_ge(sem("mod_ready"), 1)
            for j in range(4):
                act.dma_start(rows0s[0:NB, 512 * j:512 * (j + 1)], mods[32 * j + 1:32 * j + 1 + NB, 0, :]).then_inc(sem("mod_rows0_full"), 16)
            even_tiles("hT_made", "hT_copied_a")
            act.wait_ge(sem("lb_less_max"), 2)
            act.activation(lbl[:, :, :], lbl[:, :, :], ACT.Exp).then_inc(sem("lb_exp"), 1)
            for c in range(NZ):
                act.wait_ge(sem("z_made"), c + 1)
                src = B[c % 4][:, :].rearrange("p (t n) -> p t n", t=2)
                if c < KV:
                    for t in range(2):
                        done = act.activation(z[:, t, 0:AW].rearrange("p (j g d) -> p g j d", g=KV, j=GRP)[:, c],
                                              src[:, t, :].rearrange("p (j d) -> p j d", j=GRP), ACT.Copy)
                else:
                    done = act.activation(z[:, :, c * ZC:(c + 1) * ZC], src, ACT.Copy)
                done.then_inc(sem("z_copied"), 1)
            act.wait_ge(sem("z_copied"), NZ)
            act.activation(z[:, :, F0:F0 + HW_], z[:, :, F0:F0 + HW_], ACT.Sigmoid).then_inc(sem("f_sig"), 1)
            act.wait_ge(sem("qk_made"), 3)
            act.activation(qT[:, :, 0:P], B[0][:, :].rearrange("p (j t) -> p j t", j=4), ACT.Copy).then_inc(sem("qk_copied"), 1)
            act.activation(qT[:, :, P:S], B[1][:, :].rearrange("p (j t) -> p j t", j=4), ACT.Copy).then_inc(sem("qk_copied"), 1)
            act.activation(kT, B[2][:, 0:S], ACT.Copy).then_inc(sem("qk_copied"), 1)
            act.wait_ge(sem("zs_full"), 128)
            act.activation(zs[0:NB, F0:F0 + HW_], zs[0:NB, F0:F0 + HW_], ACT.Sigmoid).then_inc(sem("f_sig"), 1)
            act.activation(z[:, :, G0:G0 + HW_], z[:, :, G0:G0 + HW_], ACT.Silu).then_inc(sem("g_silu"), 1)
            act.activation(zs[0:NB, G0:G0 + HW_], zs[0:NB, G0:G0 + HW_], ACT.Silu).then_inc(sem("g_silu"), 1)
            act.wait_ge(sem("f_ready"), 1)
            act.activation(logf, z[:, :, F0:F0 + HW_], ACT.Ln).then_inc(sem("logf_ready"), 1)
            for n, t in enumerate((1, 0)):
                act.wait_ge(sem("max_ready"), n + 1)
                w = P * (t + 1)
                for hd in range(HEADS):
                    act.activation(sc[:, hd * w:(hd + 1) * w], sc[:, hd * w:(hd + 1) * w], ACT.Exp,
                                   bias=nmax[:, t, hd:hd + 1], accum_out=psums[:, t, hd:hd + 1]).then_inc(sem("probs"), 1)
                act.activation(esink[:, t, :], dsink[:, t, :], ACT.Exp).then_inc(sem("esink_ready"), 1)
                for i in range(2 * (t + 1)):
                    act.wait_ge(sem("pT_made"), 4 * n + i + 1)
                    if n and i == 0:
                        act.wait_ge(sem("pv_made"), 1)
                    act.activation(pT[:, 4 * i:4 * i + 4, :], B[3 + i][:, :].rearrange("p (n q) -> p n q", n=4),
                                   ACT.Copy).then_inc(sem("pT_copied"), 1)
            for t in range(2):
                act.wait_ge(sem("hg_made"), 4 * t + 4)
                if t:
                    act.wait_ge(sem("G_made"), 8)
                    act.wait_ge(sem("lev_ready"), 7)
                act.activation(bT, B[0][:, :], ACT.Copy).then_inc(sem("hg_copied"), 1)
                act.activation(kkT, B[1][:, :], ACT.Copy).then_inc(sem("hg_copied"), 1)
                act.activation(qqT, B[2][:, :], ACT.Copy).then_inc(sem("hg_copied"), 1)
                if t:
                    act.wait_ge(sem("st_made"), 1)
                act.activation(ks, B[3][:, :], ACT.Exp).then_inc(sem("tail_exp"), 1)
                for n in range(7):
                    act.wait_ge(sem("lev_diff"), 14 * t + 2 * n + 2)
                    act.activation(lev[n % 2], lev[n % 2], ACT.Exp).then_inc(sem("lev_exp"), 1)
                if t:
                    act.wait_ge(sem("G_made"), 16)
                    act.wait_ge(sem("hg_copied"), 6)
                    act.activation(lev[0], bT, ACT.Exp).then_inc(sem("b_exp"), 1)
                    act.activation(eb, bT.rearrange("p (h t) -> p h t", h=HH)[:, :, P - 1], ACT.Exp).then_inc(sem("b_exp"), 1)
            act.wait_ge(sem("mod_ready"), 3)
            for j in range(4):
                act.dma_start(mod_dram[:, :, 512 * j:512 * (j + 1)].rearrange("q r n -> r q n"),
                              mods[32 * j:32 * j + 1 + NB, 1:3, :]).then_inc(sem("mod_stored"), 16)
            act.wait_ge(sem("gmeans"), 1)
            act.activation(groot[:, 0:10], gmean[:, 0:10], ACT.Sqrt).then_inc(sem("groots"), 1)
            act.wait_ge(sem("smax_ready"), 1)
            act.activation(ps[0:64, :], ps[0:64, :], ACT.Exp, bias=snm[0:64, :], accum_out=ssm[0:64, :]).then_inc(sem("sprobs"), 1)
            act.activation(sesk[0:64, :], snm[0:64, :], ACT.Exp, bias=sink64[0:64, :]).then_inc(sem("sprobs"), 1)
            for i in (0, 2):
                act.wait_ge(sem("catT_made"), i + 1)
                act.activation(hT[:, 2 * i:2 * i + 2, 0:S], B[4 + i][:, :].rearrange("p (k t) -> p k t", k=2),
                               ACT.Copy).then_inc(sem("catT_copied_a"), 1)
            act.wait_ge(sem("spv_made"), 2)
            act.activation(pv[0:64, :], B[4][0:64, 0:P], ACT.Copy).then_inc(sem("pv_copied"), 1)
            act.wait_ge(sem("o64_ready"), 1)
            act.dma_start(h[0:NB, 2, 0:AW], o64[0:64, :]).then_inc(sem("o64_moved"), 16)
            for t in range(2):
                act.wait_ge(sem("x1_ready"), t + 1)
                squares(t)
            act.wait_ge(sem("means"), 5)
            for t in range(2):
                root(t)
            for t in range(2):
                store_h2(t)
            act.wait_ge(sem("gmeans"), 2)
            act.activation(groot[0:NB, 10:15], gmean[0:NB, 10:15], ACT.Sqrt).then_inc(sem("groots"), 1)
            act.wait_ge(sem("wo_dec_copied"), 1)
            for j in range(4):
                act.dma_start(tmps[0:NB, 256 * j:256 * (j + 1)], zq[32 * j:32 * j + NB, 0:4, :]).then_inc(sem("wo_dec_full"), 16)
            act.wait_ge(sem("x1_ready"), 3)
            squares(2)
            act.wait_ge(sem("means"), 6)
            root(2)
            store_h2(2)
            even_tiles("h2T_made", "h2T_copied_a")
            act.wait_ge(sem("top_ready"), 1)
            for t in range(3):
                act.activation(topw[:, t, :], top8[:, t, 0:TOPK], ACT.Exp, bias=ntop[:, t:t + 1],
                               accum_out=tsum[:, t:t + 1]).then_inc(sem("top_exp"), 1)

            def store(e, it, i):
                act.wait_ge(sem(f"y_stored{e}"), it * 32 + 1)
                act.wait_ge(chunks_used, it * PER + (PRE + 20 + 4 * e))
                act.activation(ysb[e], B[4 + e][:, :], ACT.Copy).then_inc(sem(f"y_copied{e}"), 1)
                act.wait_ge(sem(f"y_copied{e}"), it + 2)
                for a in range(2):
                    act.dma_start(y_dram[bass.ds(i * P + 64 * e, SLOTS), 512 * a:512 * (a + 1)],
                                  ysb[e][64 * a:64 * (a + 1), :]).then_inc(sem(f"y_stored{e}"), 16)

            act.wait_ge(sem("stored"), 16 * N_STORED)
            act.wait_ge(sem("npass_ready"), 1)
            passes = act.value_load(npass[0:1, 0:1], min_val=1, max_val=MAXPASS)
            count_from_one(act, "y_copied0", "y_copied1", "y_stored0", "y_stored1", "gT_copied")
            with act.Fori(0, passes) as p:
                act.wait_ge(sem("y_added"), p * (3 * TOPK) + 1)
                with act.Fori(0, PAIRS) as i:
                    it = act.snap(p * PAIRS + i)
                    act.wait_ge(sem("xT_made"), it * 2 + 3)
                    act.activation(xT[:, 4:8, :], B[7][:, :].rearrange("p (k t) -> p k t", k=4), ACT.Copy).then_inc(sem("xT_copied_a"), 1)
                    for e in range(2):
                        act.wait_ge(sem("glu_ready"), it * 2 + (e + 1))
                        act.activation(sg, glu, ACT.Sigmoid, scale=ALPHA).then_inc(sem("sig_ready"), 1)
                        act.wait_ge(sem("gT_made"), it * 2 + (e + 2))
                        act.activation(gT[e], B[6 + e][:, :], ACT.Copy).then_inc(sem("gT_copied"), 1)
                        if e:
                            store(0, it, i)
                    store(1, it, i)
            for t in range(3):
                act.wait_ge(sem("x2_ready"), t + 1)
                act.activation(moe[0:NT[t], t, :], x[0:NT[t], t, :], ACT.Square,
                               accum_out=ssum3[0:NT[t], t:t + 1]).then_inc(sem("sums"), 1)
                act.wait_ge(sem("means"), 6 + t + 1)
                root(t)

        @block.tensor
        def _(pe):
            def landed(n):
                pe.wait_ge(full[place(n)], 16 * loads(n))

            def turn(out, in_, rows):
                return pe.transpose(out, in_, ident[0:rows, 0:rows])

            def pick_rows(out, j):
                return pe.matmul(out, lhsT=C("pick", slice(32 * j, 32 * j + 32)), rhs=mods[32 * j:32 * j + 32, 0, :],
                                 start=True, stop=True)

            def transpose_tiles(src, made):
                for k in range(KT):
                    for t in range(3):
                        mm = turn(B[k][:, P * t:P * t + NT[t]], src[0:NT[t], t, P * k:P * (k + 1)], NT[t])
                    mm.then_inc(sem(made), 1)

            def modulation(first, k, bank):
                landed(first + k)
                for j in range(4):
                    mm = pe.matmul(bank[32 * j:32 * j + 32, :], lhsT=scT[:, k, :], rhs=chunk(first + k)[:, 512 * j:512 * (j + 1)],
                                   start=(k == 0), stop=(k == N_ADA - 1), skip_group_check=True)
                mm.then_inc(chunks_used, 1)

            pe.wait_ge(sem("const_full"), 16)
            pe.wait_ge(sem("c_silu"), 1)
            for k in range(KT):
                mm = turn(B[0][:, 16 * k:16 * k + 9], crow[0:9, P * k:P * (k + 1)], 9)
            mm.then_inc(sem("cT_made"), 1)
            pe.wait_ge(sem("scT_ready"), 1)
            for k in range(N_ADA):
                modulation(0, k, B[1])
            pe.wait_ge(sem("mod_ready"), 1)
            for n in range(2):
                pick_rows(B[2 + n][:, :], 2 + n)
                mm = pick_rows(B[4 + n][:, :], n)
            mm.then_inc(sem("bc1_made"), 1)
            pe.wait_ge(sem("h_ready"), 3)
            transpose_tiles(h, "hT_made")
            pe.wait_ge(sem("hT_copied_a"), 4)
            pe.wait_ge(sem("hT_copied_d"), 4)
            for c in range(NZ):
                n = Z0 + c
                w = chunk(n).rearrange("p (k n) -> p k n", k=KT)
                landed(n)
                if c >= 4:
                    pe.wait_ge(sem("z_copied"), c - 3)
                for t in range(2):
                    for k in range(KT):
                        mm = pe.matmul(B[c % 4][:, ZC * t:ZC * (t + 1)], lhsT=hT[:, k, P * t:P * (t + 1)], rhs=w[:, k, :],
                                       start=(k == 0), stop=(k == KT - 1))
                mm.then_inc(sem("z_made"), 1)
                if c >= 2:
                    pe.wait_ge(sem("z_dec_copied"), c - 1)
                for k in range(KT):
                    for j in range(4):
                        mm = pe.matmul(B[4 + c % 2][32 * j:32 * j + 32, 0:64], lhsT=hT[:, k, S:S + 32], rhs=w[:, k, 64 * j:64 * (j + 1)],
                                       start=(k == 0), stop=(k == KT - 1), skip_group_check=True)
                mm.then_inc(chunks_used, 1)
            pe.wait_ge(sem("z_copied"), NZ)
            pe.wait_ge(sem("rotated"), 1)
            for t in range(2):
                for j in range(GRP):
                    mm = turn(B[t][:, P * j:P * (j + 1)], z[:, t, P * j:P * (j + 1)], P)
                mm.then_inc(sem("qk_made"), 1)
            for t in range(2):
                mm = turn(B[2][:, P * t:P * (t + 1)], z[:, t, K0:K0 + P], P)
            mm.then_inc(sem("qk_made"), 1)
            pe.wait_ge(sem("qk_copied"), 3)
            pe.wait_ge(sem("z_dec_copied"), NZ)
            for jj in range(2):
                for g in range(KV):
                    for j in (2 * jj, 2 * jj + 1):
                        mm = pe.matmul(B[3 + 2 * g + jj][:, 256 * (j % 2):256 * (j % 2 + 1)],
                                       lhsT=qT[64 * g:64 * g + 64, j, P:S], rhs=kT[64 * g:64 * g + 64, :], start=True, stop=True)
                    mm.then_inc(sem("sc_made"), 1)
            for g in range(KV):
                for j in range(GRP):
                    mm = pe.matmul(B[(7 + g) % 8][:, P * j:P * (j + 1)],
                                   lhsT=qT[64 * g:64 * g + 64, j, 0:P], rhs=kT[64 * g:64 * g + 64, 0:P], start=True, stop=True)
                mm.then_inc(sem("sc_made"), 1)
            for n, t in enumerate((1, 0)):
                nb = t + 1
                for i in range(2 * nb):
                    per = 4 // nb
                    pe.wait_ge(sem("probs"), 8 * n + per * (i + 1))
                    if n:
                        pe.wait_ge(sem("pT_copied"), i + 1)
                    for u in range(4):
                        m = 4 * i + u
                        mm = turn(B[3 + i][:, P * u:P * (u + 1)], sc[:, P * m:P * (m + 1)], P)
                    mm.then_inc(sem("pT_made"), 1)
                pe.wait_ge(sem("pT_copied"), 4 * n + 2 * nb)
                for hd in range(HEADS):
                    g = hd // GRP
                    for s in range(nb):
                        mm = pe.matmul(B[1 + n][:, HD * hd:HD * (hd + 1)], lhsT=pT[:, nb * hd + s, :],
                                       rhs=z[:, s, V0 + HD * g:V0 + HD * (g + 1)], start=(s == 0), stop=(s == nb - 1))
                mm.then_inc(sem("pv_made"), 1)
            pe.wait_ge(sem("k_ready"), 1)
            for t in range(2):
                if t == 0:
                    pe.wait_ge(sem("att_summed"), 2)
                    pe.wait_ge(sem("masked"), 6)
                else:
                    pe.wait_ge(sem("hg_copied"), 3)
                    pe.wait_ge(sem("st_copied"), 1)
                for hd in range(HH):
                    c = slice(P * hd, P * (hd + 1))
                    mm = pe.matmul(B[0][:, c], lhsT=logf[:, t, c], rhs=C("incl"), start=True, stop=True)
                mm.then_inc(sem("hg_made"), 1)
                for hd in range(HH):
                    mm = turn(B[1][:, P * hd:P * (hd + 1)], z[:, t, F0 + P * hd:F0 + P * (hd + 1)], P)
                mm.then_inc(sem("hg_made"), 1)
                for hd in range(HH):
                    mm = turn(B[2][:, P * hd:P * (hd + 1)], z[:, t, Q0 + P * hd:Q0 + P * (hd + 1)], P)
                mm.then_inc(sem("hg_made"), 1)
                pe.matmul(B[3][:, :], lhsT=C("after"), rhs=logf[:, t, :], start=True, stop=True).then_inc(sem("hg_made"), 1)
                pe.wait_ge(sem("hg_copied"), 3 * t + 3)
                for n in range(8):
                    g = 8 * t + n
                    if n:
                        pe.wait_ge(sem("lev_ready"), 7 * t + n)
                    if g >= 2:
                        pe.wait_ge(sem("lev_masked"), g - 1)
                    for hd in range(HH):
                        c = slice(P * hd, P * (hd + 1))
                        left = kkT if n == 0 else lev[(n - 1) % 2]
                        right = qqT if n == 0 else lev[(n - 1) % 2]
                        mm = pe.matmul(B[4 + n % 2][:, c], lhsT=left[:, c], rhs=right[:, c], start=True, stop=True)
                    mm.then_inc(sem("G_made"), 1)
                    modulation((ADA1, ADA2)[t], n, B[(7, 2)[t]])
                pe.wait_ge(sem("ks_ready"), t + 1)
                for hd in range(HH):
                    c = slice(P * hd, P * (hd + 1))
                    mm = pe.matmul(B[3][:, c], lhsT=ks[:, c], rhs=z[:, t, I0 + P * hd:I0 + P * (hd + 1)], start=True, stop=True)
                mm.then_inc(sem("st_made"), 1)
                pe.wait_ge(sem("lev_masked"), 8 * t + 8)
                if t:
                    pe.wait_ge(sem("qb_ready"), 1)
                    pe.wait_ge(sem("mod_ready"), 2)
                for hd in range(HH):
                    c = slice(P * hd, P * (hd + 1))
                    mm = pe.matmul(B[6 + t][:, c], lhsT=amat[:, hd, :], rhs=z[:, t, I0 + P * hd:I0 + P * (hd + 1)],
                                   start=True, stop=(t == 0))
                    if t:
                        mm = pe.matmul(B[6 + t][:, c], lhsT=lev[0][:, c], rhs=st[:, c], start=False, stop=True)
                mm.then_inc(sem("hgo_made"), 1)
            pe.wait_ge(sem("cache_full"), 32)
            pe.wait_ge(sem("hg_copied"), 6)
            for b in range(NB):
                mm = turn(B[b // 4][:, P * (b % 4):P * (b % 4 + 1)], kc[:, b, :], P)
                if b % 4 == 3:
                    mm.then_inc(sem("kcT_made"), 1)
            pe.wait_ge(sem("rotated"), 2)
            pe.wait_ge(sem("mod_ready"), 3)
            turn(B[2][:, 0:NB], zs[0:NB, K0:K0 + P], NB)
            for j in range(GRP):
                mm = turn(B[2][:, 16 + 8 * j:24 + 8 * j], zs[0:NB, P * j:P * (j + 1)], NB)
            mm.then_inc(sem("snew_made"), 1)
            pe.wait_ge(sem("kcT_copied"), 2)
            pe.wait_ge(sem("snew_copied"), 3)
            pe.wait_ge(sem("state_final"), HH)
            for b in range(NB):
                mm = pe.matmul(B[3][0:64, 0:129], lhsT=qbd[:, 64 * b:64 * b + 64], rhs=kcT[:, b, :], start=(b == 0), stop=(b == NB - 1))
            mm.then_inc(sem("ss_made"), 1)
            pe.wait_ge(sem("k_ready"), 2)
            for hd in range(HH):
                turn(B[0][:, NB * hd:NB * (hd + 1)], zs[0:NB, Q0 + P * hd:Q0 + P * (hd + 1)], NB)
                mm = turn(B[0][:, 32 + NB * hd:32 + NB * (hd + 1)], zs[0:NB, F0 + P * hd:F0 + P * (hd + 1)], NB)
            mm.then_inc(sem("sqf_made"), 1)
            pe.wait_ge(sem("cat_ready"), 2)
            for k in range(KT):
                for t in range(2):
                    mm = turn(B[4 + k // 2][:, S * (k % 2) + P * t:S * (k % 2) + P * (t + 1)], h[:, t, P * k:P * (k + 1)], P)
                if k % 2:
                    mm.then_inc(sem("catT_made"), 1)

            def project_prompt(k):
                landed(WO0 + k // 2)
                for t in range(2):
                    for a in range(2):
                        mm = pe.matmul(B[2 * t + a][:, :], lhsT=hT[:, k, P * t:P * (t + 1)],
                                       rhs=two(chunk(WO0 + k // 2))[:, k % 2, 512 * a:512 * (a + 1)],
                                       start=(k == 0), stop=(k == KT - 1))
                return mm

            pe.wait_ge(sem("catT_copied_a"), 2)
            pe.wait_ge(sem("catT_copied_d"), 2)
            pe.wait_ge(sem("smax_ready"), 1)
            pe.wait_ge(sem("km_ready"), 1)
            project_prompt(0)
            pe.wait_ge(sem("sprobs"), 1)
            turn(B[5][:, 0:64], ps[0:64, 0:P], 64).then_inc(sem("spT_made"), 1)
            project_prompt(1)
            pe.wait_ge(sem("pbd_ready"), 1)
            for b in range(NB):
                mm = pe.matmul(B[4][0:64, 0:P], lhsT=pbd[:, 64 * b:64 * b + 64], rhs=vc[:, b, :], start=(b == 0), stop=(b == NB - 1))
            mm.then_inc(sem("spv_made"), 1)
            pe.matmul(B[5][0:64, 0:P], lhsT=C("spread", slice(0, NB)), rhs=zs[0:NB, V0:V0 + P], start=True, stop=True).then_inc(sem("spv_made"), 1)
            for b in range(NB):
                if b % 2 == 0:
                    project_prompt(2 + b // 2)
                pe.wait_ge(sem("km_ready"), b + 1)
                if b >= 2:
                    pe.wait_ge(sem("states_new"), HH * (b - 1))
                for hd in range(HH):
                    c = slice(P * hd, P * (hd + 1))
                    mm = pe.matmul(B[6 + b % 2][:, c], lhsT=km[b % 2][0:NB, c], rhs=zs[0:NB, I0 + P * hd:I0 + P * (hd + 1)], start=True, stop=True)
                mm.then_inc(sem("outer_made"), 1)
            project_prompt(6)
            project_prompt(7).then_inc(sem("wo_made"), 1)
            pe.wait_ge(sem("states_new"), HH * NB)
            pe.wait_ge(sem("pv_copied"), 1)
            for b in range(NB):
                for hd in range(HH):
                    col = NB * hd + b
                    mm = pe.matmul(B[4][:, col:col + 1], lhsT=states[:, b, hd, :], rhs=sq[:, col:col + 1], start=True, stop=True)
            mm.then_inc(sem("soT_made"), 1)
            pe.wait_ge(sem("soT_copied"), 1)
            for hd in range(HH):
                mm = turn(B[6][0:NB, P * hd:P * (hd + 1)], soT[:, NB * hd:NB * (hd + 1)], P)
            mm.then_inc(sem("so_made"), 1)
            pe.wait_ge(sem("cat_ready"), 3)
            for k in range(KT):
                mm = turn(B[7][:, NB * k:NB * (k + 1)], h[0:NB, 2, P * k:P * (k + 1)], NB)
            mm.then_inc(sem("catT_made"), 1)
            pe.wait_ge(sem("catT_copied_d"), 3)
            for k in range(KT):
                n = WO0 + k // 2
                for j in range(4):
                    mm = pe.matmul(B[5][32 * j:32 * j + 32, 0:256], lhsT=hT[:, k, S:S + 32],
                                   rhs=two(chunk(n))[:, k % 2, 256 * j:256 * (j + 1)],
                                   start=(k == 0), stop=(k == KT - 1), skip_group_check=True)
                if k % 2:
                    mm.then_inc(chunks_used, 1)
            pe.wait_ge(sem("h2_ready"), 3)
            transpose_tiles(h, "h2T_made")
            pe.wait_ge(sem("h2T_copied_a"), 4)
            pe.wait_ge(sem("h2T_copied_d"), 4)
            pe.wait_ge(sem("router_full"), 16)
            for k in range(KT):
                mm = pe.matmul(B[0][0:E, 0:NTOK], lhsT=wr[:, k, :], rhs=hT[:, k, 0:NTOK], start=(k == 0), stop=(k == KT - 1))
            mm.then_inc(sem("lgT_made"), 1)
            pe.wait_ge(sem("lgT_ready"), 1)
            for t in range(3):
                mm = turn(B[1][0:NT[t], E * t:E * (t + 1)], lgT[0:E, P * t:P * t + NT[t]], E)
            mm.then_inc(sem("lg_made"), 1)
            pe.wait_ge(sem("chosen_ready"), 1)
            for t in range(3):
                for u in range(t + 1):
                    pe.matmul(B[2][:, E * t:E * (t + 1)], lhsT=C("before" if u == t else "ones", slice(0, NT[u])),
                              rhs=chosen[0:NT[u], u, :], start=(u == 0), stop=(u == t))
            for u in range(3):
                mm = pe.matmul(B[3][0:1, 0:E], lhsT=C("ones", slice(0, NT[u]))[:, 0:1], rhs=chosen[0:NT[u], u, :], start=(u == 0), stop=(u == 2))
            mm.then_inc(sem("rank_made"), 1)

            pe.wait_ge(sem("npass_ready"), 1)
            pe.wait_ge(sem("bias_cleared"), 2)
            passes = pe.value_load(npass[0:1, 0:1], min_val=1, max_val=MAXPASS)
            total = pe.snap(passes * PAIRS)
            one = C("bias_row")
            count_from_one(pe, "xT_made", "gT_made", "bias_used0", "bias_used1")
            with pe.Fori(0, total) as it:
                def chunk_landed(n):
                    pe.wait_ge(full[place(n)], it * (16 * PER // RING2) + 16 * loads(n))

                def turn_g(e):
                    pe.wait_ge(sem("g_ready"), it * 2 + (e + 2))
                    for j in range(4):
                        mm = turn(B[6 + e][:, P * j:P * (j + 1)], gg[e][:, P * j:P * (j + 1)], P)
                    mm.then_inc(sem("gT_made"), 1)

                pe.wait_ge(sem("x_full"), it * 16 + 16)
                pe.wait_ge(sem("gT_copied"), it * 2 + 1)
                for k in range(KT):
                    mm = turn(B[6 + k // 4][:, P * (k % 4):P * (k % 4 + 1)], xg[:, P * k:P * (k + 1)], P)
                    if k % 4 == 3:
                        mm.then_inc(sem("xT_made"), 1)
                for e in range(2):
                    pe.wait_ge(sem(f"bias_full{e}"), it * 32 + 32)
                    pe.wait_ge(sem("u_read"), it * 2 + 1)
                    for c in range(4):
                        a = c // 2
                        pe.matmul(B[2 * e + c % 2][64 * a:64 * a + 64, :], lhsT=one, rhs=bias[e][:, 512 * c:512 * (c + 1)],
                                  start=True, stop=False, skip_group_check=True)
                    if e == 0:
                        pe.wait_ge(sem("xT_copied_d"), it + 1)
                        pe.wait_ge(sem("xT_copied_a"), it + 1)
                    for k in range(KT):
                        if e and k == 4:
                            turn_g(0)
                        n = PRE + 8 * e + k
                        chunk_landed(n)
                        for c in (0, 2, 1, 3):
                            a = c // 2
                            mm = pe.matmul(B[2 * e + c % 2][64 * a:64 * a + 64, :], lhsT=xT[:, k, 64 * e:64 * e + 64],
                                           rhs=chunk(n)[:, 512 * c:512 * (c + 1)], start=False, stop=(k == KT - 1),
                                           skip_group_check=True)
                        mm.then_inc(chunks_used, 1)
                for e in range(2):
                    pe.wait_ge(sem(f"y_copied{e}"), it + 1)
                    for a in range(2):
                        pe.matmul(B[4 + e][64 * a:64 * a + 64, :], lhsT=one,
                                  rhs=bias[e][:, FF2 + 512 * a:FF2 + 512 * (a + 1)],
                                  start=True, stop=False, skip_group_check=True)
                    pe.wait_ge(sem("gT_copied"), it * 2 + (e + 2))
                    for k in range(KT):
                        n = PRE + 16 + 4 * e + k // 2
                        if k % 2 == 0:
                            chunk_landed(n)
                        if e == 0 and k == 4:
                            turn_g(1)
                        for a in range(2):
                            mm = pe.matmul(B[4 + e][64 * a:64 * a + 64, :],
                                           lhsT=gT[e].rearrange("p (j a t) -> p j a t", j=4, a=2)[:, k % 4, k // 4, :],
                                           rhs=two(chunk(n))[:, k % 2, 512 * a:512 * (a + 1)],
                                           start=False, stop=(k == KT - 1), skip_group_check=True)
                            if k == KT - 1 and a == 0:
                                mm.then_inc(sem(f"bias_used{e}"), 1)
                        if k % 2:
                            mm.then_inc(chunks_used, 1)

        @block.vector
        def _(dve):
            steps = [0]

            def link(ins):
                steps[0] += 1
                ins.then_inc(sem("dve_step"), 1)
                dve.wait_ge(sem("dve_step"), steps[0])

            dve.memset(scT[:, :, :], 0.0)
            dve.memset(hT[:, :, NTOK:288], 0.0)
            dve.memset(zeros[:, :], 0)
            dve.memset(ba[:, :, :], 0.0)
            dve.memset(gb[:, :, :], 0.0).then_inc(sem("cleared"), 1)
            dve.wait_ge(sem("cleared"), 1)

            def means(t, m):
                dve.wait_ge(sem("sums"), 3 * m + t + 1)
                dve.tensor_scalar(ssum3[0:NT[t], t:t + 1], ssum3[0:NT[t], t:t + 1], 1.0 / D, EPS, ALU.mult, ALU.add).then_inc(sem("means"), 1)

            def scaled(t, m, out):
                n = NT[t]
                dve.wait_ge(sem("roots"), 3 * m + t + 1)
                link(dve.reciprocal(root3[0:n, t:t + 1], root3[0:n, t:t + 1]))
                link(dve.tensor_scalar(out, x[0:n, t, :], root3[0:n, t:t + 1], None, ALU.mult))

            dve.wait_ge(sem("cT_made"), 1)
            dve.tensor_copy(scT[:, :, 0:9], B[0][:, 0:P].rearrange("p (k t) -> p k t", k=KT)[:, :, 0:9]).then_inc(sem("scT_ready"), 1)
            for t in range(3):
                means(t, 0)
            for t in range(3):
                scaled(t, 0, h[0:NT[t], t, :])

            def modulation(q, used, bank, fold):
                dve.wait_ge(sem("ada_rows_full"), 16 * 16)
                dve.wait_ge(chunks_used, used)
                done = dve.tensor_tensor(mods[:, q, :], bank[:, :], ba[:, q, :], ALU.add)
                if fold is None:
                    done.then_inc(sem("mod_ready"), 1)
                    return
                link(done)
                rows, g = fold
                dve.scalar_tensor_tensor(out=mods[rows, q, :], in0=mods[rows, q, :], scalar=1.0, in1=gb[rows, g, :],
                                         op0=ALU.add, op1=ALU.mult).then_inc(sem("mod_ready"), 1)

            modulation(0, N_ADA, B[1], (slice(64, 128), 0))

            def modulated():
                dve.wait_ge(sem("bc1_made"), 1)
                for t in range(2):
                    for a in range(2):
                        c = slice(512 * a, 512 * (a + 1))
                        link(dve.tensor_tensor(h[:, t, c], h[:, t, c], B[2 + a][:, :], ALU.mult))
                        done = dve.tensor_tensor(h[:, t, c], h[:, t, c], B[4 + a][:, :], ALU.add)
                    done.then_inc(sem("h_ready"), 1)
                dve.wait_ge(sem("mod_rows0_full"), 64)
                link(dve.tensor_tensor(h[0:NB, 2, :], h[0:NB, 2, :], rows0s[0:NB, D:2 * D], ALU.mult))
                dve.tensor_tensor(h[0:NB, 2, :], h[0:NB, 2, :], rows0s[0:NB, 0:D], ALU.add).then_inc(sem("h_ready"), 1)

            def odd_tiles(made, copied):
                for k in range(1, KT, 2):
                    dve.wait_ge(sem(made), k + 1)
                    dve.tensor_copy(hT[:, k, 0:NTOK], B[k][:, 0:NTOK]).then_inc(sem(copied), 1)

            modulated()
            odd_tiles("hT_made", "hT_copied_d")
            dve.wait_ge(sem("rows_full"), 16 * 14)
            link(dve.tensor_tensor(lb, lbl[:, 0, :], lbl[:, 1, :], ALU.max))
            for r in range(2):
                dve.tensor_tensor(lbl[:, r, :], lbl[:, r, :], lb, ALU.subtract).then_inc(sem("lb_less_max"), 1)

            for c in range(NZ):
                if c == 3:
                    dve.wait_ge(sem("lb_exp"), 1)
                    link(dve.tensor_tensor(lb, lbl[:, 0, :], lbl[:, 1, :], ALU.add))
                    link(dve.reciprocal(lb, lb))
                    link(dve.tensor_tensor(lb, lb, lbl[:, 0, :], ALU.mult))
                    link(dve.tensor_scalar(oml, lb, -1.0, 1.0, ALU.mult, ALU.add))
                dve.wait_ge(chunks_used, Z0 + c + 1)
                dve.tensor_copy(zq[:, c, :], B[4 + c % 2][:, 0:64]).then_inc(sem("z_dec_copied"), 1)

            def rotary(src, n, t0, nt):
                def part(lo):
                    return src.rearrange("p t (h d) -> p t h d", d=HD)[:, :, :, lo:lo + HALF]

                def table(name):
                    tab = C(name, slice(0, n)).rearrange("p (t f) -> p t f", t=3)[:, t0:t0 + nt, :]
                    return wide(tab.unsqueeze(2), 2, 10)

                def prod(i):
                    return rtmp[0:n, 0:nt, 80 * i:80 * (i + 1)].rearrange("p t (h f) -> p t h f", h=10)

                a, b = part(0), part(HALF)
                dve.tensor_tensor(prod(0), a, table("sin"), ALU.mult)
                link(dve.tensor_tensor(prod(1), b, table("sin"), ALU.mult))
                link(dve.tensor_tensor(a, a, table("cos"), ALU.mult))
                link(dve.tensor_tensor(b, b, table("cos"), ALU.mult))
                dve.tensor_tensor(a, a, prod(1), ALU.subtract)
                dve.tensor_tensor(b, b, prod(0), ALU.add).then_inc(sem("rotated"), 1)

            dve.wait_ge(sem("z_copied"), NZ)
            dve.wait_ge(sem("const_full"), 16)
            rotary(z[:, :, 0:AW + P], P, 0, 2)
            dve.wait_ge(sem("f_sig"), 1)
            f = z[:, :, F0:F0 + HW_]
            link(dve.tensor_tensor(f, f, wide(oml.unsqueeze(1), 1, 2), ALU.mult))
            dve.tensor_tensor(f, f, wide(lb.unsqueeze(1), 1, 2), ALU.add).then_inc(sem("f_ready"), 1)
            dve.wait_ge(sem("zs_full"), 128)
            rotary(zs[0:NB, 0:AW + P].unsqueeze(1), NB, 2, 1)
            dve.wait_ge(sem("f_sig"), 2)
            fs = zs[0:NB, F0:F0 + HW_]
            link(dve.tensor_tensor(fs, fs, oml[0:NB, :], ALU.mult))
            link(dve.tensor_tensor(fs, fs, lb[0:NB, :], ALU.add))
            dve.wait_ge(sem("logf_ready"), 1)
            dve.tensor_scalar(f, f, -1.0, 1.0, ALU.mult, ALU.add).then_inc(sem("k_ready"), 1)
            dve.tensor_scalar(oml[0:NB, :], fs, -1.0, 1.0, ALU.mult, ALU.add).then_inc(sem("k_ready"), 1)
            ksam = oml[0:NB, :]

            window = C("window")
            for n, t in enumerate((1, 0)):
                w = P * (t + 1)
                nb = 4 // (t + 1)
                if n:
                    dve.wait_ge(sem("pT_made"), 4)
                for i in range(8 // nb):
                    g, first = (i % 2, 2 * (i // 2)) if t else (i, 0)
                    bank = B[3 + 2 * g + i // 2] if t else B[(7 + g) % 8]
                    hd = GRP * g + first
                    dve.wait_ge(sem("sc_made"), 4 * n + i + 1)
                    ins = dve.scalar_tensor_tensor(
                        out=sc[:, hd * w:(hd + nb) * w].rearrange("p (m s) -> p m s", s=w),
                        in0=bank[:, :].rearrange("p (m s) -> p m s", s=w), scalar=HD ** -0.5,
                        in1=wide(window[:, 2 * P - w:2 * P].unsqueeze(1), 1, nb), op0=ALU.mult, op1=ALU.add)
                    ins.then_inc(sem("masked"), 1)
                dve.wait_ge(sem("masked"), 4 if n == 0 else 6)
                link(dve.tensor_reduce(mrow[:, t, :], sc[:, 0:HEADS * w].rearrange("p (m s) -> p m s", s=w), AX.X, ALU.max))
                link(dve.tensor_tensor(mrow[:, t, :], mrow[:, t, :], sinkb, ALU.max))
                link(dve.tensor_tensor(dsink[:, t, :], sinkb, mrow[:, t, :], ALU.subtract))
                dve.tensor_scalar(nmax[:, t, :], mrow[:, t, :], -1.0, None, ALU.mult).then_inc(sem("max_ready"), 1)
            for n, t in enumerate((1, 0)):
                dve.wait_ge(sem("esink_ready"), n + 1)
                link(dve.tensor_tensor(psums[:, t, :], psums[:, t, :], esink[:, t, :], ALU.add))
                link(dve.reciprocal(psums[:, t, :], psums[:, t, :]))
                dve.wait_ge(sem("pv_made"), n + 1)
                o = h[:, t, 0:AW]
                dve.tensor_tensor(o.rearrange("p (m d) -> p m d", d=HD), B[1 + n][:, :].rearrange("p (m d) -> p m d", d=HD),
                                  wide(psums[:, t, :].unsqueeze(2), 2, HD), ALU.mult).then_inc(sem("att_summed"), 1)
            dve.wait_ge(sem("att_summed"), 2)

            def mean_of(col, n):
                link(dve.tensor_scalar(gmean[0:n, col[0]:col[1]], gmean[0:n, col[0]:col[1]], 1.0, EPS, ALU.mult, ALU.add))

            lvl_mask = C("levels").bitcast(U32).rearrange("p (n t) -> p n t", n=8)
            for t in range(2):
                if t:
                    dve.wait_ge(sem("hgo_made"), 1)
                link(dve.memset(amat[:, :, :], 0.0))
                dve.wait_ge(sem("hg_copied"), 3 * t + 3)

                def diff(n):
                    m = LEVELS[n]
                    v = bT.rearrange("p (n two m) -> p n two m", two=2, m=m)
                    d = lev[n % 2].rearrange("p (n two m) -> p n two m", two=2, m=m)
                    ref = v[:, :, 0, m - 1:m]
                    ref = ref if m == 1 else wide(ref, 2, m)
                    if n >= 2:
                        dve.wait_ge(sem("G_made"), 8 * t + n)
                    elif t:
                        dve.wait_ge(sem("G_made"), 8)
                    dve.tensor_tensor(d[:, :, 0, :], ref, v[:, :, 0, :], ALU.subtract).then_inc(sem("lev_diff"), 1)
                    dve.tensor_tensor(d[:, :, 1, :], v[:, :, 1, :], ref, ALU.subtract).then_inc(sem("lev_diff"), 1)

                def weigh(n):
                    m = LEVELS[n]
                    d = lev[n % 2].rearrange("p (n two m) -> p n two m", two=2, m=m)
                    dve.wait_ge(sem("lev_exp"), 7 * t + n + 1)
                    dve.tensor_tensor(d[:, :, 0, :], d[:, :, 0, :], kkT.rearrange("p (n two m) -> p n two m", two=2, m=m)[:, :, 0, :], ALU.mult)
                    dve.tensor_tensor(d[:, :, 1, :], d[:, :, 1, :], qqT.rearrange("p (n two m) -> p n two m", two=2, m=m)[:, :, 1, :],
                                      ALU.mult).then_inc(sem("lev_ready"), 1)

                def take_level(n):
                    dve.wait_ge(sem("G_made"), 8 * t + n + 1)
                    dve.copy_predicated(amat[:, :, :], wide(lvl_mask[:, n, :].unsqueeze(1), 1, HH),
                                        B[4 + n % 2][:, :].rearrange("p (h t) -> p h t", h=HH)).then_inc(sem("lev_masked"), 1)

                diff(0)
                diff(1)
                take_level(0)
                for n in range(7):
                    weigh(n)
                    take_level(n + 1)
                    if n + 2 < 7:
                        diff(n + 2)
                dve.wait_ge(sem("tail_exp"), t + 1)
                dve.tensor_tensor(ks, ks, z[:, t, F0:F0 + HW_], ALU.mult).then_inc(sem("ks_ready"), 1)
                if t == 0:
                    modulation(1, ADA1 + N_ADA, B[7], None)
                    dve.wait_ge(sem("st_made"), 1)
                    dve.tensor_copy(st, B[3][:, :]).then_inc(sem("st_copied"), 1)
                else:
                    dve.wait_ge(sem("b_exp"), 2)
                    dve.tensor_tensor(lev[0], lev[0], qqT, ALU.mult).then_inc(sem("qb_ready"), 1)
                    modulation(2, ADA2 + N_ADA, B[2], (slice(0, 64), 1))
                    dve.wait_ge(sem("hgo_made"), 2)
                    dve.wait_ge(sem("st_made"), 2)
                    for hd in range(HH):
                        c = slice(P * hd, P * (hd + 1))
                        dve.scalar_tensor_tensor(out=st[:, c], in0=st[:, c], scalar=eb[:, hd:hd + 1], in1=B[3][:, c],
                                                 op0=ALU.mult, op1=ALU.add).then_inc(sem("state_final"), 1)
            for t in range(2):
                link(dve.tensor_tensor(amat[:, :, :].rearrange("p h t -> p (h t)"), h[:, t, 0:AW], h[:, t, 0:AW], ALU.mult))
                link(dve.tensor_reduce(gmean[:, t:t + 1], amat[:, :, :].rearrange("p h t -> p (h t)"), AX.X, ALU.add))
                dve.wait_ge(sem("hgo_made"), 2)
                link(dve.tensor_copy(h[:, t, AW:D], B[6 + t][:, :]))
                link(dve.tensor_tensor(amat[:, :, :].rearrange("p h t -> p (h t)"), h[:, t, AW:D], h[:, t, AW:D], ALU.mult))
                link(dve.tensor_reduce(gmean[:, 2 + 4 * t:6 + 4 * t], amat[:, :, :], AX.X, ALU.add))
            link(dve.tensor_scalar(gmean[:, 0:2], gmean[:, 0:2], 1.0 / AW, EPS, ALU.mult, ALU.add))
            dve.tensor_scalar(gmean[:, 2:10], gmean[:, 2:10], 1.0 / P, EPS, ALU.mult, ALU.add).then_inc(sem("gmeans"), 1)

            def normed(t, n, c0, h0, silu):
                link(dve.reciprocal(groot[0:n, c0:c0 + 1], groot[0:n, c0:c0 + 1]))
                link(dve.reciprocal(groot[0:n, h0:h0 + HH], groot[0:n, h0:h0 + HH]))
                dve.scalar_tensor_tensor(out=h[0:n, t, 0:AW], in0=h[0:n, t, 0:AW], scalar=groot[0:n, c0:c0 + 1],
                                         in1=g_att[0:n, :], op0=ALU.mult, op1=ALU.mult)
                for hd in range(HH):
                    c = slice(AW + P * hd, AW + P * (hd + 1))
                    ins = dve.scalar_tensor_tensor(out=h[0:n, t, c], in0=h[0:n, t, c], scalar=groot[0:n, h0 + hd:h0 + hd + 1],
                                                   in1=g_hg[0:n, P * hd:P * (hd + 1)], op0=ALU.mult, op1=ALU.mult)
                link(ins)
                dve.tensor_tensor(h[0:n, t, AW:D], h[0:n, t, AW:D], silu, ALU.mult).then_inc(sem("cat_ready"), 1)

            dve.wait_ge(sem("mod_ready"), 3)
            link(dve.memset(qbd, 0.0))
            for i in range(2):
                dve.wait_ge(sem("kcT_made"), i + 1)
                dve.tensor_copy(kcT[:, 4 * i:4 * i + 4, 0:P], B[i][:, :].rearrange("p (b s) -> p b s", b=4)).then_inc(sem("kcT_copied"), 1)
            dve.wait_ge(sem("snew_made"), 1)
            dve.tensor_copy(kcT[:, :, P], B[2][:, 0:NB]).then_inc(sem("snew_copied"), 1)
            for g in range(KV):
                r = slice(64 * g, 64 * g + 64)
                dve.tensor_copy(qbd[r, :].rearrange("p (b c) -> p b c", b=NB)[:, :, GRP * g:GRP * (g + 1)],
                                B[2][r, 16:48].rearrange("p (j b) -> p b j", j=GRP)).then_inc(sem("snew_copied"), 1)
            dve.wait_ge(sem("kcT_made"), 2)
            link(dve.memset(pbd, 0.0))
            dve.wait_ge(sem("ss_made"), 1)
            link(dve.tensor_scalar(ps[0:64, :], B[3][0:64, 0:129], HD ** -0.5, None, ALU.mult))
            link(dve.tensor_reduce(smx[0:64, :], ps[0:64, :], AX.X, ALU.max))
            dve.tensor_scalar(snm[0:64, :], smx[0:64, :], sink64[0:64, :], -1.0, ALU.max, ALU.mult).then_inc(sem("smax_ready"), 1)
            dve.wait_ge(sem("sqf_made"), 1)
            link(dve.tensor_copy(sq, B[0][:, 0:64]))
            onehot = C("onehot", slice(0, NB))

            def mask_keys(b):
                dve.tensor_scalar(km[b % 2][0:NB, :], ksam, onehot[:, b:b + 1], None, ALU.mult).then_inc(sem("km_ready"), 1)

            dve.wait_ge(sem("k_ready"), 2)
            mask_keys(0)
            mask_keys(1)
            dve.wait_ge(sem("g_silu"), 2)
            dve.wait_ge(sem("groots"), 1)
            for t in range(2):
                normed(t, P, t, 2 + 4 * t, z[:, t, G0:G0 + HW_])
            for i in (1, 3):
                dve.wait_ge(sem("catT_made"), i + 1)
                dve.tensor_copy(hT[:, 2 * i:2 * i + 2, 0:S], B[4 + i][:, :].rearrange("p (k t) -> p k t", k=2)).then_inc(sem("catT_copied_d"), 1)
            dve.wait_ge(sem("spT_made"), 1)
            dve.tensor_copy(pbd.rearrange("p (b c) -> p b c", b=NB)[:, :, 0:HEADS],
                            B[5][:, 0:64].rearrange("p (b h) -> p b h", b=NB)).then_inc(sem("pbd_ready"), 1)
            dve.wait_ge(sem("states_full"), 16 * NB)
            for b in range(NB):
                dve.wait_ge(sem("outer_made"), b + 1)
                for hd in range(HH):
                    fcol = 32 + NB * hd + b
                    dve.scalar_tensor_tensor(out=states[:, b, hd, :], in0=states[:, b, hd, :], scalar=sq[:, fcol:fcol + 1],
                                             in1=B[6 + b % 2][:, P * hd:P * (hd + 1)], op0=ALU.mult, op1=ALU.add).then_inc(sem("states_new"), 1)
                if b + 2 < NB:
                    mask_keys(b + 2)
            dve.wait_ge(sem("sprobs"), 2)
            link(dve.tensor_tensor(ssm[0:64, :], ssm[0:64, :], sesk[0:64, :], ALU.add))
            link(dve.reciprocal(ssm[0:64, :], ssm[0:64, :]))
            dve.tensor_tensor(sra[0:64, :], ssm[0:64, :], C("group", slice(0, 64))[:, 0:1], ALU.mult)
            link(dve.tensor_tensor(srb[0:64, :], ssm[0:64, :], C("group", slice(0, 64))[:, 1:2], ALU.mult))
            dve.wait_ge(sem("pv_copied"), 1)
            link(dve.scalar_tensor_tensor(out=pv[0:64, :], in0=B[5][0:64, 0:P], scalar=ps[0:64, P:P + 1], in1=pv[0:64, :],
                                          op0=ALU.mult, op1=ALU.add))
            link(dve.tensor_scalar(o64[0:64, :], pv[0:64, 0:HD], sra[0:64, :], None, ALU.mult))
            dve.scalar_tensor_tensor(out=o64[0:64, :], in0=pv[0:64, HD:P], scalar=srb[0:64, :], in1=o64[0:64, :],
                                     op0=ALU.mult, op1=ALU.add).then_inc(sem("o64_ready"), 1)
            dve.wait_ge(sem("wo_made"), 1)
            dve.wait_ge(sem("mod_rows_full"), 32)
            for t in range(2):
                for a in range(2):
                    c = slice(512 * a, 512 * (a + 1))
                    ins = dve.tensor_tensor(h[:, t, c], B[2 * t + a][:, :], rows1[:, c], ALU.mult)
                link(ins)
                dve.tensor_tensor(x[:, t, :], x[:, t, :], h[:, t, :], ALU.add).then_inc(sem("x1_ready"), 1)
                dve.wait_ge(sem("x1_ready"), t + 1)

            def second_norm(t, scale, shift):
                r = slice(0, NT[t])
                dve.wait_ge(sem("roots"), 3 + t + 1)
                link(dve.reciprocal(root3[r, t:t + 1], root3[r, t:t + 1]))
                link(dve.scalar_tensor_tensor(out=h[r, t, :], in0=x[r, t, :], scalar=root3[r, t:t + 1], in1=scale,
                                              op0=ALU.mult, op1=ALU.mult))
                dve.tensor_tensor(h[r, t, :], h[r, t, :], shift, ALU.add).then_inc(sem("h2_ready"), 1)

            for t in range(2):
                means(t, 1)
            for t in range(2):
                second_norm(t, scale2, rows1[:, D:2 * D])
            dve.memset(hT[:, :, NTOK:288], 0.0)
            dve.wait_ge(sem("soT_made"), 1)
            dve.tensor_copy(soT, B[4][:, 0:HH * NB]).then_inc(sem("soT_copied"), 1)
            sqs = ks[0:NB, :]
            dve.wait_ge(sem("o64_moved"), 16)
            dve.wait_ge(sem("st_made"), 2)
            link(dve.tensor_tensor(sqs, h[0:NB, 2, 0:AW], h[0:NB, 2, 0:AW], ALU.mult))
            link(dve.tensor_reduce(gmean[0:NB, 10:11], sqs, AX.X, ALU.add))
            dve.wait_ge(sem("so_made"), 1)
            link(dve.tensor_copy(h[0:NB, 2, AW:D], B[6][0:NB, :]))
            link(dve.tensor_tensor(sqs, h[0:NB, 2, AW:D], h[0:NB, 2, AW:D], ALU.mult))
            link(dve.tensor_reduce(gmean[0:NB, 11:15], sqs.rearrange("p (h v) -> p h v", h=HH), AX.X, ALU.add))
            dve.tensor_scalar(gmean[0:NB, 11:15], gmean[0:NB, 11:15], 1.0 / P, EPS, ALU.mult, ALU.add)
            dve.tensor_scalar(gmean[0:NB, 10:11], gmean[0:NB, 10:11], 1.0 / AW, EPS, ALU.mult, ALU.add).then_inc(sem("gmeans"), 1)
            dve.wait_ge(sem("groots"), 2)
            normed(2, NB, 10, 11, zs[0:NB, G0:G0 + HW_])
            dve.wait_ge(sem("catT_made"), 5)
            dve.tensor_copy(hT[:, :, S:NTOK], B[7][:, 0:NB * KT].rearrange("p (k b) -> p k b", k=KT)).then_inc(sem("catT_copied_d"), 1)
            dve.wait_ge(chunks_used, PRE)
            dve.tensor_copy(zq[:, 0:4, :], B[5][:, 0:256].rearrange("p (c n) -> p c n", c=4)).then_inc(sem("wo_dec_copied"), 1)
            dve.wait_ge(sem("mod_rows_s_full"), 48)
            dve.wait_ge(sem("wo_dec_full"), 64)
            link(dve.tensor_tensor(tmps[0:NB, :], tmps[0:NB, :], rows1s[0:NB, 0:D], ALU.mult))
            dve.tensor_tensor(x[0:NB, 2, :], x[0:NB, 2, :], tmps[0:NB, :], ALU.add).then_inc(sem("x1_ready"), 1)
            dve.wait_ge(sem("x1_ready"), 3)
            means(2, 1)
            second_norm(2, rows2s[0:NB, 0:D], rows1s[0:NB, D:2 * D])
            odd_tiles("h2T_made", "h2T_copied_d")
            dve.tensor_copy(tok_i[:, :], C("tok"))
            link(dve.memset(lg[:, :, :], 0.0))
            dve.wait_ge(sem("lgT_made"), 1)
            dve.tensor_scalar(lgT[0:E, :], B[0][0:E, 0:NTOK], brout[0:E, :], None, ALU.add).then_inc(sem("lgT_ready"), 1)
            dve.wait_ge(sem("lg_made"), 1)
            dve.tensor_copy(lg[:, 0:2, :], B[1][:, 0:2 * E].rearrange("p (t e) -> p t e", t=2))
            link(dve.tensor_copy(lg[0:NB, 2, :], B[1][0:NB, 2 * E:3 * E]))
            for t in range(3):
                ins = dve.max(top8[:, t, :], lg[:, t, :])
            link(ins)
            for t in range(3):
                ins = dve.max_index(top8i[:, t, :], top8[:, t, :], lg[:, t, :])
            link(ins)
            dve.tensor_scalar(ntop, top8[:, :, 0], -1.0, None, ALU.mult).then_inc(sem("top_ready"), 1)
            link(dve.tensor_copy(topf[:, :, :], top8i[:, :, 0:TOPK]))
            link(dve.tensor_tensor(onek[:, :, :, :].rearrange("p t k e -> p (t k) e"), wide(C("iota").unsqueeze(1), 1, 3 * TOPK),
                                   wide(topf.rearrange("p t k -> p (t k)").unsqueeze(2), 2, E), ALU.is_equal))
            dve.tensor_reduce(chosen[:, :, :], onek[:, :, :, :].rearrange("p t k e -> p t e k"), AX.X, ALU.add).then_inc(sem("chosen_ready"), 1)
            dve.wait_ge(sem("rank_made"), 1)
            rank = B[2][:, 0:3 * E]
            dve.tensor_tensor(slotf.rearrange("p (t e) -> p t e", t=3), rank.rearrange("p (t e) -> p t e", t=3),
                              wide(C("e64").unsqueeze(1), 1, 3), ALU.add)
            link(dve.tensor_scalar(over, rank, float(SLOTS), None, ALU.is_ge))
            for m in range(2, MAXPASS):
                link(dve.scalar_tensor_tensor(out=over, in0=rank, scalar=float(SLOTS * m), in1=over, op0=ALU.is_ge, op1=ALU.add))
            link(dve.scalar_tensor_tensor(out=slotf, in0=over, scalar=float(ROWS - SLOTS), in1=slotf, op0=ALU.mult, op1=ALU.add))
            link(dve.tensor_tensor(hit[:, :, :, :], onek[:, :, :, :],
                                   wide(slotf.rearrange("p (t e) -> p t e", t=3).unsqueeze(2), 2, TOPK), ALU.mult))
            link(dve.tensor_reduce(topf[:, :, :], hit[:, :, :, :], AX.X, ALU.add))
            dve.tensor_copy(slot_u[:, :, :], topf[:, :, :]).then_inc(sem("slots_ready"), 1)
            link(dve.tensor_tensor(hit[:, :, :, :], onek[:, :, :, :],
                                   wide(over.rearrange("p (t e) -> p t e", t=3).unsqueeze(2), 2, TOPK), ALU.mult))
            link(dve.tensor_reduce(passf[:, :, :], hit[:, :, :, :], AX.X, ALU.add))
            dve.scalar_tensor_tensor(out=row_u[:, :, :], in0=passf[:, :, :], scalar=-float(ROWS), in1=topf[:, :, :],
                                     op0=ALU.mult, op1=ALU.add).then_inc(sem("slots_ready"), 1)
            link(dve.tensor_reduce(cmax[0:1, :], B[3][0:1, 0:E], AX.X, ALU.max))
            dve.memset(chit[0:1, 0:1], 1.0)
            for m in range(1, MAXPASS):
                ins = dve.tensor_scalar(chit[0:1, m:m + 1], cmax[0:1, :], float(SLOTS * m), None, ALU.is_gt)
            link(ins)
            link(dve.tensor_reduce(csum[0:1, :], chit[0:1, :], AX.X, ALU.add))
            dve.tensor_copy(npass[:, :], csum[0:1, :]).then_inc(sem("npass_ready"), 1)
            dve.wait_ge(sem("stored"), 16 * N_STORED)
            for e in range(2):
                dve.memset(bias[e], 0.0).then_inc(sem("bias_cleared"), 1)
            dve.wait_ge(sem("top_exp"), 3)
            link(dve.reciprocal(tsum, tsum))
            link(dve.tensor_tensor(topw[:, :, :], topw[:, :, :], wide(tsum.unsqueeze(2), 2, TOPK), ALU.mult))

            dve.wait_ge(sem("npass_ready"), 1)
            passes = dve.value_load(npass[0:1, 0:1], min_val=1, max_val=MAXPASS)
            link(dve.memset(moe[:, :, :], 0.0))
            link(dve.memset(now, 0.0))
            count_from_one(dve, "g_ready", "u_read", "y_added")
            with dve.Fori(0, passes) as p:
                with dve.Fori(0, PAIRS) as i:
                    it = dve.snap(p * PAIRS + i)
                    dve.wait_ge(sem("xT_made"), it * 2 + 2)
                    dve.tensor_copy(xT[:, 0:4, :], B[6][:, :].rearrange("p (k t) -> p k t", k=4)).then_inc(sem("xT_copied_d"), 1)
                    for e in range(2):
                        dve.wait_ge(chunks_used, it * PER + (PRE + 8 * (e + 1)))
                        dve.wait_ge(sem("g_ready"), it * 2 + (e + 1))
                        for b in range(2):
                            u = B[2 * e + b][:, :].rearrange("p (n two) -> p n two", two=2)
                            ins = dve.tensor_scalar(glu[:, 256 * b:256 * (b + 1)], u[:, :, 0], LIMIT, None, ALU.min)
                        ins.then_inc(sem("glu_ready"), 1)
                        for b in range(2):
                            u = B[2 * e + b][:, :].rearrange("p (n two) -> p n two", two=2)
                            ins = dve.tensor_scalar(lin[:, 256 * b:256 * (b + 1)], u[:, :, 1], LIMIT, -LIMIT, ALU.min, ALU.max)
                        ins.then_inc(sem("u_read"), 1)
                        dve.wait_ge(sem("u_read"), it * 2 + (e + 2))
                        dve.scalar_tensor_tensor(out=lin, in0=lin, scalar=1.0, in1=glu, op0=ALU.add, op1=ALU.mult).then_inc(sem("lin_ready"), 1)
                        dve.wait_ge(sem("lin_ready"), it * 2 + (e + 1))
                        dve.wait_ge(sem("sig_ready"), it * 2 + (e + 1))
                        dve.wait_ge(sem("gT_made"), it * 2 + 1)
                        dve.tensor_tensor(gg[e], lin, sg, ALU.mult).then_inc(sem("g_ready"), 1)
                with dve.If(p < passes - 1):
                    dve.tensor_scalar(passw[:, :, :], passf[:, :, :], now, None, ALU.is_equal).then_inc(sem("pass_step"), 1)
                    dve.wait_ge(sem("pass_step"), p * 3 + 1)
                    dve.tensor_tensor(passw[:, :, :], passw[:, :, :], topw[:, :, :], ALU.mult).then_inc(sem("pass_step"), 1)
                    dve.wait_ge(sem("pass_step"), p * 3 + 2)
                    for n in range(3 * TOPK):
                        t, k = divmod(n, TOPK)
                        r = slice(0, NT[t])
                        dve.wait_ge(sem("y_part"), p * (16 * 3 * TOPK) + 16 * (n + 1))
                        dve.scalar_tensor_tensor(out=moe[r, t, :], in0=xg[r, :], scalar=passw[r, t, k:k + 1],
                                                 in1=moe[r, t, :], op0=ALU.mult, op1=ALU.add).then_inc(sem("y_added"), 1)
                        dve.wait_ge(sem("y_added"), p * (3 * TOPK) + (n + 2))
                    dve.tensor_scalar(now, now, 1.0, None, ALU.add).then_inc(sem("pass_step"), 1)
                    dve.wait_ge(sem("pass_step"), p * 3 + 3)
                    dve.nop(nofuse=True)
            link(dve.tensor_scalar(passw[:, :, :], passf[:, :, :], now, None, ALU.is_equal))
            link(dve.tensor_tensor(passw[:, :, :], passw[:, :, :], topw[:, :, :], ALU.mult))
            dve.wait_ge(sem("gfin_full"), 16)

            def final_norm(t):
                n = NT[t]
                dve.wait_ge(sem("roots"), 6 + t + 1)
                link(dve.reciprocal(root3[0:n, t:t + 1], root3[0:n, t:t + 1]))
                dve.scalar_tensor_tensor(out=x[0:n, t, :], in0=x[0:n, t, :], scalar=root3[0:n, t:t + 1], in1=g_fin[0:n, :],
                                         op0=ALU.mult, op1=ALU.mult).then_inc(sem("result"), 1)

            for t in range(3):
                n = NT[t]
                for k in range(TOPK):
                    dve.wait_ge(y_full(t, k), 64 if t else 32)
                    link(dve.scalar_tensor_tensor(out=moe[0:n, t, :], in0=yk[t][k][0:n, :], scalar=passw[0:n, t, k:k + 1],
                                                  in1=moe[0:n, t, :], op0=ALU.mult, op1=ALU.add))
                    if k == 1 and t:
                        means(t - 1, 2)
                link(dve.tensor_tensor(moe[0:n, t, :], moe[0:n, t, :], rows2s[0:n, D:2 * D] if t == 2 else gate2, ALU.mult))
                dve.tensor_tensor(x[0:n, t, :], x[0:n, t, :], moe[0:n, t, :], ALU.add).then_inc(sem("x2_ready"), 1)
                if t:
                    final_norm(t - 1)
            means(2, 2)
            final_norm(2)


INS = ["x_prompt", "x_sample", "c_prompt", "c_sample", "cache_k_win", "cache_v_win", "state_hgrn", "w_ada", "b_ada",
       "g_mix", "g_ffn", "w_in", "attn_sinks", "g_attn_out", "hg_lb_logits", "g_hg_out", "w_out", "w_router",
       "b_router", "w_up", "b_up", "w_down", "b_down", "g_final"]
OUTS = [("yp", (1, S, D)), ("ys", (NB, 1, D)), ("kwp", (1, 1, WIN, KV, HD)), ("vwp", (1, 1, WIN, KV, HD)),
        ("hgp", (1, 1, HH, P, P)), ("kws", (1, NB, WIN, KV, HD)), ("vws", (1, NB, WIN, KV, HD)),
        ("hgs", (1, NB, HH, P, P))]


def kernel(**inputs):
    import concourse.bacc as bacc
    from concourse.bass_utils import run_bass_kernel_spmd as run

    nc = bacc.Bacc("TRN2", target_bir_lowering=False, num_devices=1)
    arrays, ins, outs = {}, {}, {}
    given = {name: np.ascontiguousarray(inputs[name]) for name in INS}
    given["const"] = constants()
    for name, a in given.items():
        arrays[f"in_{name}"] = a
        ins[name] = nc.dram_tensor(f"in_{name}", a.shape, mybir.dt.from_np(a.dtype), kind="ExternalInput").ap()
    for name, shape in OUTS:
        outs[name] = nc.dram_tensor(f"out_{name}", shape, F32, kind="ExternalOutput").ap()
    hybrid_layer(nc, ins, outs)
    r = run(nc, [arrays], core_ids=[0])
    return tuple(r.results[0][f"out_{name}"] for name, _ in OUTS)
```

```python
from contextlib import ExitStack

import numpy as np

import concourse.bass as bass
from concourse import mybir

F32 = mybir.dt.float32
I32 = mybir.dt.int32
U32 = mybir.dt.uint32
ALU = mybir.AluOpType
ACT = mybir.ActivationFunctionType
AX = mybir.AxisListType

P = 128
D = 1024
KT = D // P
S = 256
NB = 8
NTOK = S + NB
HEADS, KV, HD = 8, 2, 64
GRP = HEADS // KV
WIN = 128
ROT = HD // 4
HALF = ROT // 2
AW = HEADS * HD
HH = 4
HW_ = HH * P
QKV = AW + 2 * KV * HD
IN_COLS = QKV + 4 * HW_
ZC = 256
NZ = IN_COLS // ZC
E = 32
TOPK = 4
FF2 = 2 * D
EPS = 1e-5
PAST = 2048
SLOTS = 64
ARENA = 29300
N_STORED = 2 + 2 + 2 + 1 + NB
ROWS = E * SLOTS
MAXPASS = -(-NTOK // SLOTS)
PAIRS = E // 2
LIMIT = 7.0
ALPHA = 1.702
NEG = -1e30
LEVELS = [1 << i for i in range(7)]

RING = 8
RING2 = 12
CH = 2048
N_ADA = 8
Z0 = N_ADA
ADA1 = Z0 + NZ
ADA2 = ADA1 + N_ADA
WO0 = ADA2 + N_ADA
PRE = WO0 + 4
PER = 24

_COLS = {}
_at = 0
for _name, _n in (("ident", P), ("incl", P), ("after", P), ("before", P), ("ones", P), ("levels", 8 * P),
                  ("window", 2 * P), ("pick", P), ("cos", 3 * HALF), ("sin", 3 * HALF), ("e64", E),
                  ("iota", E), ("tok", 3), ("spread", 64), ("onehot", NB), ("bias_row", SLOTS), ("group", 2)):
    _COLS[_name] = (_at, _at + _n)
    _at += _n
NCONST = _at


def constants():
    c = np.zeros((P, NCONST), np.float32)

    def put(name, a, rows=P):
        lo, hi = _COLS[name]
        c[:rows, lo:hi] = np.asarray(a, np.float32).reshape(rows, hi - lo)

    r = np.arange(P)
    put("ident", np.eye(P))
    put("incl", r[:, None] <= r[None, :])
    put("after", r[:, None] > r[None, :])
    put("before", r[:, None] < r[None, :])
    put("ones", np.ones((P, P)))
    masks = [np.eye(P)]
    for m in LEVELS:
        same = r[:, None] // (2 * m) == r[None, :] // (2 * m)
        masks.append(same & (r[:, None] % (2 * m) < m) & (r[None, :] % (2 * m) >= m))
    put("levels", np.stack(masks, 1))
    diff = r[:, None] + P - np.arange(2 * P)[None, :]
    put("window", np.where((diff >= 0) & (diff <= WIN), 0.0, NEG))
    pick = np.zeros((P, P))
    pick[::32] = 1
    put("pick", pick)
    inv = np.float32(500000.0) ** (-(np.arange(HALF, dtype=np.float32) * np.float32(2.0) / np.float32(ROT)))
    pos = np.zeros((3, P), np.float32)
    pos[0], pos[1], pos[2] = r, r + P, PAST
    ang = (pos[:, :, None] * inv.astype(np.float32)[None, None, :]).astype(np.float32)
    put("cos", np.cos(ang).transpose(1, 0, 2))
    put("sin", np.sin(ang).transpose(1, 0, 2))
    put("e64", np.tile(np.arange(E) * SLOTS, (P, 1)))
    put("iota", np.tile(np.arange(E), (P, 1)))
    put("tok", np.stack([r, r + P, r + 2 * P], 1))
    put("spread", np.repeat(np.eye(NB), HEADS, 1), NB)
    put("onehot", np.eye(NB), NB)
    br = np.zeros((P, SLOTS))
    br[0] = 1
    put("bias_row", br)
    h = np.arange(64) % HEADS
    put("group", np.stack([h < GRP, h >= GRP], 1), 64)
    return c


def wide(ap, dim, n):
    shape = list(ap.shape)
    shape[dim] = n
    return ap.broadcast_to(shape)


def hybrid_layer(nc, A, O):
    with ExitStack() as ctx:
        sems = {}

        def sem(name):
            if name not in sems:
                sems[name] = ctx.enter_context(nc.semaphore(name))
            return sems[name]

        def sb(name, shape, dt=F32):
            return ctx.enter_context(nc.sbuf_tensor(name, shape, dt))

        B = [ctx.enter_context(nc.psum_tensor(f"bank{i}", [P, 512], F32)) for i in range(8)]

        const = sb("const", [P, NCONST])

        def C(name, rows=slice(0, P)):
            lo, hi = _COLS[name]
            return const[rows, lo:hi]

        ident = C("ident")
        ring = sb("ring", [P, RING, CH])
        x = sb("x", [P, 3, D])
        mods = sb("mods", [P, 3, 512])
        slot_u = sb("slot_u", [P, 3, TOPK], U32)
        row_u = sb("row_u", [P, 3, TOPK], U32)
        topw = sb("topw", [P, 3, TOPK])
        npass = sb("npass", [1, 1], I32)
        small = sb("small", [P, 256])
        zeros = sb("zeros", [P, MAXPASS * ROWS // P], I32)
        tok_i = sb("tok_i", [P, 3], I32)
        idx = sb("idx", [P, 1], I32)

        arena = sb("arena", [P, ARENA])
        top = [0]

        def take(n, at=None):
            lo = top[0] if at is None else at
            if at is None:
                top[0] += n
            assert lo + n <= ARENA, (lo, n)
            return arena[:, lo:lo + n]

        z_at = top[0]
        z = take(2 * IN_COLS).rearrange("p (t c) -> p t c", t=2)
        zs_at = top[0]
        zs = take(IN_COLS)
        zq = take(NZ * 64).rearrange("p (c n) -> p c n", c=NZ)
        h = take(3 * D).rearrange("p (t c) -> p t c", t=3)
        hT_at = top[0]
        hT = take(KT * 288).rearrange("p (k t) -> p k t", k=KT)
        bT, kkT, qqT = (take(HW_, hT_at + n * HW_) for n in range(3))
        lb, oml, g_att, g_hg = (take(512) for _ in range(4))
        ada_at = top[0]
        ba = take(3 * 512).rearrange("p (q c) -> p q c", q=3)
        gb = take(2 * 512).rearrange("p (q c) -> p q c", q=2)
        scT = take(KT * 32).rearrange("p (k t) -> p k t", k=KT)
        take(840)
        vc = take(NB * P, ada_at + 1024).rearrange("p (b c) -> p b c", b=NB)
        kcT = take(NB * 129, ada_at + 2048).rearrange("p (b s) -> p b s", b=NB)
        qbd = take(NB * 72, ada_at + 3080)
        pbd = take(NB * 72, ada_at)
        att_at = top[0]
        qT = take(4 * S).rearrange("p (j t) -> p j t", j=4)
        kT = take(S)
        sc_at = top[0]
        sc = take(HEADS * 2 * P)
        pT = take(HEADS * 2 * P).rearrange("p (n q) -> p n q", q=P)
        crow = take(D, sc_at)
        states = take(NB * HW_, att_at).rearrange("p (b h v) -> p b h v", b=NB, h=HH)
        km = [take(HW_, att_at + 4096 + n * HW_) for n in range(2)]
        kc = take(NB * P, att_at + 4096).rearrange("p (b c) -> p b c", b=NB)
        logf_at = top[0]
        logf = take(2 * HW_).rearrange("p (t c) -> p t c", t=2)
        lbl = take(2 * 512, logf_at).rearrange("p (q c) -> p q c", q=2)
        ps = take(129, logf_at)
        pv = take(P, logf_at + 129)
        o64 = take(64, logf_at + 257)
        sq = take(2 * HH * NB, logf_at + 321)
        soT = take(HH * NB, logf_at + 385)
        lev = [take(HW_), take(HW_), take(HW_, ada_at + 3080)]
        amat = take(HW_).rearrange("p (h t) -> p h t", h=HH)
        ks = take(HW_)
        st = take(HW_)
        rows0s = take(2 * D, z_at)
        rows1 = take(2 * D, z_at)
        scale2 = take(D, z_at + 2 * D)
        tmps = take(D, z_at + 3 * D)
        lgT = take(NTOK, z_at + 4 * D)
        lg = take(3 * E, z_at + 4 * D + 264).rearrange("p (t e) -> p t e", t=3)
        chosen = take(3 * E, z_at + 4 * D + 360).rearrange("p (t e) -> p t e", t=3)
        onek = take(3 * TOPK * E, z_at + 4 * D + 456).rearrange("p (t k e) -> p t k e", t=3, k=TOPK)
        hit = take(3 * TOPK * E, zs_at).rearrange("p (t k e) -> p t k e", t=3, k=TOPK)
        over = take(3 * E, zs_at + 384).rearrange("p (t e) -> p t e", t=3)
        slotf = take(3 * E, zs_at + 480).rearrange("p (t e) -> p t e", t=3)
        wr = take(KT * E, z_at + 5 * D).rearrange("p (k e) -> p k e", k=KT)
        bias = [take(FF2 + D, n * 3 * D) for n in range(2)]
        top2 = [6 * D]

        def later(n):
            top2[0] += n
            return take(n, top2[0] - n)

        xg = later(D)
        xT = later(D).rearrange("p (k t) -> p k t", k=KT)
        glu, lin, sg = (later(512) for _ in range(3))
        diag = glu.rearrange("p (k t) -> p k t", k=TOPK)
        gg = [later(512) for _ in range(2)]
        gT = [later(512) for _ in range(2)]
        ysb = [later(512) for _ in range(2)]
        yk = [[ring[:, (t * TOPK + k) // 2, D * (k % 2):D * (k % 2 + 1)] for k in range(TOPK)] for t in range(3)]
        moe = later(3 * D).rearrange("p (t c) -> p t c", t=3)
        g_fin = later(D)
        more_ring = [later(CH) for n in range(RING2 - RING)]
        gate2 = later(D)
        rows2s = later(2 * D)
        rows1s = take(2 * D, zs_at + 640)

        scol = [0]

        def stat(n):
            scol[0] += n
            return small[:, scol[0] - n:scol[0]]

        ssum3, root3 = stat(3), stat(3)
        sinkb, sink64, brout = stat(HEADS), stat(1), stat(1)
        mrow = stat(2 * HEADS).rearrange("p (t h) -> p t h", t=2)
        nmax = stat(2 * HEADS).rearrange("p (t h) -> p t h", t=2)
        dsink = stat(2 * HEADS).rearrange("p (t h) -> p t h", t=2)
        esink = stat(2 * HEADS).rearrange("p (t h) -> p t h", t=2)
        psums = stat(2 * HEADS).rearrange("p (t h) -> p t h", t=2)
        smx, snm, ssm, sesk, sra, srb = (stat(1) for _ in range(6))
        gmean, groot = stat(15), stat(15)
        eb = stat(HH)
        top8 = stat(24).rearrange("p (t k) -> p t k", t=3)
        topf = stat(12).rearrange("p (t k) -> p t k", t=3)
        ntop, tsum = stat(3), stat(3)
        cmax, csum = stat(1), stat(1)
        chit = stat(MAXPASS)
        passf = stat(12).rearrange("p (t k) -> p t k", t=3)
        now, passw = stat(1), stat(12).rearrange("p (t k) -> p t k", t=3)
        top8i = sb("top8i", [P, 24], U32)[:, :].rearrange("p (t k) -> p t k", t=3)
        rtmp = take(2 * 160, ada_at + 3080).rearrange("p (t n) -> p t n", t=2)

        mod_dram = nc.dram_tensor("mod_rows", [2, 1 + NB, 2 * D], F32, kind="Internal").ap()
        h2_dram = nc.dram_tensor("h2_rows", [NTOK, D], F32, kind="Internal").ap()
        y_dram = nc.dram_tensor("y_rows", [ROWS, D], F32, kind="Internal").ap()
        list_dram = nc.dram_tensor("slot_tokens", [MAXPASS * ROWS, 1], I32, kind="Internal").ap()

        full = [sem(f"ring_full{i}") for i in range(RING2)]
        chunks_used = sem("chunks_used")

        NT = [P, P, NB]
        Q0, F0, I0, G0 = QKV, QKV + HW_, QKV + 2 * HW_, QKV + 3 * HW_
        K0, V0 = AW, AW + P

        w_ada = A["w_ada"][0].rearrange("(k p) n -> k p n", p=P)
        w_in = A["w_in"][0].rearrange("(k p) n -> p k n", p=P)
        w_out = A["w_out"][0].rearrange("(c two p) n -> c p two n", two=2, p=P)
        w_up = A["w_up"][0].rearrange("e (k p) n -> (e k) p n", p=P)
        w_down = A["w_down"][0].rearrange("e (c two p) n -> (e c) p two n", two=2, p=P)

        def place(n):
            c = (n - PRE) % RING2
            return n % RING if n < PRE else (PRE + c) % RING if c < RING else c

        def loads(n):
            return sum(place(m) == place(n) for m in range(n + 1))

        def chunk(n):
            return ring[:, place(n), :] if place(n) < RING else more_ring[place(n) - RING]

        def two(ap):
            return ap.rearrange("p (two n) -> p two n", two=2)

        def count_from_one(engine, *names):
            for name in names:
                engine.sem_inc(sem(name), 1)

        LAST = (0, 2, 1)

        def y_full(t, k):
            return sem(f"y_full{t}" if t else f"y_full0_{k // 2}")

        block = ctx.enter_context(nc.Block())

        @block.sync
        def _(sp):
            def room(n):
                if n >= RING:
                    sp.wait_ge(chunks_used, n - RING + 1)

            for k in range(N_ADA):
                room(k)
                sp.dma_start(chunk(k), w_ada[k, :, 0:CH]).then_inc(full[place(k)], 16)
            for c in range(NZ):
                room(Z0 + c)
                if c == 3:
                    sp.wait_ge(sem("mod_rows0_full"), 64)
                sp.dma_start(chunk(Z0 + c).rearrange("p (k n) -> p k n", k=KT),
                             w_in[:, :, c * ZC:(c + 1) * ZC]).then_inc(full[place(Z0 + c)], 16)
            for q, first in ((1, ADA1), (2, ADA2)):
                for k in range(N_ADA):
                    room(first + k)
                    sp.dma_start(chunk(first + k), w_ada[k, :, q * CH:(q + 1) * CH]).then_inc(full[place(first + k)], 16)
            for c in range(4):
                room(WO0 + c)
                sp.dma_start(two(chunk(WO0 + c)), w_out[c]).then_inc(full[place(WO0 + c)], 16)

            def expert_chunk(c, pair):
                n = PRE + c
                if c < 16:
                    sp.dma_start(chunk(n), w_up[pair * 16 + c]).then_inc(full[place(n)], 16)
                else:
                    sp.dma_start(two(chunk(n)), w_down[pair * 8 + (c - 16)]).then_inc(full[place(n)], 16)

            for c in range(4):
                room(PRE + c)
                expert_chunk(c, 0)
            sp.wait_ge(sem("cat_ready"), 3)
            sp.wait_ge(sem("stored"), 16 * N_STORED)
            for c in range(RING, RING + 2):
                expert_chunk(c, 0)
            sp.wait_ge(sem("wo_dec_full"), 64)
            for c in range(4, RING):
                room(PRE + c)
                expert_chunk(c, 0)
            for c in range(RING + 2, RING2):
                expert_chunk(c, 0)
            sp.wait_ge(sem("npass_ready"), 1)
            sp.wait_ge(sem("bias_cleared"), 2)
            passes = sp.value_load(npass[0:1, 0:1], min_val=1, max_val=MAXPASS)
            total = sp.snap(passes * PAIRS)
            with sp.Fori(0, total) as it:
                for c in range(RING2, PER):
                    sp.wait_ge(chunks_used, it * PER + (PRE + c - RING2 + 1))
                    expert_chunk(c, it % PAIRS)
                with sp.If(it < total - 1):
                    for c in range(RING2):
                        sp.wait_ge(chunks_used, it * PER + (PRE + PER + c - RING2 + 1))
                        expert_chunk(c, (it + 1) % PAIRS)
            for n, t in enumerate(LAST):
                sp.wait_ge(sem("result"), n + 1)
                dst = O["yp"][0, P * t:P * t + P] if t < 2 else O["ys"].rearrange("b s d -> (b s) d")
                sp.dma_start(dst, x[0:NT[t], t, :]).then_inc(sem("result_stored"), 16)
            sp.wait_ge(sem("result_stored"), 48)

        @block.gpsimd
        def _(pool):
            pool.wait_ge(sem("cleared"), 1)
            for q in range(3):
                for j in range(4):
                    n0 = q * CH + j * 512
                    pool.dma_start(ba[32 * j:32 * j + 9, q, :],
                                   wide(A["b_ada"][0:1, n0:n0 + 512], 0, 9)).then_inc(sem("ada_rows_full"), 16)
            for j in range(2):
                pool.dma_start(gb[64 + 32 * j:64 + 32 * j + 9, 0, :],
                               wide(A["g_mix"][0:1, j * 512:(j + 1) * 512], 0, 9)).then_inc(sem("ada_rows_full"), 16)
                pool.dma_start(gb[32 * j:32 * j + 9, 1, :],
                               wide(A["g_ffn"][0:1, j * 512:(j + 1) * 512], 0, 9)).then_inc(sem("ada_rows_full"), 16)
            pool.dma_start(lbl[:, 0, :], wide(A["hg_lb_logits"][0:1, :], 0, P)).then_inc(sem("rows_full"), 16)
            pool.dma_start(lbl[:, 1, :], wide(A["hg_lb_logits"][1:2, :], 0, P)).then_inc(sem("rows_full"), 16)
            pool.dma_start(g_att, wide(A["g_attn_out"][0:1, :], 0, P)).then_inc(sem("rows_full"), 16)
            pool.dma_start(g_hg, wide(A["g_hg_out"].rearrange("a h v -> a (h v)"), 0, P)).then_inc(sem("rows_full"), 16)
            pool.dma_start(sinkb, wide(A["attn_sinks"][0:1, :], 0, P)).then_inc(sem("rows_full"), 16)
            for b in range(NB):
                pool.dma_start(sink64[HEADS * b:HEADS * (b + 1), :],
                               A["attn_sinks"].rearrange("a h -> h a")).then_inc(sem("rows_full"), 16)
            pool.dma_start(brout[0:E, :], A["b_router"].rearrange("a e -> e a")).then_inc(sem("rows_full"), 16)
            for src, dst in (("cache_k_win", "kws"), ("cache_v_win", "vws")):
                pool.dma_start(O[dst][0, :, 0:WIN - 1].rearrange("b s g d -> b (s g d)"),
                               A[src][0, :, 1:WIN].rearrange("b s g d -> b (s g d)")).then_inc(sem("stored"), 16)
            pool.dma_start(list_dram.rearrange("(p n) a -> p (n a)", p=P), zeros[:, :]).then_inc(sem("list_cleared"), 16)
            pool.wait_ge(sem("z_dec_copied"), NZ)
            for j in range(4):
                pool.dma_start(zs[0:NB, P * j:P * (j + 1)], zq[32 * j:32 * j + NB, 0:KV, :]).then_inc(sem("zs_full"), 16)
                pool.dma_start(zs[0:NB, :].rearrange("p (c j n) -> p c j n", c=NZ, j=4)[:, KV:, j, :],
                               zq[32 * j:32 * j + NB, KV:, :]).then_inc(sem("zs_full"), 16)
            pool.wait_ge(sem("rotated"), 1)
            pool.dma_start(O["kwp"][0, 0].rearrange("s g d -> s (g d)"), z[:, 1, K0:K0 + P]).then_inc(sem("stored"), 16)
            pool.dma_start(O["vwp"][0, 0].rearrange("s g d -> s (g d)"), z[:, 1, V0:V0 + P]).then_inc(sem("stored"), 16)
            pool.wait_ge(sem("rotated"), 2)
            pool.dma_start(O["kws"][0, :, WIN - 1].rearrange("b g d -> b (g d)"), zs[0:NB, K0:K0 + P]).then_inc(sem("stored"), 16)
            pool.dma_start(O["vws"][0, :, WIN - 1].rearrange("b g d -> b (g d)"), zs[0:NB, V0:V0 + P]).then_inc(sem("stored"), 16)
            pool.wait_ge(sem("att_summed"), 2)
            pool.dma_start(kc, A["cache_k_win"][0].rearrange("b s g d -> s b (g d)")).then_inc(sem("keys_full"), 16)
            for b in range(NB):
                pool.dma_start(states[:, b], A["state_hgrn"][0, b].rearrange("h k v -> k h v")).then_inc(sem("states_full"), 16)
            pool.wait_ge(sem("mod_ready"), 3)
            pool.dma_start(vc, A["cache_v_win"][0].rearrange("b s g d -> s b (g d)")).then_inc(sem("cache_full"), 16)
            pool.wait_ge(sem("stored"), 16 * 6)
            pool.wait_ge(sem("mod_stored"), 64)
            pool.wait_ge(sem("cat_ready"), 2)
            pool.dma_start(rows1, wide(mod_dram[0, 0:1, :], 0, P)).then_inc(sem("mod_rows_full"), 16)
            pool.dma_start(scale2, wide(mod_dram[1, 0:1, 0:D], 0, P)).then_inc(sem("mod_rows_full"), 16)
            pool.dma_start(wr, A["w_router"][0].rearrange("(k p) e -> p k e", p=P)).then_inc(sem("router_full"), 16)
            pool.wait_ge(sem("state_final"), HH)
            pool.dma_start(O["hgp"][0, 0].rearrange("h k v -> k h v"), st.rearrange("p (h v) -> p h v", h=HH)).then_inc(sem("stored"), 16)
            pool.wait_ge(sem("states_new"), NB * HH)
            for b in range(NB):
                pool.dma_start(O["hgs"][0, b].rearrange("h k v -> k h v"), states[:, b]).then_inc(sem("stored"), 16)
            pool.wait_ge(sem("cat_ready"), 3)
            pool.wait_ge(sem("stored"), 16 * N_STORED)
            pool.dma_start(rows1s[0:NB, :], mod_dram[0, 1:1 + NB, :]).then_inc(sem("mod_rows_s_full"), 16)
            pool.dma_start(rows2s[0:NB, :], mod_dram[1, 1:1 + NB, :]).then_inc(sem("mod_rows_s_full"), 16)
            pool.dma_start(gate2, wide(mod_dram[1, 0:1, D:2 * D], 0, P)).then_inc(sem("mod_rows_s_full"), 16)
            pool.wait_ge(sem("stored"), 16 * N_STORED)
            pool.dma_start(g_fin, wide(A["g_final"].rearrange("(a n) -> a n", a=1), 0, P)).then_inc(sem("mod_rows_s_full"), 16)
            pool.wait_ge(sem("list_cleared"), 16)
            for t in range(3):
                pool.wait_ge(sem("slots_ready"), 1 + t // 2)
                for k in range(TOPK):
                    pool.indirect_dma_start(
                        out=list_dram, out_offset=bass.IndirectOffsetOnAxis(ap=slot_u[0:NT[t], t, k:k + 1], axis=0),
                        in_=tok_i[0:NT[t], t:t + 1], in_offset=None).then_inc(sem("list_full"), 16)
            pool.wait_ge(sem("npass_ready"), 1)
            passes = pool.value_load(npass[0:1, 0:1], min_val=1, max_val=MAXPASS)
            pool.wait_ge(sem("list_full"), 16 * 3 * TOPK)
            pool.wait_ge(sem("h2_stored"), 48)
            with pool.Fori(0, passes) as p:
                with pool.Fori(0, PAIRS) as i:
                    it = pool.snap(p * PAIRS + i)
                    pool.wait_ge(sem("xT_made"), it * 2 + 1)
                    pool.dma_start(idx[:, :], list_dram[bass.ds(it * P, P), :]).then_inc(sem("idx_full"), 16)
                    pool.wait_ge(sem("idx_full"), it * 16 + 16)
                    pool.nop(nofuse=True)
                    pool.indirect_dma_start(
                        out=xg, out_offset=None, in_=h2_dram,
                        in_offset=bass.IndirectOffsetOnAxis(ap=idx[:, 0:1].bitcast(U32), axis=0)).then_inc(sem("x_full"), 16)
                    row = pool.snap(i * 2)
                    pool.wait_ge(sem("bias_cleared"), 2)
                    for e in range(2):
                        pool.wait_ge(sem(f"bias_used{e}"), it + 1)
                        pool.dma_start(bias[e][0:1, 0:FF2],
                                       A["b_up"][0][bass.ds(row + e, 1), :]).then_inc(sem(f"bias_full{e}"), 16)
                        pool.dma_start(bias[e][0:1, FF2:FF2 + D],
                                       A["b_down"][0][bass.ds(row + e, 1), :]).then_inc(sem(f"bias_full{e}"), 16)
                pool.wait_ge(sem("slots_ready"), 4)
                for e in range(2):
                    pool.wait_ge(sem(f"y_stored{e}"), (p + 1) * (32 * PAIRS) + 1)
                with pool.If(p < passes - 1):
                    for n in range(3 * TOPK):
                        t, k = divmod(n, TOPK)
                        pool.wait_ge(sem("y_added"), p * (3 * TOPK) + n + 1)
                        pool.nop(nofuse=True)
                        pool.indirect_dma_start(
                            out=xg[0:NT[t], :], out_offset=None, in_=y_dram,
                            in_offset=bass.IndirectOffsetOnAxis(ap=row_u[0:NT[t], t, k:k + 1], axis=0)).then_inc(sem("y_part"), 16)
                    pool.wait_ge(sem("y_added"), (p + 1) * (3 * TOPK) + 1)
            total = pool.snap(passes * PAIRS)
            pool.wait_ge(chunks_used, total * PER + PRE)
            pool.nop(nofuse=True)
            for t in range(3):
                for k in range(TOPK):
                    pool.indirect_dma_start(
                        out=yk[t][k][0:NT[t], :], out_offset=None, in_=y_dram,
                        in_offset=bass.IndirectOffsetOnAxis(ap=row_u[0:NT[t], t, k:k + 1], axis=0)).then_inc(y_full(t, k), 16)

        @block.scalar
        def _(act):
            act.dma_start(crow[0:1, :], A["c_prompt"]).then_inc(sem("c_full"), 16)
            act.dma_start(crow[1:9, :], A["c_sample"]).then_inc(sem("c_full"), 16)
            act.dma_start(const[:, :], A["const"]).then_inc(sem("const_full"), 16)
            act.dma_start(x[:, 0, :], A["x_prompt"][0, 0:P]).then_inc(sem("x_full_in"), 16)
            act.dma_start(x[:, 1, :], A["x_prompt"][0, P:S]).then_inc(sem("x_full_in"), 16)
            act.dma_start(x[0:NB, 2, :], A["x_sample"].rearrange("b s d -> (b s) d")).then_inc(sem("x_full_in"), 16)
            act.wait_ge(sem("c_full"), 32)
            act.activation(crow[0:9, :], crow[0:9, :], ACT.Silu).then_inc(sem("c_silu"), 1)

            def squares(t):
                act.activation(h[0:NT[t], t, :], x[0:NT[t], t, :], ACT.Square,
                               accum_out=ssum3[0:NT[t], t:t + 1]).then_inc(sem("sums"), 1)

            def root(t):
                act.activation(root3[0:NT[t], t:t + 1], ssum3[0:NT[t], t:t + 1], ACT.Sqrt).then_inc(sem("roots"), 1)

            def store_h2(t):
                act.wait_ge(sem("h2_ready"), t + 1)
                act.dma_start(h2_dram[P * t:P * t + NT[t], :], h[0:NT[t], t, :]).then_inc(sem("h2_stored"), 16)

            act.wait_ge(sem("x_full_in"), 48)
            for t in range(3):
                squares(t)
            act.wait_ge(sem("means"), 3)
            for t in range(3):
                root(t)

            def even_tiles(made, copied):
                for k in range(0, KT, 2):
                    act.wait_ge(sem(made), k + 1)
                    act.activation(hT[:, k, 0:NTOK], B[k][:, 0:NTOK], ACT.Copy).then_inc(sem(copied), 1)

            act.wait_ge(sem("mod_ready"), 1)
            for j in range(4):
                act.dma_start(rows0s[0:NB, 512 * j:512 * (j + 1)], mods[32 * j + 1:32 * j + 1 + NB, 0, :]).then_inc(sem("mod_rows0_full"), 16)
            even_tiles("hT_made", "hT_copied_a")
            act.wait_ge(sem("lb_less_max"), 2)
            act.activation(lbl[:, :, :], lbl[:, :, :], ACT.Exp).then_inc(sem("lb_exp"), 1)
            for c in range(NZ):
                act.wait_ge(sem("z_made"), c + 1)
                src = B[c % 4][:, :].rearrange("p (t n) -> p t n", t=2)
                if c < KV:
                    for t in range(2):
                        done = act.activation(z[:, t, 0:AW].rearrange("p (j g d) -> p g j d", g=KV, j=GRP)[:, c],
                                              src[:, t, :].rearrange("p (j d) -> p j d", j=GRP), ACT.Copy)
                else:
                    done = act.activation(z[:, :, c * ZC:(c + 1) * ZC], src, ACT.Copy)
                done.then_inc(sem("z_copied"), 1)
            act.wait_ge(sem("z_copied"), NZ)
            act.activation(z[:, :, F0:F0 + HW_], z[:, :, F0:F0 + HW_], ACT.Sigmoid).then_inc(sem("f_sig"), 1)
            act.wait_ge(sem("qk_made"), 3)
            act.activation(qT[:, :, 0:P], B[0][:, :].rearrange("p (j t) -> p j t", j=4), ACT.Copy).then_inc(sem("qk_copied"), 1)
            act.activation(qT[:, :, P:S], B[1][:, :].rearrange("p (j t) -> p j t", j=4), ACT.Copy).then_inc(sem("qk_copied"), 1)
            act.activation(kT, B[2][:, 0:S], ACT.Copy).then_inc(sem("qk_copied"), 1)
            act.activation(z[:, :, G0:G0 + HW_], z[:, :, G0:G0 + HW_], ACT.Silu).then_inc(sem("g_silu"), 1)
            act.wait_ge(sem("zs_full"), 128)
            act.activation(zs[0:NB, F0:F0 + HW_], zs[0:NB, F0:F0 + HW_], ACT.Sigmoid).then_inc(sem("f_sig"), 1)
            act.activation(zs[0:NB, G0:G0 + HW_], zs[0:NB, G0:G0 + HW_], ACT.Silu).then_inc(sem("g_silu"), 1)
            act.wait_ge(sem("f_ready"), 1)
            act.activation(logf, z[:, :, F0:F0 + HW_], ACT.Ln).then_inc(sem("logf_ready"), 1)
            for n, t in enumerate((1, 0)):
                act.wait_ge(sem("max_ready"), n + 1)
                w = P * (t + 1)
                for hd in range(HEADS):
                    act.activation(sc[:, hd * w:(hd + 1) * w], sc[:, hd * w:(hd + 1) * w], ACT.Exp,
                                   bias=nmax[:, t, hd:hd + 1], accum_out=psums[:, t, hd:hd + 1]).then_inc(sem("probs"), 1)
                act.activation(esink[:, t, :], dsink[:, t, :], ACT.Exp).then_inc(sem("esink_ready"), 1)
                for i in range(2 * (t + 1)):
                    act.wait_ge(sem("pT_made"), 4 * n + i + 1)
                    if n and i == 0:
                        act.wait_ge(sem("pv_made"), 1)
                    act.activation(pT[:, 4 * i:4 * i + 4, :], B[3 + i][:, :].rearrange("p (n q) -> p n q", n=4),
                                   ACT.Copy).then_inc(sem("pT_copied"), 1)
            for n, t in enumerate((1, 0)):
                act.wait_ge(sem("att_summed"), n + 1)
                act.activation(z[:, t, 0:AW], h[:, t, 0:AW], ACT.Square, accum_out=gmean[:, t:t + 1]).then_inc(sem("gsums"), 1)

            def hgrn_squares(t):
                act.wait_ge(sem("hgo_made"), t + 1)
                for hd in range(HH):
                    act.activation(z[:, t, Q0 + P * hd:Q0 + P * (hd + 1)], B[6 + t][:, P * hd:P * (hd + 1)], ACT.Square,
                                   accum_out=gmean[:, 2 + 4 * t + hd:3 + 4 * t + hd]).then_inc(sem("gsums"), 1)

            for t in range(2):
                act.wait_ge(sem("hg_made"), 4 * t + 4)
                if t:
                    act.wait_ge(sem("G_made"), 8)
                    act.wait_ge(sem("lev_ready"), 7)
                act.activation(bT, B[0][:, :], ACT.Copy).then_inc(sem("hg_copied"), 1)
                act.activation(kkT, B[1][:, :], ACT.Copy).then_inc(sem("hg_copied"), 1)
                act.activation(qqT, B[2][:, :], ACT.Copy).then_inc(sem("hg_copied"), 1)
                if t:
                    act.wait_ge(sem("st_made"), 1)
                act.activation(ks, B[3][:, :], ACT.Exp).then_inc(sem("tail_exp"), 1)
                for n in range(7):
                    act.wait_ge(sem("lev_diff"), 14 * t + 2 * n + 2)
                    act.activation(lev[n % 3], lev[n % 3], ACT.Exp).then_inc(sem("lev_exp"), 1)
                    if t and n == 3:
                        hgrn_squares(0)
                if t:
                    act.wait_ge(sem("G_made"), 16)
                    act.wait_ge(sem("hg_copied"), 6)
                    act.activation(lev[0], bT, ACT.Exp).then_inc(sem("b_exp"), 1)
                    act.activation(eb, bT.rearrange("p (h t) -> p h t", h=HH)[:, :, P - 1], ACT.Exp).then_inc(sem("b_exp"), 1)
            hgrn_squares(1)
            act.wait_ge(sem("mod_ready"), 3)
            for j in range(4):
                act.dma_start(mod_dram[:, :, 512 * j:512 * (j + 1)].rearrange("q r n -> r q n"),
                              mods[32 * j:32 * j + 1 + NB, 1:3, :]).then_inc(sem("mod_stored"), 16)
            act.wait_ge(sem("gmeans"), 1)
            act.activation(groot[:, 0:10], gmean[:, 0:10], ACT.Sqrt).then_inc(sem("groots"), 1)
            act.wait_ge(sem("smax_ready"), 1)
            act.activation(ps[0:64, :], ps[0:64, :], ACT.Exp, bias=snm[0:64, :], accum_out=ssm[0:64, :]).then_inc(sem("sprobs"), 1)
            act.activation(sesk[0:64, :], snm[0:64, :], ACT.Exp, bias=sink64[0:64, :]).then_inc(sem("sprobs"), 1)
            for i in (0, 2):
                act.wait_ge(sem("catT_made"), i + 1)
                act.activation(hT[:, 2 * i:2 * i + 2, 0:S], B[4 + i][:, :].rearrange("p (k t) -> p k t", k=2),
                               ACT.Copy).then_inc(sem("catT_copied_a"), 1)
            act.wait_ge(sem("spv_made"), 2)
            act.activation(pv[0:64, :], B[4][0:64, 0:P], ACT.Copy).then_inc(sem("pv_copied"), 1)
            act.wait_ge(sem("o64_ready"), 1)
            act.dma_start(h[0:NB, 2, 0:AW], o64[0:64, :]).then_inc(sem("o64_moved"), 16)
            for t in range(2):
                act.wait_ge(sem("x1_ready"), t + 1)
                squares(t)
            act.wait_ge(sem("means"), 5)
            for t in range(2):
                root(t)
            for t in range(2):
                store_h2(t)
            def copy_h2T(i):
                act.wait_ge(sem("h2T_made"), i + 1)
                act.activation(hT[:, 2 * i:2 * i + 2, 0:S], B[i][:, :].rearrange("p (k t) -> p k t", k=2),
                               ACT.Copy).then_inc(sem("h2T_copied_a"), 1)

            copy_h2T(0)
            act.wait_ge(sem("gmeans"), 2)
            act.activation(groot[0:NB, 10:15], gmean[0:NB, 10:15], ACT.Sqrt).then_inc(sem("groots"), 1)
            copy_h2T(2)
            act.wait_ge(sem("wo_dec_copied"), 1)
            for j in range(4):
                act.dma_start(tmps[0:NB, 256 * j:256 * (j + 1)], zq[32 * j:32 * j + NB, 0:4, :]).then_inc(sem("wo_dec_full"), 16)
            act.wait_ge(sem("x1_ready"), 3)
            squares(2)
            act.wait_ge(sem("means"), 6)
            root(2)
            store_h2(2)
            for t in range(3):
                r = slice(0, NT[t])
                act.wait_ge(sem("top_ready"), 1 + t // 2)
                act.activation(topw[r, t, :], top8[r, t, 0:TOPK], ACT.Exp, bias=ntop[r, t:t + 1],
                               accum_out=tsum[r, t:t + 1]).then_inc(sem("top_exp"), 1)

            def store(e, it, i):
                act.wait_ge(sem(f"y_stored{e}"), it * 32 + 1)
                act.wait_ge(chunks_used, it * PER + (PRE + 20 + 4 * e))
                act.activation(ysb[e], B[4 + e][:, :], ACT.Copy).then_inc(sem(f"y_copied{e}"), 1)
                act.wait_ge(sem(f"y_copied{e}"), it + 2)
                for a in range(2):
                    act.dma_start(y_dram[bass.ds(i * P + 64 * e, SLOTS), 512 * a:512 * (a + 1)],
                                  ysb[e][64 * a:64 * (a + 1), :]).then_inc(sem(f"y_stored{e}"), 16)

            act.wait_ge(sem("stored"), 16 * N_STORED)
            act.wait_ge(sem("npass_ready"), 1)
            passes = act.value_load(npass[0:1, 0:1], min_val=1, max_val=MAXPASS)
            count_from_one(act, "y_copied0", "y_copied1", "y_stored0", "y_stored1", "gT_copied")
            with act.Fori(0, passes) as p:
                act.wait_ge(sem("y_added"), p * (3 * TOPK) + 1)
                with act.Fori(0, PAIRS) as i:
                    it = act.snap(p * PAIRS + i)
                    act.wait_ge(sem("xT_made"), it * 2 + 3)
                    act.activation(xT[:, 4:8, :], B[7][:, :].rearrange("p (k t) -> p k t", k=4), ACT.Copy).then_inc(sem("xT_copied_a"), 1)
                    for e in range(2):
                        act.wait_ge(sem("glu_ready"), it * 2 + (e + 1))
                        act.activation(sg, glu, ACT.Sigmoid, scale=ALPHA).then_inc(sem("sig_ready"), 1)
                        act.wait_ge(sem("gT_made"), it * 2 + (e + 2))
                        act.activation(gT[e], B[6 + e][:, :], ACT.Copy).then_inc(sem("gT_copied"), 1)
                        if e:
                            store(0, it, i)
                    store(1, it, i)
            for n, t in enumerate(LAST):
                act.wait_ge(sem("x2_ready"), n + 1)
                act.activation(moe[0:NT[t], t, :], x[0:NT[t], t, :], ACT.Square,
                               accum_out=ssum3[0:NT[t], t:t + 1]).then_inc(sem("sums"), 1)
                act.wait_ge(sem("means"), 6 + n + 1)
                root(t)

        @block.tensor
        def _(pe):
            def landed(n):
                pe.wait_ge(full[place(n)], 16 * loads(n))

            def turn(out, in_, rows):
                return pe.transpose(out, in_, ident[0:rows, 0:rows])

            def pick_rows(out, j):
                return pe.matmul(out, lhsT=C("pick", slice(32 * j, 32 * j + 32)), rhs=mods[32 * j:32 * j + 32, 0, :],
                                 start=True, stop=True)

            def transpose_tiles(src, made):
                for k in range(KT):
                    for t in range(3):
                        mm = turn(B[k][:, P * t:P * t + NT[t]], src[0:NT[t], t, P * k:P * (k + 1)], NT[t])
                    mm.then_inc(sem(made), 1)

            def modulation(first, k, bank):
                landed(first + k)
                for j in range(4):
                    mm = pe.matmul(bank[32 * j:32 * j + 32, :], lhsT=scT[:, k, :], rhs=chunk(first + k)[:, 512 * j:512 * (j + 1)],
                                   start=(k == 0), stop=(k == N_ADA - 1), skip_group_check=True)
                mm.then_inc(chunks_used, 1)

            pe.wait_ge(sem("const_full"), 16)
            pe.wait_ge(sem("c_silu"), 1)
            for k in range(KT):
                mm = turn(B[0][:, 16 * k:16 * k + 9], crow[0:9, P * k:P * (k + 1)], 9)
            mm.then_inc(sem("adaln_made"), 1)
            pe.wait_ge(sem("scT_ready"), 1)
            for k in range(N_ADA):
                modulation(0, k, B[1])
            pe.wait_ge(sem("mod_ready"), 1)
            for n in range(2):
                pick_rows(B[2 + n][:, :], 2 + n)
                mm = pick_rows(B[4 + n][:, :], n)
            mm.then_inc(sem("adaln_made"), 1)
            pe.wait_ge(sem("h_ready"), 3)
            transpose_tiles(h, "hT_made")
            pe.wait_ge(sem("hT_copied_a"), 4)
            pe.wait_ge(sem("hT_copied_d"), 4)
            for c in range(NZ):
                n = Z0 + c
                w = chunk(n).rearrange("p (k n) -> p k n", k=KT)
                landed(n)
                if c >= 4:
                    pe.wait_ge(sem("z_copied"), c - 3)
                for t in range(2):
                    for k in range(KT):
                        mm = pe.matmul(B[c % 4][:, ZC * t:ZC * (t + 1)], lhsT=hT[:, k, P * t:P * (t + 1)], rhs=w[:, k, :],
                                       start=(k == 0), stop=(k == KT - 1))
                mm.then_inc(sem("z_made"), 1)
                if c >= 2:
                    pe.wait_ge(sem("z_dec_copied"), c - 1)
                for k in range(KT):
                    for j in range(4):
                        mm = pe.matmul(B[4 + c % 2][32 * j:32 * j + 32, 0:64], lhsT=hT[:, k, S:S + 32], rhs=w[:, k, 64 * j:64 * (j + 1)],
                                       start=(k == 0), stop=(k == KT - 1), skip_group_check=True)
                mm.then_inc(chunks_used, 1)
            pe.wait_ge(sem("z_copied"), NZ)
            pe.wait_ge(sem("rotated"), 1)
            for t in range(2):
                for j in range(GRP):
                    mm = turn(B[t][:, P * j:P * (j + 1)], z[:, t, P * j:P * (j + 1)], P)
                mm.then_inc(sem("qk_made"), 1)
            for t in range(2):
                mm = turn(B[2][:, P * t:P * (t + 1)], z[:, t, K0:K0 + P], P)
            mm.then_inc(sem("qk_made"), 1)
            pe.wait_ge(sem("qk_copied"), 3)
            pe.wait_ge(sem("z_dec_copied"), NZ)
            for jj in range(2):
                for g in range(KV):
                    for j in (2 * jj, 2 * jj + 1):
                        mm = pe.matmul(B[3 + 2 * g + jj][:, 256 * (j % 2):256 * (j % 2 + 1)],
                                       lhsT=qT[64 * g:64 * g + 64, j, P:S], rhs=kT[64 * g:64 * g + 64, :], start=True, stop=True)
                    mm.then_inc(sem("sc_made"), 1)
            for g in range(KV):
                for j in range(GRP):
                    mm = pe.matmul(B[(7 + g) % 8][:, P * j:P * (j + 1)],
                                   lhsT=qT[64 * g:64 * g + 64, j, 0:P], rhs=kT[64 * g:64 * g + 64, 0:P], start=True, stop=True)
                mm.then_inc(sem("sc_made"), 1)
            for n, t in enumerate((1, 0)):
                nb = t + 1
                for i in range(2 * nb):
                    per = 4 // nb
                    pe.wait_ge(sem("probs"), 8 * n + per * (i + 1))
                    if n:
                        pe.wait_ge(sem("pT_copied"), i + 1)
                    for u in range(4):
                        m = 4 * i + u
                        mm = turn(B[3 + i][:, P * u:P * (u + 1)], sc[:, P * m:P * (m + 1)], P)
                    mm.then_inc(sem("pT_made"), 1)
                pe.wait_ge(sem("pT_copied"), 4 * n + 2 * nb)
                for hd in range(HEADS):
                    g = hd // GRP
                    for s in range(nb):
                        mm = pe.matmul(B[1 + n][:, HD * hd:HD * (hd + 1)], lhsT=pT[:, nb * hd + s, :],
                                       rhs=z[:, s, V0 + HD * g:V0 + HD * (g + 1)], start=(s == 0), stop=(s == nb - 1))
                mm.then_inc(sem("pv_made"), 1)
            pe.wait_ge(sem("k_ready"), 1)
            for t in range(2):
                if t == 0:
                    pe.wait_ge(sem("att_summed"), 2)
                    pe.wait_ge(sem("masked"), 6)
                else:
                    pe.wait_ge(sem("hg_copied"), 3)
                    pe.wait_ge(sem("st_copied"), 1)
                for hd in range(HH):
                    c = slice(P * hd, P * (hd + 1))
                    mm = pe.matmul(B[0][:, c], lhsT=logf[:, t, c], rhs=C("incl"), start=True, stop=True)
                mm.then_inc(sem("hg_made"), 1)
                for hd in range(HH):
                    mm = turn(B[1][:, P * hd:P * (hd + 1)], z[:, t, F0 + P * hd:F0 + P * (hd + 1)], P)
                mm.then_inc(sem("hg_made"), 1)
                for hd in range(HH):
                    mm = turn(B[2][:, P * hd:P * (hd + 1)], z[:, t, Q0 + P * hd:Q0 + P * (hd + 1)], P)
                mm.then_inc(sem("hg_made"), 1)
                pe.matmul(B[3][:, :], lhsT=C("after"), rhs=logf[:, t, :], start=True, stop=True).then_inc(sem("hg_made"), 1)
                pe.wait_ge(sem("hg_copied"), 3 * t + 3)
                for n in range(8):
                    g = 8 * t + n
                    if n:
                        pe.wait_ge(sem("lev_ready"), 7 * t + n)
                    if g >= 2:
                        pe.wait_ge(sem("lev_masked"), g - 1)
                    for hd in range(HH):
                        c = slice(P * hd, P * (hd + 1))
                        left = kkT if n == 0 else lev[(n - 1) % 3]
                        right = qqT if n == 0 else lev[(n - 1) % 3]
                        mm = pe.matmul(B[4 + n % 2][:, c], lhsT=left[:, c], rhs=right[:, c], start=True, stop=True)
                    mm.then_inc(sem("G_made"), 1)
                    modulation((ADA1, ADA2)[t], n, B[(7, 2)[t]])
                pe.wait_ge(sem("ks_ready"), t + 1)
                for hd in range(HH):
                    c = slice(P * hd, P * (hd + 1))
                    mm = pe.matmul(B[3][:, c], lhsT=ks[:, c], rhs=z[:, t, I0 + P * hd:I0 + P * (hd + 1)], start=True, stop=True)
                mm.then_inc(sem("st_made"), 1)
                pe.wait_ge(sem("lev_masked"), 8 * t + 8)
                if t:
                    pe.wait_ge(sem("dec_operand"), 1)
                    pe.wait_ge(sem("mod_ready"), 2)
                for hd in range(HH):
                    c = slice(P * hd, P * (hd + 1))
                    mm = pe.matmul(B[6 + t][:, c], lhsT=amat[:, hd, :], rhs=z[:, t, I0 + P * hd:I0 + P * (hd + 1)],
                                   start=True, stop=(t == 0))
                    if t:
                        mm = pe.matmul(B[6 + t][:, c], lhsT=lev[0][:, c], rhs=st[:, c], start=False, stop=True)
                mm.then_inc(sem("hgo_made"), 1)
            pe.wait_ge(sem("keys_full"), 16)
            pe.wait_ge(sem("hg_copied"), 6)
            for b in range(NB):
                mm = turn(B[b // 4][:, P * (b % 4):P * (b % 4 + 1)], kc[:, b, :], P)
                if b % 4 == 3:
                    mm.then_inc(sem("kcT_made"), 1)
            pe.wait_ge(sem("rotated"), 2)
            pe.wait_ge(sem("mod_ready"), 3)
            turn(B[2][:, 0:NB], zs[0:NB, K0:K0 + P], NB)
            for j in range(GRP):
                mm = turn(B[2][:, 16 + 8 * j:24 + 8 * j], zs[0:NB, P * j:P * (j + 1)], NB)
            mm.then_inc(sem("snew_made"), 1)
            pe.wait_ge(sem("kcT_copied"), 2)
            pe.wait_ge(sem("snew_copied"), 3)
            pe.wait_ge(sem("state_final"), HH)
            for b in range(NB):
                mm = pe.matmul(B[3][0:64, 0:129], lhsT=qbd[:, 64 * b:64 * b + 64], rhs=kcT[:, b, :], start=(b == 0), stop=(b == NB - 1))
            mm.then_inc(sem("ss_made"), 1)
            pe.wait_ge(sem("k_ready"), 2)
            for hd in range(HH):
                turn(B[0][:, NB * hd:NB * (hd + 1)], zs[0:NB, Q0 + P * hd:Q0 + P * (hd + 1)], NB)
                mm = turn(B[0][:, 32 + NB * hd:32 + NB * (hd + 1)], zs[0:NB, F0 + P * hd:F0 + P * (hd + 1)], NB)
            mm.then_inc(sem("sqf_made"), 1)
            pe.wait_ge(sem("cat_ready"), 2)
            for k in range(KT):
                for t in range(2):
                    mm = turn(B[4 + k // 2][:, S * (k % 2) + P * t:S * (k % 2) + P * (t + 1)], h[:, t, P * k:P * (k + 1)], P)
                if k % 2:
                    mm.then_inc(sem("catT_made"), 1)

            def project_prompt(k):
                landed(WO0 + k // 2)
                for t in range(2):
                    for a in range(2):
                        mm = pe.matmul(B[2 * t + a][:, :], lhsT=hT[:, k, P * t:P * (t + 1)],
                                       rhs=two(chunk(WO0 + k // 2))[:, k % 2, 512 * a:512 * (a + 1)],
                                       start=(k == 0), stop=(k == KT - 1))
                return mm

            pe.wait_ge(sem("catT_copied_a"), 2)
            pe.wait_ge(sem("catT_copied_d"), 2)
            pe.wait_ge(sem("smax_ready"), 1)
            pe.wait_ge(sem("km_ready"), 1)
            project_prompt(0)
            pe.wait_ge(sem("sprobs"), 1)
            turn(B[5][:, 0:64], ps[0:64, 0:P], 64).then_inc(sem("spT_made"), 1)
            project_prompt(1)
            pe.wait_ge(sem("dec_operand"), 2)
            pe.wait_ge(sem("cache_full"), 16)
            for b in range(NB):
                mm = pe.matmul(B[4][0:64, 0:P], lhsT=pbd[:, 64 * b:64 * b + 64], rhs=vc[:, b, :], start=(b == 0), stop=(b == NB - 1))
            mm.then_inc(sem("spv_made"), 1)
            pe.matmul(B[5][0:64, 0:P], lhsT=C("spread", slice(0, NB)), rhs=zs[0:NB, V0:V0 + P], start=True, stop=True).then_inc(sem("spv_made"), 1)
            for b in range(NB):
                if b % 2 == 0:
                    project_prompt(2 + b // 2)
                pe.wait_ge(sem("km_ready"), b + 1)
                if b >= 2:
                    pe.wait_ge(sem("states_new"), HH * (b - 1))
                for hd in range(HH):
                    c = slice(P * hd, P * (hd + 1))
                    mm = pe.matmul(B[6 + b % 2][:, c], lhsT=km[b % 2][0:NB, c], rhs=zs[0:NB, I0 + P * hd:I0 + P * (hd + 1)], start=True, stop=True)
                mm.then_inc(sem("outer_made"), 1)
            project_prompt(6)
            project_prompt(7).then_inc(sem("wo_made"), 1)
            pe.wait_ge(sem("states_new"), HH * NB)
            pe.wait_ge(sem("pv_copied"), 1)
            for b in range(NB):
                for hd in range(HH):
                    col = NB * hd + b
                    mm = pe.matmul(B[4][:, col:col + 1], lhsT=states[:, b, hd, :], rhs=sq[:, col:col + 1], start=True, stop=True)
            mm.then_inc(sem("soT_made"), 1)
            pe.wait_ge(sem("soT_copied"), 1)
            for hd in range(HH):
                mm = turn(B[6][0:NB, P * hd:P * (hd + 1)], soT[:, NB * hd:NB * (hd + 1)], P)
            mm.then_inc(sem("so_made"), 1)
            pe.wait_ge(sem("h2_ready"), 2)
            for k in range(KT):
                for t in range(2):
                    mm = turn(B[k // 2][:, S * (k % 2) + P * t:S * (k % 2) + P * (t + 1)], h[:, t, P * k:P * (k + 1)], P)
                if k % 2:
                    mm.then_inc(sem("h2T_made"), 1)

            def router(out, cols):
                for k in range(KT):
                    mm = pe.matmul(out, lhsT=wr[:, k, :], rhs=hT[:, k, cols], start=(k == 0), stop=(k == KT - 1))
                mm.then_inc(sem("lgT_made"), 1)

            def rank(out, t):
                for u in range(t + 1):
                    mm = pe.matmul(out, lhsT=C("before" if u == t else "ones", slice(0, NT[u]))[:, 0:NT[t]],
                                   rhs=chosen[0:NT[u], u, :], start=(u == 0), stop=(u == t))
                return mm

            pe.wait_ge(sem("h2T_copied_a"), 2)
            pe.wait_ge(sem("h2T_copied_d"), 2)
            pe.wait_ge(sem("router_full"), 16)
            router(B[4][0:E, 0:S], slice(0, S))
            pe.wait_ge(sem("cat_ready"), 3)
            for k in range(KT):
                mm = turn(B[7][:, NB * k:NB * (k + 1)], h[0:NB, 2, P * k:P * (k + 1)], NB)
            mm.then_inc(sem("catT_made"), 1)
            pe.wait_ge(sem("lgT_ready"), 1)
            for t in range(2):
                mm = turn(B[0][:, E * t:E * (t + 1)], lgT[0:E, P * t:P * (t + 1)], E)
            mm.then_inc(sem("lg_made"), 1)
            pe.wait_ge(sem("catT_copied_d"), 3)
            for k in range(KT):
                n = WO0 + k // 2
                for j in range(4):
                    mm = pe.matmul(B[5][32 * j:32 * j + 32, 0:256], lhsT=hT[:, k, S:S + 32],
                                   rhs=two(chunk(n))[:, k % 2, 256 * j:256 * (j + 1)],
                                   start=(k == 0), stop=(k == KT - 1), skip_group_check=True)
                if k % 2:
                    mm.then_inc(chunks_used, 1)
            pe.wait_ge(sem("chosen_ready"), 1)
            for t in range(2):
                mm = rank(B[1][:, E * t:E * (t + 1)], t)
            mm.then_inc(sem("rank_made"), 1)
            pe.wait_ge(sem("h2_ready"), 3)
            for k in range(KT):
                mm = turn(B[7][:, NB * k:NB * (k + 1)], h[0:NB, 2, P * k:P * (k + 1)], NB)
            mm.then_inc(sem("h2T_made"), 1)
            pe.wait_ge(sem("h2T_copied_d"), 3)
            router(B[2][0:E, 0:NB], slice(S, NTOK))
            pe.wait_ge(sem("lgT_ready"), 2)
            turn(B[3][0:NB, 0:E], lgT[0:E, S:NTOK], E).then_inc(sem("lg_made"), 1)
            pe.wait_ge(sem("chosen_ready"), 2)
            rank(B[6][0:NB, 0:E], 2)
            for u in range(3):
                mm = pe.matmul(B[0][0:1, 0:E], lhsT=C("ones", slice(0, NT[u]))[:, 0:1], rhs=chosen[0:NT[u], u, :], start=(u == 0), stop=(u == 2))
            mm.then_inc(sem("rank_made"), 1)

            pe.wait_ge(sem("npass_ready"), 1)
            pe.wait_ge(sem("bias_cleared"), 2)
            passes = pe.value_load(npass[0:1, 0:1], min_val=1, max_val=MAXPASS)
            total = pe.snap(passes * PAIRS)
            one = C("bias_row")
            count_from_one(pe, "xT_made", "gT_made", "bias_used0", "bias_used1")
            with pe.Fori(0, total) as it:
                def chunk_landed(n):
                    pe.wait_ge(full[place(n)], it * (16 * PER // RING2) + 16 * loads(n))

                def turn_g(e):
                    pe.wait_ge(sem("g_ready"), it * 2 + (e + 2))
                    for j in range(4):
                        mm = turn(B[6 + e][:, P * j:P * (j + 1)], gg[e][:, P * j:P * (j + 1)], P)
                    mm.then_inc(sem("gT_made"), 1)

                pe.wait_ge(sem("x_full"), it * 16 + 16)
                pe.wait_ge(sem("gT_copied"), it * 2 + 1)
                for k in range(KT):
                    mm = turn(B[6 + k // 4][:, P * (k % 4):P * (k % 4 + 1)], xg[:, P * k:P * (k + 1)], P)
                    if k % 4 == 3:
                        mm.then_inc(sem("xT_made"), 1)
                for e in range(2):
                    pe.wait_ge(sem("u_read"), it * 2 + 1)
                    if e == 0:
                        pe.wait_ge(sem("xT_copied_d"), it + 1)
                        pe.wait_ge(sem("xT_copied_a"), it + 1)
                    for k in range(KT):
                        if e and k == 4:
                            turn_g(0)
                        n = PRE + 8 * e + k
                        if k == KT - 1:
                            pe.wait_ge(sem(f"bias_full{e}"), it * 32 + 32)
                            for c in (0, 2, 1, 3):
                                a = c // 2
                                pe.matmul(B[2 * e + c % 2][64 * a:64 * a + 64, :], lhsT=one, rhs=bias[e][:, 512 * c:512 * (c + 1)],
                                          start=False, stop=False, skip_group_check=True)
                        chunk_landed(n)
                        for c in (0, 2, 1, 3):
                            a = c // 2
                            mm = pe.matmul(B[2 * e + c % 2][64 * a:64 * a + 64, :], lhsT=xT[:, k, 64 * e:64 * e + 64],
                                           rhs=chunk(n)[:, 512 * c:512 * (c + 1)], start=(k == 0), stop=(k == KT - 1),
                                           skip_group_check=True)
                        mm.then_inc(chunks_used, 1)
                for e in range(2):
                    pe.wait_ge(sem(f"y_copied{e}"), it + 1)
                    for a in range(2):
                        pe.matmul(B[4 + e][64 * a:64 * a + 64, :], lhsT=one,
                                  rhs=bias[e][:, FF2 + 512 * a:FF2 + 512 * (a + 1)],
                                  start=True, stop=False, skip_group_check=True)
                    pe.wait_ge(sem("gT_copied"), it * 2 + (e + 2))
                    for k in range(KT):
                        n = PRE + 16 + 4 * e + k // 2
                        if k % 2 == 0:
                            chunk_landed(n)
                        if e == 0 and k == 4:
                            turn_g(1)
                        for a in range(2):
                            mm = pe.matmul(B[4 + e][64 * a:64 * a + 64, :],
                                           lhsT=gT[e].rearrange("p (j a t) -> p j a t", j=4, a=2)[:, k % 4, k // 4, :],
                                           rhs=two(chunk(n))[:, k % 2, 512 * a:512 * (a + 1)],
                                           start=False, stop=(k == KT - 1), skip_group_check=True)
                            if k == KT - 1 and a == 0:
                                mm.then_inc(sem(f"bias_used{e}"), 1)
                        if k % 2:
                            mm.then_inc(chunks_used, 1)
            pe.wait_ge(sem("diag_ready"), TOPK)
            pe.wait_ge(y_full(1, 0), 64)
            for k in range(TOPK):
                for a in range(2):
                    mm = pe.matmul(B[a][:, :], lhsT=diag[:, k, :], rhs=yk[1][k][:, 512 * a:512 * (a + 1)],
                                   start=(k == 0), stop=(k == TOPK - 1))
            mm.then_inc(sem("rows_summed"), 1)

        @block.vector
        def _(dve):
            steps = [0]

            def link(ins):
                steps[0] += 1
                ins.then_inc(sem("dve_step"), 1)
                dve.wait_ge(sem("dve_step"), steps[0])

            dve.memset(scT[:, :, :], 0.0)
            dve.memset(hT[:, :, NTOK:288], 0.0)
            dve.memset(zeros[:, :], 0)
            dve.memset(passf[:, :, :], 0.0)
            dve.memset(topw[:, :, :], 0.0)
            dve.memset(ba[:, :, :], 0.0)
            dve.memset(gb[:, :, :], 0.0).then_inc(sem("cleared"), 1)
            dve.wait_ge(sem("cleared"), 1)

            def means(t, m):
                dve.wait_ge(sem("sums"), 3 * m + t + 1)
                dve.tensor_scalar(ssum3[0:NT[t], t:t + 1], ssum3[0:NT[t], t:t + 1], 1.0 / D, EPS, ALU.mult, ALU.add).then_inc(sem("means"), 1)

            def scaled(t, m, out):
                n = NT[t]
                dve.wait_ge(sem("roots"), 3 * m + t + 1)
                link(dve.reciprocal(root3[0:n, t:t + 1], root3[0:n, t:t + 1]))
                link(dve.tensor_scalar(out, x[0:n, t, :], root3[0:n, t:t + 1], None, ALU.mult))

            dve.wait_ge(sem("adaln_made"), 1)
            dve.tensor_copy(scT[:, :, 0:9], B[0][:, 0:P].rearrange("p (k t) -> p k t", k=KT)[:, :, 0:9]).then_inc(sem("scT_ready"), 1)
            for t in range(3):
                means(t, 0)
            for t in range(3):
                scaled(t, 0, h[0:NT[t], t, :])

            def modulation(q, used, bank, fold):
                dve.wait_ge(sem("ada_rows_full"), 16 * 16)
                dve.wait_ge(chunks_used, used)
                done = dve.tensor_tensor(mods[:, q, :], bank[:, :], ba[:, q, :], ALU.add)
                if fold is None:
                    done.then_inc(sem("mod_ready"), 1)
                    return
                link(done)
                rows, g = fold
                dve.scalar_tensor_tensor(out=mods[rows, q, :], in0=mods[rows, q, :], scalar=1.0, in1=gb[rows, g, :],
                                         op0=ALU.add, op1=ALU.mult).then_inc(sem("mod_ready"), 1)

            modulation(0, N_ADA, B[1], (slice(64, 128), 0))

            def modulated():
                dve.wait_ge(sem("adaln_made"), 2)
                for t in range(2):
                    for a in range(2):
                        c = slice(512 * a, 512 * (a + 1))
                        link(dve.tensor_tensor(h[:, t, c], h[:, t, c], B[2 + a][:, :], ALU.mult))
                        done = dve.tensor_tensor(h[:, t, c], h[:, t, c], B[4 + a][:, :], ALU.add)
                    done.then_inc(sem("h_ready"), 1)
                dve.wait_ge(sem("mod_rows0_full"), 64)
                link(dve.tensor_tensor(h[0:NB, 2, :], h[0:NB, 2, :], rows0s[0:NB, D:2 * D], ALU.mult))
                dve.tensor_tensor(h[0:NB, 2, :], h[0:NB, 2, :], rows0s[0:NB, 0:D], ALU.add).then_inc(sem("h_ready"), 1)

            def odd_tiles(made, copied):
                for k in range(1, KT, 2):
                    dve.wait_ge(sem(made), k + 1)
                    dve.tensor_copy(hT[:, k, 0:NTOK], B[k][:, 0:NTOK]).then_inc(sem(copied), 1)

            modulated()
            odd_tiles("hT_made", "hT_copied_d")
            dve.wait_ge(sem("rows_full"), 16 * 14)
            link(dve.tensor_tensor(lb, lbl[:, 0, :], lbl[:, 1, :], ALU.max))
            for r in range(2):
                dve.tensor_tensor(lbl[:, r, :], lbl[:, r, :], lb, ALU.subtract).then_inc(sem("lb_less_max"), 1)

            for c in range(NZ):
                if c == 3:
                    dve.wait_ge(sem("lb_exp"), 1)
                    link(dve.tensor_tensor(lb, lbl[:, 0, :], lbl[:, 1, :], ALU.add))
                    link(dve.reciprocal(lb, lb))
                    link(dve.tensor_tensor(lb, lb, lbl[:, 0, :], ALU.mult))
                    link(dve.tensor_scalar(oml, lb, -1.0, 1.0, ALU.mult, ALU.add))
                dve.wait_ge(chunks_used, Z0 + c + 1)
                dve.tensor_copy(zq[:, c, :], B[4 + c % 2][:, 0:64]).then_inc(sem("z_dec_copied"), 1)

            def rotary(src, n, t0, nt):
                def part(lo):
                    return src.rearrange("p t (h d) -> p t h d", d=HD)[:, :, :, lo:lo + HALF]

                def table(name):
                    tab = C(name, slice(0, n)).rearrange("p (t f) -> p t f", t=3)[:, t0:t0 + nt, :]
                    return wide(tab.unsqueeze(2), 2, 10)

                def prod(i):
                    return rtmp[0:n, 0:nt, 80 * i:80 * (i + 1)].rearrange("p t (h f) -> p t h f", h=10)

                a, b = part(0), part(HALF)
                dve.tensor_tensor(prod(0), a, table("sin"), ALU.mult)
                link(dve.tensor_tensor(prod(1), b, table("sin"), ALU.mult))
                link(dve.tensor_tensor(a, a, table("cos"), ALU.mult))
                link(dve.tensor_tensor(b, b, table("cos"), ALU.mult))
                dve.tensor_tensor(a, a, prod(1), ALU.subtract)
                dve.tensor_tensor(b, b, prod(0), ALU.add).then_inc(sem("rotated"), 1)

            dve.wait_ge(sem("z_copied"), NZ)
            dve.wait_ge(sem("const_full"), 16)
            rotary(z[:, :, 0:AW + P], P, 0, 2)
            dve.wait_ge(sem("f_sig"), 1)
            f = z[:, :, F0:F0 + HW_]
            link(dve.tensor_tensor(f, f, wide(oml.unsqueeze(1), 1, 2), ALU.mult))
            dve.tensor_tensor(f, f, wide(lb.unsqueeze(1), 1, 2), ALU.add).then_inc(sem("f_ready"), 1)
            ksam = oml[0:NB, :]
            window = C("window")
            for n, t in enumerate((1, 0)):
                w = P * (t + 1)
                nb = 4 // (t + 1)
                if n:
                    dve.wait_ge(sem("zs_full"), 128)
                    rotary(zs[0:NB, 0:AW + P].unsqueeze(1), NB, 2, 1)
                    dve.wait_ge(sem("f_sig"), 2)
                    fs = zs[0:NB, F0:F0 + HW_]
                    link(dve.tensor_tensor(fs, fs, oml[0:NB, :], ALU.mult))
                    link(dve.tensor_tensor(fs, fs, lb[0:NB, :], ALU.add))
                    dve.wait_ge(sem("logf_ready"), 1)
                    dve.tensor_scalar(f, f, -1.0, 1.0, ALU.mult, ALU.add).then_inc(sem("k_ready"), 1)
                    dve.tensor_scalar(oml[0:NB, :], fs, -1.0, 1.0, ALU.mult, ALU.add).then_inc(sem("k_ready"), 1)
                    dve.wait_ge(sem("pT_made"), 4)
                for i in range(8 // nb):
                    g, first = (i % 2, 2 * (i // 2)) if t else (i, 0)
                    bank = B[3 + 2 * g + i // 2] if t else B[(7 + g) % 8]
                    hd = GRP * g + first
                    dve.wait_ge(sem("sc_made"), 4 * n + i + 1)
                    ins = dve.scalar_tensor_tensor(
                        out=sc[:, hd * w:(hd + nb) * w].rearrange("p (m s) -> p m s", s=w),
                        in0=bank[:, :].rearrange("p (m s) -> p m s", s=w), scalar=HD ** -0.5,
                        in1=wide(window[:, 2 * P - w:2 * P].unsqueeze(1), 1, nb), op0=ALU.mult, op1=ALU.add)
                    ins.then_inc(sem("masked"), 1)
                dve.wait_ge(sem("masked"), 4 if n == 0 else 6)
                link(dve.tensor_reduce(mrow[:, t, :], sc[:, 0:HEADS * w].rearrange("p (m s) -> p m s", s=w), AX.X, ALU.max))
                link(dve.tensor_tensor(mrow[:, t, :], mrow[:, t, :], sinkb, ALU.max))
                link(dve.tensor_tensor(dsink[:, t, :], sinkb, mrow[:, t, :], ALU.subtract))
                dve.tensor_scalar(nmax[:, t, :], mrow[:, t, :], -1.0, None, ALU.mult).then_inc(sem("max_ready"), 1)
            for n, t in enumerate((1, 0)):
                dve.wait_ge(sem("esink_ready"), n + 1)
                link(dve.tensor_tensor(psums[:, t, :], psums[:, t, :], esink[:, t, :], ALU.add))
                link(dve.reciprocal(psums[:, t, :], psums[:, t, :]))
                dve.wait_ge(sem("pv_made"), n + 1)
                o = h[:, t, 0:AW]
                dve.tensor_tensor(o.rearrange("p (m d) -> p m d", d=HD), B[1 + n][:, :].rearrange("p (m d) -> p m d", d=HD),
                                  wide(psums[:, t, :].unsqueeze(2), 2, HD), ALU.mult).then_inc(sem("att_summed"), 1)
            dve.wait_ge(sem("att_summed"), 2)

            lvl_mask = C("levels").bitcast(U32).rearrange("p (n t) -> p n t", n=8)
            for t in range(2):
                if t:
                    dve.wait_ge(sem("hgo_made"), 1)
                link(dve.memset(amat[:, :, :], 0.0))
                dve.wait_ge(sem("hg_copied"), 3 * t + 3)

                def diff(n):
                    m = LEVELS[n]
                    v = bT.rearrange("p (n two m) -> p n two m", two=2, m=m)
                    d = lev[n % 3].rearrange("p (n two m) -> p n two m", two=2, m=m)
                    ref = v[:, :, 0, m - 1:m]
                    ref = ref if m == 1 else wide(ref, 2, m)
                    if n >= 3:
                        dve.wait_ge(sem("G_made"), 8 * t + n - 1)
                    elif t:
                        dve.wait_ge(sem("G_made"), 8)
                    dve.tensor_tensor(d[:, :, 0, :], ref, v[:, :, 0, :], ALU.subtract).then_inc(sem("lev_diff"), 1)
                    dve.tensor_tensor(d[:, :, 1, :], v[:, :, 1, :], ref, ALU.subtract).then_inc(sem("lev_diff"), 1)

                def weigh(n):
                    m = LEVELS[n]
                    d = lev[n % 3].rearrange("p (n two m) -> p n two m", two=2, m=m)
                    dve.wait_ge(sem("lev_exp"), 7 * t + n + 1)
                    dve.tensor_tensor(d[:, :, 0, :], d[:, :, 0, :], kkT.rearrange("p (n two m) -> p n two m", two=2, m=m)[:, :, 0, :], ALU.mult)
                    dve.tensor_tensor(d[:, :, 1, :], d[:, :, 1, :], qqT.rearrange("p (n two m) -> p n two m", two=2, m=m)[:, :, 1, :],
                                      ALU.mult).then_inc(sem("lev_ready"), 1)

                def take_level(n):
                    if 8 * t + n:
                        dve.wait_ge(sem("lev_masked"), 8 * t + n)
                    dve.wait_ge(sem("G_made"), 8 * t + n + 1)
                    dve.copy_predicated(amat[:, :, :], wide(lvl_mask[:, n, :].unsqueeze(1), 1, HH),
                                        B[4 + n % 2][:, :].rearrange("p (h t) -> p h t", h=HH)).then_inc(sem("lev_masked"), 1)

                diff(0)
                diff(1)
                diff(2)
                take_level(0)
                weigh(0)
                for n in range(7):
                    if n + 1 < 7:
                        weigh(n + 1)
                    take_level(n + 1)
                    if n + 3 < 7:
                        diff(n + 3)
                dve.wait_ge(sem("tail_exp"), t + 1)
                dve.tensor_tensor(ks, ks, z[:, t, F0:F0 + HW_], ALU.mult).then_inc(sem("ks_ready"), 1)
                if t == 0:
                    modulation(1, ADA1 + N_ADA, B[7], None)
                    dve.wait_ge(sem("st_made"), 1)
                    dve.tensor_copy(st, B[3][:, :]).then_inc(sem("st_copied"), 1)
                else:
                    dve.wait_ge(sem("b_exp"), 2)
                    dve.tensor_tensor(lev[0], lev[0], qqT, ALU.mult).then_inc(sem("dec_operand"), 1)
                    modulation(2, ADA2 + N_ADA, B[2], (slice(0, 64), 1))
                    dve.wait_ge(sem("hgo_made"), 2)
                    dve.wait_ge(sem("st_made"), 2)
                    for hd in range(HH):
                        c = slice(P * hd, P * (hd + 1))
                        dve.scalar_tensor_tensor(out=st[:, c], in0=st[:, c], scalar=eb[:, hd:hd + 1], in1=B[3][:, c],
                                                 op0=ALU.mult, op1=ALU.add).then_inc(sem("state_final"), 1)

            def normed(t, n, c0, h0, hgrn, silu):
                link(dve.reciprocal(groot[0:n, c0:c0 + 1], groot[0:n, c0:c0 + 1]))
                link(dve.reciprocal(groot[0:n, h0:h0 + HH], groot[0:n, h0:h0 + HH]))
                dve.scalar_tensor_tensor(out=h[0:n, t, 0:AW], in0=h[0:n, t, 0:AW], scalar=groot[0:n, c0:c0 + 1],
                                         in1=g_att[0:n, :], op0=ALU.mult, op1=ALU.mult)
                for hd in range(HH):
                    c = slice(AW + P * hd, AW + P * (hd + 1))
                    ins = dve.scalar_tensor_tensor(out=h[0:n, t, c], in0=hgrn[0:n, P * hd:P * (hd + 1)], scalar=groot[0:n, h0 + hd:h0 + hd + 1],
                                                   in1=g_hg[0:n, P * hd:P * (hd + 1)], op0=ALU.mult, op1=ALU.mult)
                link(ins)
                dve.tensor_tensor(h[0:n, t, AW:D], h[0:n, t, AW:D], silu, ALU.mult).then_inc(sem("cat_ready"), 1)

            dve.wait_ge(sem("mod_ready"), 3)
            link(dve.memset(qbd, 0.0))
            for i in range(2):
                dve.wait_ge(sem("kcT_made"), i + 1)
                dve.tensor_copy(kcT[:, 4 * i:4 * i + 4, 0:P], B[i][:, :].rearrange("p (b s) -> p b s", b=4)).then_inc(sem("kcT_copied"), 1)
            dve.wait_ge(sem("snew_made"), 1)
            dve.tensor_copy(kcT[:, :, P], B[2][:, 0:NB]).then_inc(sem("snew_copied"), 1)
            for g in range(KV):
                r = slice(64 * g, 64 * g + 64)
                dve.tensor_copy(qbd[r, :].rearrange("p (b c) -> p b c", b=NB)[:, :, GRP * g:GRP * (g + 1)],
                                B[2][r, 16:48].rearrange("p (j b) -> p b j", j=GRP)).then_inc(sem("snew_copied"), 1)
            dve.wait_ge(sem("kcT_made"), 2)
            link(dve.memset(pbd, 0.0))
            dve.wait_ge(sem("gsums"), 10)
            link(dve.tensor_scalar(gmean[:, 0:2], gmean[:, 0:2], 1.0 / AW, EPS, ALU.mult, ALU.add))
            dve.tensor_scalar(gmean[:, 2:10], gmean[:, 2:10], 1.0 / P, EPS, ALU.mult, ALU.add).then_inc(sem("gmeans"), 1)
            dve.wait_ge(sem("g_silu"), 2)
            dve.wait_ge(sem("groots"), 1)
            for t in range(2):
                normed(t, P, t, 2 + 4 * t, B[6 + t], z[:, t, G0:G0 + HW_])
            dve.wait_ge(sem("ss_made"), 1)
            link(dve.tensor_scalar(ps[0:64, :], B[3][0:64, 0:129], HD ** -0.5, None, ALU.mult))
            link(dve.tensor_reduce(smx[0:64, :], ps[0:64, :], AX.X, ALU.max))
            dve.tensor_scalar(snm[0:64, :], smx[0:64, :], sink64[0:64, :], -1.0, ALU.max, ALU.mult).then_inc(sem("smax_ready"), 1)
            dve.wait_ge(sem("sqf_made"), 1)
            link(dve.tensor_copy(sq, B[0][:, 0:64]))
            onehot = C("onehot", slice(0, NB))

            def mask_keys(b):
                dve.tensor_scalar(km[b % 2][0:NB, :], ksam, onehot[:, b:b + 1], None, ALU.mult).then_inc(sem("km_ready"), 1)

            dve.wait_ge(sem("k_ready"), 2)
            mask_keys(0)
            mask_keys(1)
            for i in (1, 3):
                dve.wait_ge(sem("catT_made"), i + 1)
                dve.tensor_copy(hT[:, 2 * i:2 * i + 2, 0:S], B[4 + i][:, :].rearrange("p (k t) -> p k t", k=2)).then_inc(sem("catT_copied_d"), 1)
            dve.wait_ge(sem("spT_made"), 1)
            dve.tensor_copy(pbd.rearrange("p (b c) -> p b c", b=NB)[:, :, 0:HEADS],
                            B[5][:, 0:64].rearrange("p (b h) -> p b h", b=NB)).then_inc(sem("dec_operand"), 1)
            dve.wait_ge(sem("states_full"), 16 * NB)
            for b in range(NB):
                dve.wait_ge(sem("outer_made"), b + 1)
                for hd in range(HH):
                    fcol = 32 + NB * hd + b
                    dve.scalar_tensor_tensor(out=states[:, b, hd, :], in0=states[:, b, hd, :], scalar=sq[:, fcol:fcol + 1],
                                             in1=B[6 + b % 2][:, P * hd:P * (hd + 1)], op0=ALU.mult, op1=ALU.add).then_inc(sem("states_new"), 1)
                if b + 2 < NB:
                    mask_keys(b + 2)
            dve.wait_ge(sem("sprobs"), 2)
            link(dve.tensor_tensor(ssm[0:64, :], ssm[0:64, :], sesk[0:64, :], ALU.add))
            link(dve.reciprocal(ssm[0:64, :], ssm[0:64, :]))
            dve.tensor_tensor(sra[0:64, :], ssm[0:64, :], C("group", slice(0, 64))[:, 0:1], ALU.mult)
            link(dve.tensor_tensor(srb[0:64, :], ssm[0:64, :], C("group", slice(0, 64))[:, 1:2], ALU.mult))
            dve.wait_ge(sem("pv_copied"), 1)
            link(dve.scalar_tensor_tensor(out=pv[0:64, :], in0=B[5][0:64, 0:P], scalar=ps[0:64, P:P + 1], in1=pv[0:64, :],
                                          op0=ALU.mult, op1=ALU.add))
            link(dve.tensor_scalar(o64[0:64, :], pv[0:64, 0:HD], sra[0:64, :], None, ALU.mult))
            dve.scalar_tensor_tensor(out=o64[0:64, :], in0=pv[0:64, HD:P], scalar=srb[0:64, :], in1=o64[0:64, :],
                                     op0=ALU.mult, op1=ALU.add).then_inc(sem("o64_ready"), 1)
            dve.wait_ge(sem("wo_made"), 1)
            dve.wait_ge(sem("mod_rows_full"), 32)
            for t in range(2):
                for a in range(2):
                    c = slice(512 * a, 512 * (a + 1))
                    ins = dve.tensor_tensor(h[:, t, c], B[2 * t + a][:, :], rows1[:, c], ALU.mult)
                link(ins)
                dve.tensor_tensor(x[:, t, :], x[:, t, :], h[:, t, :], ALU.add).then_inc(sem("x1_ready"), 1)
                dve.wait_ge(sem("x1_ready"), t + 1)

            def second_norm(t, scale, shift):
                r = slice(0, NT[t])
                dve.wait_ge(sem("roots"), 3 + t + 1)
                link(dve.reciprocal(root3[r, t:t + 1], root3[r, t:t + 1]))
                link(dve.scalar_tensor_tensor(out=h[r, t, :], in0=x[r, t, :], scalar=root3[r, t:t + 1], in1=scale,
                                              op0=ALU.mult, op1=ALU.mult))
                dve.tensor_tensor(h[r, t, :], h[r, t, :], shift, ALU.add).then_inc(sem("h2_ready"), 1)

            for t in range(2):
                means(t, 1)
            for t in range(2):
                second_norm(t, scale2, rows1[:, D:2 * D])
            dve.memset(hT[:, :, NTOK:288], 0.0)
            dve.wait_ge(sem("soT_made"), 1)
            dve.tensor_copy(soT, B[4][:, 0:HH * NB]).then_inc(sem("soT_copied"), 1)
            sqs = ks[0:NB, :]
            dve.wait_ge(sem("o64_moved"), 16)
            dve.wait_ge(sem("st_made"), 2)
            link(dve.tensor_tensor(sqs, h[0:NB, 2, 0:AW], h[0:NB, 2, 0:AW], ALU.mult))
            link(dve.tensor_reduce(gmean[0:NB, 10:11], sqs, AX.X, ALU.add))
            dve.wait_ge(sem("so_made"), 1)
            link(dve.tensor_copy(h[0:NB, 2, AW:D], B[6][0:NB, :]))
            link(dve.tensor_tensor(sqs, h[0:NB, 2, AW:D], h[0:NB, 2, AW:D], ALU.mult))
            link(dve.tensor_reduce(gmean[0:NB, 11:15], sqs.rearrange("p (h v) -> p h v", h=HH), AX.X, ALU.add))
            dve.tensor_scalar(gmean[0:NB, 11:15], gmean[0:NB, 11:15], 1.0 / P, EPS, ALU.mult, ALU.add)
            dve.tensor_scalar(gmean[0:NB, 10:11], gmean[0:NB, 10:11], 1.0 / AW, EPS, ALU.mult, ALU.add).then_inc(sem("gmeans"), 1)
            for i in (1, 3):
                dve.wait_ge(sem("h2T_made"), i + 1)
                dve.tensor_copy(hT[:, 2 * i:2 * i + 2, 0:S], B[i][:, :].rearrange("p (k t) -> p k t", k=2)).then_inc(sem("h2T_copied_d"), 1)
            dve.wait_ge(sem("groots"), 2)
            normed(2, NB, 10, 11, h[:, 2, AW:D], zs[0:NB, G0:G0 + HW_])
            dve.wait_ge(sem("catT_made"), 5)
            dve.tensor_copy(hT[:, :, S:NTOK], B[7][:, 0:NB * KT].rearrange("p (k b) -> p k b", k=KT)).then_inc(sem("catT_copied_d"), 1)

            def choose(ts, r, cols, logits, turned, nth):
                nt = len(range(3)[ts])
                dve.wait_ge(sem("lgT_made"), nth)
                dve.tensor_scalar(lgT[0:E, cols], logits, brout[0:E, :], None, ALU.add).then_inc(sem("lgT_ready"), 1)
                dve.wait_ge(sem("lg_made"), nth)
                link(dve.tensor_copy(lg[r, ts, :], turned.rearrange("p (t e) -> p t e", t=nt)))
                for t in range(3)[ts]:
                    ins = dve.max(top8[r, t, :], lg[r, t, :])
                link(ins)
                for t in range(3)[ts]:
                    ins = dve.max_index(top8i[r, t, :], top8[r, t, :], lg[r, t, :])
                link(ins)
                dve.tensor_scalar(ntop[r, ts], top8[r, ts, 0], -1.0, None, ALU.mult).then_inc(sem("top_ready"), 1)
                link(dve.tensor_copy(topf[r, ts, :], top8i[r, ts, 0:TOPK]))
                iota = C("iota", r).unsqueeze(1)
                link(dve.tensor_tensor(onek[r, ts, :, :].rearrange("p t k e -> p (t k) e"), wide(iota, 1, nt * TOPK),
                                       wide(topf[r, ts, :].rearrange("p t k -> p (t k)").unsqueeze(2), 2, E), ALU.is_equal))
                dve.tensor_reduce(chosen[r, ts, :], onek[r, ts, :, :].rearrange("p t k e -> p t e k"), AX.X, ALU.add).then_inc(sem("chosen_ready"), 1)

            def number(ts, r, ranks, nth):
                nt = len(range(3)[ts])
                dve.wait_ge(sem("rank_made"), nth)
                ranks = ranks.rearrange("p (t e) -> p t e", t=nt)
                dve.tensor_tensor(slotf[r, ts, :], ranks, wide(C("e64", r).unsqueeze(1), 1, nt), ALU.add)
                link(dve.tensor_scalar(over[r, ts, :], ranks, float(SLOTS), None, ALU.is_ge))
                for m in range(2, MAXPASS):
                    link(dve.scalar_tensor_tensor(out=over[r, ts, :], in0=ranks, scalar=float(SLOTS * m), in1=over[r, ts, :],
                                                  op0=ALU.is_ge, op1=ALU.add))
                link(dve.scalar_tensor_tensor(out=slotf[r, ts, :], in0=over[r, ts, :], scalar=float(ROWS - SLOTS), in1=slotf[r, ts, :],
                                              op0=ALU.mult, op1=ALU.add))
                link(dve.tensor_tensor(hit[r, ts, :, :], onek[r, ts, :, :], wide(slotf[r, ts, :].unsqueeze(2), 2, TOPK), ALU.mult))
                link(dve.tensor_reduce(topf[r, ts, :], hit[r, ts, :, :], AX.X, ALU.add))
                dve.tensor_copy(slot_u[r, ts, :], topf[r, ts, :]).then_inc(sem("slots_ready"), 1)

            prompt = slice(0, 2), slice(0, P)
            decode = slice(2, 3), slice(0, NB)
            dve.tensor_copy(tok_i[:, :], C("tok"))
            choose(*prompt, slice(0, S), B[4][0:E, 0:S], B[0][:, 0:2 * E], 1)
            dve.wait_ge(chunks_used, PRE)
            dve.tensor_copy(zq[:, 0:4, :], B[5][:, 0:256].rearrange("p (c n) -> p c n", c=4)).then_inc(sem("wo_dec_copied"), 1)
            number(*prompt, B[1][:, 0:2 * E], 1)
            dve.wait_ge(sem("mod_rows_s_full"), 64)
            dve.wait_ge(sem("wo_dec_full"), 64)
            link(dve.tensor_tensor(tmps[0:NB, :], tmps[0:NB, :], rows1s[0:NB, 0:D], ALU.mult))
            dve.tensor_tensor(x[0:NB, 2, :], x[0:NB, 2, :], tmps[0:NB, :], ALU.add).then_inc(sem("x1_ready"), 1)
            dve.wait_ge(sem("x1_ready"), 3)
            means(2, 1)
            second_norm(2, rows2s[0:NB, 0:D], rows1s[0:NB, D:2 * D])
            dve.wait_ge(sem("h2T_made"), 5)
            dve.tensor_copy(hT[:, :, S:NTOK], B[7][:, 0:NB * KT].rearrange("p (k b) -> p k b", k=KT)).then_inc(sem("h2T_copied_d"), 1)
            choose(*decode, slice(S, NTOK), B[2][0:E, 0:NB], B[3][0:NB, 0:E], 2)
            number(*decode, B[6][0:NB, 0:E], 2)
            link(dve.tensor_reduce(cmax[0:1, :], B[0][0:1, 0:E], AX.X, ALU.max))
            dve.memset(chit[0:1, 0:1], 1.0)
            for m in range(1, MAXPASS):
                ins = dve.tensor_scalar(chit[0:1, m:m + 1], cmax[0:1, :], float(SLOTS * m), None, ALU.is_gt)
            link(ins)
            link(dve.tensor_reduce(csum[0:1, :], chit[0:1, :], AX.X, ALU.add))
            dve.tensor_copy(npass[:, :], csum[0:1, :]).then_inc(sem("npass_ready"), 1)
            for ts, r in (prompt, decode):
                link(dve.tensor_tensor(hit[r, ts, :, :], onek[r, ts, :, :], wide(over[r, ts, :].unsqueeze(2), 2, TOPK), ALU.mult))
                link(dve.tensor_reduce(passf[r, ts, :], hit[r, ts, :, :], AX.X, ALU.add))
                dve.scalar_tensor_tensor(out=row_u[r, ts, :], in0=passf[r, ts, :], scalar=-float(ROWS), in1=topf[r, ts, :],
                                         op0=ALU.mult, op1=ALU.add).then_inc(sem("slots_ready"), 1)
            dve.wait_ge(sem("stored"), 16 * N_STORED)
            for e in range(2):
                dve.memset(bias[e], 0.0).then_inc(sem("bias_cleared"), 1)
            dve.wait_ge(sem("top_exp"), 3)
            for ts, r in (prompt, decode):
                link(dve.reciprocal(tsum[r, ts], tsum[r, ts]))
                link(dve.tensor_tensor(topw[r, ts, :], topw[r, ts, :], wide(tsum[r, ts].unsqueeze(2), 2, TOPK), ALU.mult))

            dve.wait_ge(sem("npass_ready"), 1)
            passes = dve.value_load(npass[0:1, 0:1], min_val=1, max_val=MAXPASS)
            link(dve.memset(moe[:, :, :], 0.0))
            link(dve.memset(now, 0.0))
            count_from_one(dve, "g_ready", "u_read", "y_added")
            with dve.Fori(0, passes) as p:
                with dve.Fori(0, PAIRS) as i:
                    it = dve.snap(p * PAIRS + i)
                    dve.wait_ge(sem("xT_made"), it * 2 + 2)
                    dve.tensor_copy(xT[:, 0:4, :], B[6][:, :].rearrange("p (k t) -> p k t", k=4)).then_inc(sem("xT_copied_d"), 1)
                    for e in range(2):
                        dve.wait_ge(chunks_used, it * PER + (PRE + 8 * (e + 1)))
                        dve.wait_ge(sem("g_ready"), it * 2 + (e + 1))
                        for b in range(2):
                            u = B[2 * e + b][:, :].rearrange("p (n two) -> p n two", two=2)
                            ins = dve.tensor_scalar(glu[:, 256 * b:256 * (b + 1)], u[:, :, 0], LIMIT, None, ALU.min)
                        ins.then_inc(sem("glu_ready"), 1)
                        for b in range(2):
                            u = B[2 * e + b][:, :].rearrange("p (n two) -> p n two", two=2)
                            ins = dve.tensor_scalar(lin[:, 256 * b:256 * (b + 1)], u[:, :, 1], LIMIT, -LIMIT, ALU.min, ALU.max)
                        ins.then_inc(sem("u_read"), 1)
                        dve.wait_ge(sem("u_read"), it * 2 + (e + 2))
                        dve.scalar_tensor_tensor(out=lin, in0=lin, scalar=1.0, in1=glu, op0=ALU.add, op1=ALU.mult).then_inc(sem("lin_ready"), 1)
                        dve.wait_ge(sem("lin_ready"), it * 2 + (e + 1))
                        dve.wait_ge(sem("sig_ready"), it * 2 + (e + 1))
                        dve.wait_ge(sem("gT_made"), it * 2 + 1)
                        dve.tensor_tensor(gg[e], lin, sg, ALU.mult).then_inc(sem("g_ready"), 1)
                with dve.If(p < passes - 1):
                    dve.tensor_scalar(passw[:, :, :], passf[:, :, :], now, None, ALU.is_equal).then_inc(sem("pass_step"), 1)
                    dve.wait_ge(sem("pass_step"), p * 3 + 1)
                    dve.tensor_tensor(passw[:, :, :], passw[:, :, :], topw[:, :, :], ALU.mult).then_inc(sem("pass_step"), 1)
                    dve.wait_ge(sem("pass_step"), p * 3 + 2)
                    for n in range(3 * TOPK):
                        t, k = divmod(n, TOPK)
                        r = slice(0, NT[t])
                        dve.wait_ge(sem("y_part"), p * (16 * 3 * TOPK) + 16 * (n + 1))
                        dve.scalar_tensor_tensor(out=moe[r, t, :], in0=xg[r, :], scalar=passw[r, t, k:k + 1],
                                                 in1=moe[r, t, :], op0=ALU.mult, op1=ALU.add).then_inc(sem("y_added"), 1)
                        dve.wait_ge(sem("y_added"), p * (3 * TOPK) + (n + 2))
                    dve.tensor_scalar(now, now, 1.0, None, ALU.add).then_inc(sem("pass_step"), 1)
                    dve.wait_ge(sem("pass_step"), p * 3 + 3)
                    dve.nop(nofuse=True)
            link(dve.tensor_scalar(passw[:, :, :], passf[:, :, :], now, None, ALU.is_equal))
            link(dve.tensor_tensor(passw[:, :, :], passw[:, :, :], topw[:, :, :], ALU.mult))
            for k in range(TOPK):
                dve.tensor_scalar(diag[:, k, :], ident, passw[:, 1, k:k + 1], None, ALU.mult).then_inc(sem("diag_ready"), 1)
            link(dve.tensor_tensor(moe[:, 1, :], moe[:, 1, :], gate2, ALU.mult))
            link(dve.tensor_tensor(x[:, 1, :], x[:, 1, :], moe[:, 1, :], ALU.add))

            def last_means(n):
                t = LAST[n]
                dve.wait_ge(sem("sums"), 6 + n + 1)
                dve.tensor_scalar(ssum3[0:NT[t], t:t + 1], ssum3[0:NT[t], t:t + 1], 1.0 / D, EPS, ALU.mult, ALU.add).then_inc(sem("means"), 1)

            def final_norm(n):
                t = LAST[n]
                r = slice(0, NT[t])
                dve.wait_ge(sem("roots"), 6 + n + 1)
                link(dve.reciprocal(root3[r, t:t + 1], root3[r, t:t + 1]))
                dve.scalar_tensor_tensor(out=x[r, t, :], in0=x[r, t, :], scalar=root3[r, t:t + 1], in1=g_fin[r, :],
                                         op0=ALU.mult, op1=ALU.mult).then_inc(sem("result"), 1)

            for n, t in enumerate((0, 2)):
                r = slice(0, NT[t])
                for k in range(TOPK):
                    dve.wait_ge(y_full(t, k), 64 if t else 32)
                    link(dve.scalar_tensor_tensor(out=moe[r, t, :], in0=yk[t][k][r, :], scalar=passw[r, t, k:k + 1],
                                                  in1=moe[r, t, :], op0=ALU.mult, op1=ALU.add))
                    if k == 1 and n:
                        last_means(0)
                link(dve.tensor_tensor(moe[r, t, :], moe[r, t, :], rows2s[r, D:2 * D] if t == 2 else gate2, ALU.mult))
                dve.tensor_tensor(x[r, t, :], x[r, t, :], moe[r, t, :], ALU.add).then_inc(sem("x2_ready"), 1)
                if n:
                    final_norm(0)
            last_means(1)
            dve.wait_ge(sem("rows_summed"), 1)
            for a in range(2):
                c = slice(512 * a, 512 * (a + 1))
                done = dve.tensor_tensor(moe[:, 1, c], B[a][:, :], gate2[:, c], ALU.mult)
            link(done)
            dve.tensor_tensor(x[:, 1, :], x[:, 1, :], moe[:, 1, :], ALU.add).then_inc(sem("x2_ready"), 1)
            final_norm(1)
            last_means(2)
            final_norm(2)


INS = ["x_prompt", "x_sample", "c_prompt", "c_sample", "cache_k_win", "cache_v_win", "state_hgrn", "w_ada", "b_ada",
       "g_mix", "g_ffn", "w_in", "attn_sinks", "g_attn_out", "hg_lb_logits", "g_hg_out", "w_out", "w_router",
       "b_router", "w_up", "b_up", "w_down", "b_down", "g_final"]
OUTS = [("yp", (1, S, D)), ("ys", (NB, 1, D)), ("kwp", (1, 1, WIN, KV, HD)), ("vwp", (1, 1, WIN, KV, HD)),
        ("hgp", (1, 1, HH, P, P)), ("kws", (1, NB, WIN, KV, HD)), ("vws", (1, NB, WIN, KV, HD)),
        ("hgs", (1, NB, HH, P, P))]


def kernel(**inputs):
    import concourse.bacc as bacc
    from concourse.bass_utils import run_bass_kernel_spmd as run

    nc = bacc.Bacc("TRN2", target_bir_lowering=False, num_devices=1)
    arrays, ins, outs = {}, {}, {}
    given = {name: np.ascontiguousarray(inputs[name]) for name in INS}
    given["const"] = constants()
    for name, a in given.items():
        arrays[f"in_{name}"] = a
        ins[name] = nc.dram_tensor(f"in_{name}", a.shape, mybir.dt.from_np(a.dtype), kind="ExternalInput").ap()
    for name, shape in OUTS:
        outs[name] = nc.dram_tensor(f"out_{name}", shape, F32, kind="ExternalOutput").ap()
    hybrid_layer(nc, ins, outs)
    r = run(nc, [arrays], core_ids=[0])
    return tuple(r.results[0][f"out_{name}"] for name, _ in OUTS)
```
